# Optimizing a Trainium2 kernel written in Bass

```python
import math
import jax, jax.numpy as jnp
from jax import lax
import numpy as np

D_MODEL = 2048
BATCH = 1
SEQ = 256
DEPTH = 1

ATT_HEADS = 16
ATT_KV_HEADS = 4
ATT_HEAD_DIM = 64
ATT_GROUP = ATT_HEADS // ATT_KV_HEADS
WINDOW = 128
ATT_BLOCK = 128
M_HEADS = 4
M_QK_DIM = 128
M_V_DIM = 256
M_CHUNK = 64
CONV_WIDTH = 4
D_FF = 5632
EPS = 1e-6

ATT_Q = ATT_HEADS * ATT_HEAD_DIM
ATT_KV = ATT_KV_HEADS * ATT_HEAD_DIM
M_QK = M_HEADS * M_QK_DIM
M_V = M_HEADS * M_V_DIM
IN_SIZES = (ATT_Q, ATT_KV, ATT_KV, M_QK, M_QK, M_V, M_V, M_HEADS, M_HEADS, D_MODEL, D_MODEL)
D_IN = ATT_Q + 2 * ATT_KV + 2 * M_QK + 2 * M_V + 2 * M_HEADS + 2 * D_MODEL

kernel_name = "hybrid_swa_mlstm_macaron_block"

def rmsnorm(x, g):
    xf = x.astype(jnp.float32)
    y = xf * lax.rsqrt(jnp.mean(xf * xf, axis=-1, keepdims=True) + EPS)
    return (y * g.astype(jnp.float32)).astype(x.dtype)

def swiglu(x, wg, wu, wd):
    return (jax.nn.silu(x @ wg) * (x @ wu)) @ wd

def alibi_slopes(n):
    return jnp.exp2(-8.0 * jnp.arange(1, n + 1, dtype=jnp.float32) / n)

def split_columns(z):
    parts = []
    off = 0
    for size in IN_SIZES:
        parts.append(z[..., off:off + size])
        off += size
    return parts

def causal_depthwise_conv(x, w, b):
    S = x.shape[1]
    xp = jnp.pad(x, ((0, 0), (CONV_WIDTH - 1, 0), (0, 0)))
    y = xp[:, 0:S] * w[0]
    for j in range(1, CONV_WIDTH):
        y = y + xp[:, j:j + S] * w[j]
    return y + b

def sliding_window_attention(q, k, v, sinks):
    B, S = q.shape[0], q.shape[1]
    nb = S // ATT_BLOCK
    qb = q.reshape(B, nb, ATT_BLOCK, ATT_KV_HEADS, ATT_GROUP, ATT_HEAD_DIM)
    kb = k.reshape(B, nb, ATT_BLOCK, ATT_KV_HEADS, ATT_HEAD_DIM)
    vb = v.reshape(B, nb, ATT_BLOCK, ATT_KV_HEADS, ATT_HEAD_DIM)
    zpad = jnp.zeros_like(kb[:, :1])
    kk = jnp.concatenate([jnp.concatenate([zpad, kb[:, :-1]], axis=1), kb], axis=2)
    vv = jnp.concatenate([jnp.concatenate([zpad, vb[:, :-1]], axis=1), vb], axis=2)
    scale = 1.0 / math.sqrt(ATT_HEAD_DIM)
    s = jnp.einsum('bnqhgd,bnkhd->bnhgqk', qb, kk).astype(jnp.float32) * scale
    qi = jnp.arange(ATT_BLOCK)[:, None]
    kj = jnp.arange(2 * ATT_BLOCK)[None, :]
    dist = qi - kj + ATT_BLOCK
    blk = jnp.arange(nb)[:, None, None]
    valid = (dist >= 0) & (dist < WINDOW) & (blk * ATT_BLOCK + kj - ATT_BLOCK >= 0)
    slopes = alibi_slopes(ATT_HEADS).reshape(ATT_KV_HEADS, ATT_GROUP)
    s = s - slopes[None, None, :, :, None, None] * dist.astype(jnp.float32)[None, None, None, None]
    s = jnp.where(valid[None, :, None, None], s, -jnp.inf)
    sink = sinks.astype(jnp.float32).reshape(ATT_KV_HEADS, ATT_GROUP)[None, None, :, :, None, None]
    m = jnp.maximum(jnp.max(s, axis=-1, keepdims=True), sink)
    p = jnp.exp(s - m)
    p = p / (jnp.sum(p, axis=-1, keepdims=True) + jnp.exp(sink - m))
    o = jnp.einsum('bnhgqk,bnkhd->bnqhgd', p.astype(vv.dtype), vv)
    return o.reshape(B, S, ATT_Q)

def mlstm_chunkwise(q, k, v, i_pre, f_pre):
    B, S = q.shape[0], q.shape[1]
    nc = S // M_CHUNK
    L = M_CHUNK
    f32 = jnp.float32

    def chunks(t, d):
        return t.astype(f32).reshape(B, nc, L, M_HEADS, d).transpose(0, 3, 1, 2, 4)

    qc = chunks(q, M_QK_DIM)
    kc = chunks(k, M_QK_DIM) * (1.0 / math.sqrt(M_QK_DIM))
    vc = chunks(v, M_V_DIM)
    logi = i_pre.astype(f32).reshape(B, nc, L, M_HEADS).transpose(0, 3, 1, 2)
    logf = jax.nn.log_sigmoid(f_pre.astype(f32)).reshape(B, nc, L, M_HEADS).transpose(0, 3, 1, 2)
    b = jnp.cumsum(logf, axis=-1)
    b_last = b[..., -1]
    g = b_last[..., None] - b + logi

    def step(carry, xs):
        C, n, m = carry
        bl, gs, ks, vs = xs
        m_new = jnp.maximum(bl + m, jnp.max(gs, axis=-1))
        decay = jnp.exp(bl + m - m_new)
        w = jnp.exp(gs - m_new[..., None])
        C_new = decay[..., None, None] * C + jnp.einsum('bhl,bhlk,bhlv->bhkv', w, ks, vs)
        n_new = decay[..., None] * n + jnp.einsum('bhl,bhlk->bhk', w, ks)
        return (C_new, n_new, m_new), (C, n, m)

    init = (jnp.zeros((B, M_HEADS, M_QK_DIM, M_V_DIM), f32),
            jnp.zeros((B, M_HEADS, M_QK_DIM), f32),
            jnp.zeros((B, M_HEADS), f32))
    xs = (jnp.moveaxis(b_last, 2, 0), jnp.moveaxis(g, 2, 0), jnp.moveaxis(kc, 2, 0), jnp.moveaxis(vc, 2, 0))
    _, (C_in, n_in, m_in) = lax.scan(step, init, xs)
    C_in = jnp.moveaxis(C_in, 0, 2)
    n_in = jnp.moveaxis(n_in, 0, 2)
    m_in = jnp.moveaxis(m_in, 0, 2)

    a = b + m_in[..., None]
    D = b[..., :, None] - b[..., None, :] + logi[..., None, :]
    causal = jnp.tril(jnp.ones((L, L), dtype=bool))
    D = jnp.where(causal, D, -jnp.inf)
    m_t = jnp.maximum(a, jnp.max(D, axis=-1))
    inter_w = jnp.exp(a - m_t)
    P = jnp.einsum('bhcld,bhcsd->bhcls', qc, kc) * jnp.exp(D - m_t[..., None])
    num = jnp.einsum('bhcls,bhcsv->bhclv', P, vc) + inter_w[..., None] * jnp.einsum('bhcld,bhcdv->bhclv', qc, C_in)
    den = jnp.sum(P, axis=-1) + inter_w * jnp.einsum('bhcld,bhcd->bhcl', qc, n_in)
    h = num / jnp.maximum(jnp.abs(den), jnp.exp(-m_t))[..., None]
    return h.transpose(0, 2, 3, 1, 4).reshape(B, S, M_HEADS, M_V_DIM).astype(q.dtype)

def hybrid_mixer(u, w_in, conv_w, conv_b, attn_sinks, m_igate_b, m_fgate_b, m_head_g, w_attn_up, w_mlstm_up, w_out):
    B, S = u.shape[0], u.shape[1]
    aq, ak, av, mq, mk, mv, mo, mi, mf, ga, gm = split_columns(u @ w_in)
    att = sliding_window_attention(aq.reshape(B, S, ATT_HEADS, ATT_HEAD_DIM),
                                   ak.reshape(B, S, ATT_KV_HEADS, ATT_HEAD_DIM),
                                   av.reshape(B, S, ATT_KV_HEADS, ATT_HEAD_DIM), attn_sinks)
    qk = jax.nn.silu(causal_depthwise_conv(jnp.concatenate([mq, mk], axis=-1), conv_w, conv_b))
    h = mlstm_chunkwise(qk[..., :M_QK].reshape(B, S, M_HEADS, M_QK_DIM),
                        qk[..., M_QK:].reshape(B, S, M_HEADS, M_QK_DIM),
                        mv.reshape(B, S, M_HEADS, M_V_DIM), mi + m_igate_b, mf + m_fgate_b)
    h = rmsnorm(h, m_head_g.reshape(M_HEADS, M_V_DIM)).reshape(B, S, M_V)
    h = jax.nn.sigmoid(mo) * h
    y = jax.nn.sigmoid(ga) * (att @ w_attn_up) + jax.nn.sigmoid(gm) * (h @ w_mlstm_up)
    return y @ w_out

def setup_inputs(seed: int = 0) -> dict:
    key = jax.random.key(seed)
    ks = jax.random.split(key, 24)
    Ld = DEPTH

    def nrm(k, shape, scale):
        return jax.random.normal(k, shape, jnp.float32) * scale

    def gain(k, n):
        return 1.0 + 0.02 * jax.random.normal(k, (Ld, n), jnp.float32)

    dsc = D_MODEL ** -0.5
    fsc = D_FF ** -0.5
    return {
        "x": nrm(ks[0], (BATCH, SEQ, D_MODEL), 1.0),
        "ffn1_pre_g": gain(ks[1], D_MODEL),
        "ffn1_wg": nrm(ks[2], (Ld, D_MODEL, D_FF), dsc),
        "ffn1_wu": nrm(ks[3], (Ld, D_MODEL, D_FF), dsc),
        "ffn1_wd": nrm(ks[4], (Ld, D_FF, D_MODEL), fsc),
        "ffn1_post_g": gain(ks[5], D_MODEL),
        "mix_pre_g": gain(ks[6], D_MODEL),
        "w_in": nrm(ks[7], (Ld, D_MODEL, D_IN), dsc),
        "conv_w": nrm(ks[8], (Ld, CONV_WIDTH, 2 * M_QK), CONV_WIDTH ** -0.5),
        "conv_b": nrm(ks[9], (Ld, 2 * M_QK), 0.02),
        "attn_sinks": nrm(ks[10], (Ld, ATT_HEADS), 0.5),
        "m_igate_b": nrm(ks[11], (Ld, M_HEADS), 0.1),
        "m_fgate_b": jnp.linspace(3.0, 6.0, M_HEADS, dtype=jnp.float32)[None, :] + nrm(ks[12], (Ld, M_HEADS), 0.1),
        "m_head_g": gain(ks[13], M_V),
        "w_attn_up": nrm(ks[14], (Ld, ATT_Q, D_MODEL), ATT_Q ** -0.5),
        "w_mlstm_up": nrm(ks[15], (Ld, M_V, D_MODEL), M_V ** -0.5),
        "w_out": nrm(ks[16], (Ld, D_MODEL, D_MODEL), dsc),
        "mix_post_g": gain(ks[17], D_MODEL),
        "ffn2_pre_g": gain(ks[18], D_MODEL),
        "ffn2_wg": nrm(ks[19], (Ld, D_MODEL, D_FF), dsc),
        "ffn2_wu": nrm(ks[20], (Ld, D_MODEL, D_FF), dsc),
        "ffn2_wd": nrm(ks[21], (Ld, D_FF, D_MODEL), fsc),
        "ffn2_post_g": gain(ks[22], D_MODEL),
    }

def reference(x, ffn1_pre_g, ffn1_wg, ffn1_wu, ffn1_wd, ffn1_post_g, mix_pre_g, w_in, conv_w, conv_b,
              attn_sinks, m_igate_b, m_fgate_b, m_head_g, w_attn_up, w_mlstm_up, w_out, mix_post_g,
              ffn2_pre_g, ffn2_wg, ffn2_wu, ffn2_wd, ffn2_post_g):
    h = x
    for l in range(DEPTH):
        f = swiglu(rmsnorm(h, ffn1_pre_g[l]), ffn1_wg[l], ffn1_wu[l], ffn1_wd[l])
        h = h + 0.5 * rmsnorm(f, ffn1_post_g[l])
        y = hybrid_mixer(rmsnorm(h, mix_pre_g[l]), w_in[l], conv_w[l], conv_b[l], attn_sinks[l],
                         m_igate_b[l], m_fgate_b[l], m_head_g[l], w_attn_up[l], w_mlstm_up[l], w_out[l])
        h = h + rmsnorm(y, mix_post_g[l])
        f = swiglu(rmsnorm(h, ffn2_pre_g[l]), ffn2_wg[l], ffn2_wu[l], ffn2_wd[l])
        h = h + 0.5 * rmsnorm(f, ffn2_post_g[l])
    return h


_drawn_inputs = setup_inputs


def setup_inputs(seed=0):
    import zlib

    import numpy as np

    out = dict(_drawn_inputs(seed))
    spreads = {}
    factors = {'ffn1_pre_g': 2.901,
     'ffn1_post_g': 4.286,
     'conv_b': 5.032,
     'm_igate_b': 64.0,
     'm_head_g': 12.284,
     'mix_post_g': 11.02,
     'ffn2_pre_g': 19.41,
     'ffn2_post_g': 34.702,
     'attn_sinks': 5.657}
    for name, (base, spread) in spreads.items():
        noise = np.random.default_rng([zlib.crc32(name.encode()), seed]).standard_normal(out[name].shape)
        drawn = base * np.exp(spread * noise) if base else spread * noise
        out[name] = __import__('jax').numpy.asarray(drawn.astype(out[name].dtype))
    for name, factor in factors.items():
        out[name] = (out[name] * factor).astype(out[name].dtype)
    return out
```

```python
from contextlib import ExitStack

import numpy as np

import concourse.bass as bass
from concourse import mybir

F32 = mybir.dt.float32
F32R = mybir.dt.float32r
ALU = mybir.AluOpType
ACT = mybir.ActivationFunctionType
AX = mybir.AxisListType

P = 128
EPS = 1e-6
MASKED = -1e30


def hybrid_layer(nc: bass.Bass, x, ffn1_pre_g, ffn1_wg, ffn1_wu, ffn1_wd, ffn1_post_g, mix_pre_g,
                 w_in, conv_w, conv_b, attn_sinks, m_igate_b, m_fgate_b, m_head_g, w_attn_up,
                 w_mlstm_up, w_out, mix_post_g, ffn2_pre_g, ffn2_wg, ffn2_wu, ffn2_wd, ffn2_post_g,
                 out):
    _, SEQ, D = x.shape
    F = ffn1_wg.shape[2]
    NT = SEQ // P
    ND = D // P
    NF = F // P
    COLS = 512
    NCB = D // COLS
    HEADS = attn_sinks.shape[1]
    KVH = 4
    GROUP = HEADS // KVH
    HD = 64
    MH = m_igate_b.shape[1]
    CONV = conv_w.shape[1]
    MQK = conv_w.shape[2] // 2
    QKD = MQK // MH
    MV = m_head_g.shape[1]
    VD = MV // MH
    ATT_Q, ATT_KV = HEADS * HD, KVH * HD
    assert NT == 2 and ND == 16 and NCB == 4 and QKD == P and VD == 2 * P and ATT_Q == MV == 1024

    HALF = 1024
    RAW = 4
    SPL = 4
    KC = 4
    BLOCK_CHUNKS = ND // KC
    NFB = F // COLS
    UP_CHUNKS = NFB * 2 * BLOCK_CHUNKS
    UPK = ATT_Q // P
    UP_BLOCK_CHUNKS = UPK // KC
    OFF_K = ATT_Q
    OFF_MQ = ATT_Q + 2 * ATT_KV
    OFF_MK = OFF_MQ + MQK
    OFF_MV = OFF_MK + MQK
    OFF_MO = OFF_MV + MV
    OFF_GATES = OFF_MO + MV
    OFF_GA = OFF_GATES + 2 * MH
    OFF_GM = OFF_GA + D
    IN_BLOCKS = ([("k", 0, OFF_K)] + [("q", j, j * COLS) for j in range(2)]
                 + [("mqk", 0, OFF_MQ), ("mqk", 1, OFF_MK)]
                 + [("mv", j, OFF_MV + j * COLS) for j in range(2)]
                 + [("mo", j, OFF_MO + j * COLS) for j in range(2)]
                 + [("ga", j, OFF_GA + j * COLS) for j in range(4)]
                 + [("gm", j, OFF_GM + j * COLS) for j in range(4)])
    NIN = len(IN_BLOCKS)
    A_SLOT = NIN * 8
    M_SLOT = A_SLOT + NCB * 2 * UP_BLOCK_CHUNKS
    END_SLOT = M_SLOT + NCB * 2 * UP_BLOCK_CHUNKS
    C_UP = [0, 0]
    C_DOWN = [C_UP[0] + UP_CHUNKS, 0]
    C_MIX = C_DOWN[0] + NF
    C_OUT = C_MIX + END_SLOT // 2
    C_UP[1] = C_OUT + ND
    C_DOWN[1] = C_UP[1] + UP_CHUNKS
    H_MIX = 2 * C_MIX
    Y_END = [2 * (C_DOWN[0] + NF), 2 * (C_OUT + ND), 2 * (C_DOWN[1] + NF)]
    assert all(c % RAW == 0 for c in C_UP + C_DOWN + [C_MIX, C_OUT])
    T_DOWN = [0, NF + ND]
    T_OUT = NF

    def ends(b):
        return 8 * b + 7 if b < NIN else A_SLOT + 4 * (b - NIN) + 3

    def evac_slot(b):
        return ends(b) + 3

    EVAC_AT = {evac_slot(b): b for b in range(NIN + 2 * NCB)}
    kinds = [k for k, _, _ in IN_BLOCKS] + ["A"] * NCB + ["M"] * NCB

    def act_evacs(b):
        return sum(k not in ("A", "M") for k in kinds[:b + 1])

    def dve_evacs(b):
        return sum(k not in ("mo", "ga", "gm") for k in kinds[:b + 1])

    TURN_B = {8 * b + 9: b for b in (0, 1, 2, 3, 4)}
    TURN_COPY = {8 * b + 13: b for b in (0, 1, 2, 3, 4)}
    CONV_AT = {38 + 8 * q + c: (q, c) for q in range(2) for c in range(4)}
    SILU_AT = {43 + 8 * q: q for q in range(2)}
    G0 = 22
    NG = 2 * KVH
    SPLIT_SLOT = A_SLOT - SPL

    def group_at(s, offset):
        g, rest = divmod(s - G0 - offset, 8)
        return g if rest == 0 and 0 <= g < NG else None

    ctx = ExitStack()
    with ctx:
        def sb(name, shape, dt=F32, where=ctx):
            return where.enter_context(nc.sbuf_tensor(name, shape, dt))

        def sem(name):
            return ctx.enter_context(nc.semaphore(name))

        raw = sb("raw", [P, RAW, 2 * HALF])
        w_hi = sb("w_hi", [P, SPL, HALF], F32R)
        w_lo = sb("w_lo", [P, SPL, HALF], F32R)
        x_hi = sb("x_hi", [P, ND, SEQ], F32R)
        x_lo = sb("x_lo", [P, ND, SEQ], F32R)
        h = sb("h", [P, NT, D])
        gain = sb("gain", [P, D])
        att = gain[:, :].rearrange("p (c t) -> p c t", t=SEQ)
        rows = sb("rows", [P, P])
        cols = sb("cols", [P, P])
        ident = sb("ident", [P, P])
        dist = sb("dist", [P, 2 * P])
        future = sb("future", [P, P])
        sel = sb("sel", [MH, MH, P])
        ones = sb("ones", [P, SEQ])
        neg_half = sb("neg_half", [P, 4])
        sinks = sb("sinks", [P, HEADS])
        head_g = sb("head_g", [P, MV])
        gate_b = sb("gate_b", [MH, 2])
        wg_raw = sb("wg_raw", [P, ND, 2 * MH])
        wg_hi = sb("wg_hi", [P, ND, 2 * MH], F32R)
        wg_lo = sb("wg_lo", [P, ND, 2 * MH], F32R)
        stat = sb("stat", [P, 64])
        sq_y = stat[:, 0:8].rearrange("p (t c) -> p t c", t=NT)
        ms_y = stat[:, 8:10]
        rs_y = stat[:, 10:12]
        rs_yh = stat[:, 12:14]
        sq_h = stat[:, 14:16]
        ms_h = stat[:, 16:18]
        rs_h = stat[:, 18:20]
        rs_q = stat[:, 20:22]
        m_stat = sb("m_stat", [P, 64])
        r_col = m_stat[:, 0:8].rearrange("p (t h) -> p t h", t=NT)
        e_col = m_stat[:, 8:16].rearrange("p (t h) -> p t h", t=NT)
        den = m_stat[:, 16:24].rearrange("p (t h) -> p t h", t=NT)
        rden = m_stat[:, 24:32].rearrange("p (t h) -> p t h", t=NT)
        sq_m = m_stat[:, 32:40].rearrange("p (t h) -> p t h", t=NT)
        ms_m = m_stat[:, 40:48].rearrange("p (t h) -> p t h", t=NT)
        rs_m = m_stat[:, 48:56].rearrange("p (t h) -> p t h", t=NT)
        a_stat = sb("a_stat", [P, 2, 8, 4])
        gates_tok = sb("gates_tok", [P, NT, 2 * MH])
        G_PRE = [0, ND, 2 * ND]
        G_TAP = 3 * ND
        G_BIAS = G_TAP + CONV * 2 * MQK // P
        NROWS = G_BIAS + 2 * MQK // P

        with ExitStack() as part:
            hid = sb("hid", [P, NF, SEQ], F32, part)
            silu = sb("silu", [P, NT, COLS], F32, part)
            prod = sb("prod", [P, NT, COLS], F32, part)
        with ExitStack() as part:
            attn_in = sb("attn_in", [P, 3584], F32, part)
            m_in = sb("m_in", [P, 2 * MH * SEQ + NT * MH * (VD + 1)], F32, part)
            smo = sb("smo", [P, NT, MV], F32, part)
            y = sb("y", [P, NT, D], F32, part)
            gm = sb("gm", [P, NCB, NT * COLS], F32, part)
            rows4 = sb("rows4", [MH, 4, SEQ], F32, part)
        conv_out = m_in[:, 0:2 * MH * SEQ].rearrange("p (c t) -> p c t", t=SEQ)
        mval = m_in[:, 2 * MH * SEQ:].rearrange("p (t h d) -> p t h d", t=NT, h=MH)
        y_T = m_in[:, 0:ND * SEQ].rearrange("p (c t) -> p c t", t=SEQ)
        att_qT = attn_in[:, 0:2048].rearrange("p (c t) -> p c t", t=SEQ)
        att_kT = attn_in[:, 2048:3072].rearrange("p (c t) -> p c t", t=SEQ)
        att_v = attn_in[:, 3072:3584].rearrange("p (t d) -> p t d", t=NT)
        WTN = 3 * P
        wt = attn_in[:, 0:MH * WTN].rearrange("p (h n) -> p h n", h=MH)
        pt_m = attn_in[:, MH * WTN:2 * MH * WTN].rearrange("p (h n) -> p h n", h=MH)
        y_flat = y[:, :, :].rearrange("p t d -> p (t d)")
        CP = SEQ + CONV - 1
        conv_in = y_flat[:, 0:8 * CP].rearrange("p (c n) -> p c n", n=CP)
        stage = y_flat[:, 8 * CP:8 * CP + NT * COLS].rearrange("p (t n) -> p t n", t=NT)
        probs = gm[:, 0:2, :]
        probs_T = gm[:, 2:4, :]
        m_h = gm[:, 2:4, :]
        m_T = conv_out

        ps = ctx.enter_context(nc.psum_tensor("ps", [P, 8, COLS], F32))

        x_in = sem("x_in")
        rows_in = sem("rows_in")
        misc_in = sem("misc_in")
        wg_in = sem("wg_in")
        gain_in = sem("gain_in")
        raw_full = [sem(f"raw_full{i}") for i in range(RAW)]
        hi_ready = sem("hi_ready")
        lo_ready = sem("lo_ready")
        w_used = sem("w_used")
        const_step = sem("const_step")
        const_ready = sem("const_ready")
        rows_turned = sem("rows_turned")
        cols_ready = sem("cols_ready")
        h_turned = sem("h_turned")
        x_hi_ready = sem("x_hi_ready")
        x_lo_ready = sem("x_lo_ready")
        xs_hi_ready = sem("xs_hi_ready")
        xs_lo_ready = sem("xs_lo_ready")
        h_squared = sem("h_squared")
        h_ms = sem("h_ms")
        h_rstd = sem("h_rstd")
        y_squared = sem("y_squared")
        y_ms = sem("y_ms")
        y_rstd = sem("y_rstd")
        h_ready = sem("h_ready")
        silu_ready = sem("silu_ready")
        prod_ready = sem("prod_ready")
        prod_turned = sem("prod_turned")
        hid_a = sem("hid_a")
        hid_v = sem("hid_v")
        act_step = sem("act_step")
        dve_step = sem("dve_step")
        wg_hi_ready = sem("wg_hi_ready")
        wg_lo_ready = sem("wg_lo_ready")
        gates_done = sem("gates_done")
        gates_ready = sem("gates_ready")
        gates_turned = sem("gates_turned")
        gate_rows = sem("gate_rows")
        log_ready = sem("log_ready")
        rows_ready = sem("rows_ready")
        r_turned = sem("r_turned")
        r_cols = sem("r_cols")
        e_cols = sem("e_cols")
        ev_a = sem("ev_a")
        ev_v = sem("ev_v")
        stage_turned = sem("stage_turned")
        turn_a = sem("turn_a")
        turn_v = sem("turn_v")
        conv_ready = sem("conv_ready")
        conv_silu = sem("conv_silu")
        scored = sem("scored")
        maxed = sem("maxed")
        exped = sem("exped")
        normed = sem("normed")
        p_turned = sem("p_turned")
        pt_a = sem("pt_a")
        pt_v = sem("pt_v")
        pv_done = sem("pv_done")
        pv_out = sem("pv_out")
        neg_r = sem("neg_r")
        wt_arg = sem("wt_arg")
        wt_ready = sem("wt_ready")
        m_scored = sem("m_scored")
        pt_m_ready = sem("pt_m_ready")
        num_done = sem("num_done")
        rden_ready = sem("rden_ready")
        mh_a = sem("mh_a")
        mh_v = sem("mh_v")
        m_squared = sem("m_squared")
        m_ms = sem("m_ms")
        m_rstd = sem("m_rstd")
        m_rows = sem("m_rows")
        m_turned = sem("m_turned")
        mt_a = sem("mt_a")
        mt_v = sem("mt_v")
        att_split = sem("att_split")
        att_split_lo = sem("att_split_lo")
        ones_v = sem("ones_v")
        q_scale = sem("q_scale")
        y_ready = sem("y_ready")
        y_turned = sem("y_turned")
        yt_a = sem("yt_a")
        yt_v = sem("yt_v")
        stored = sem("stored")

        WG = [ffn1_wg[0], ffn2_wg[0]]
        WU = [ffn1_wu[0], ffn2_wu[0]]
        WD = [ffn1_wd[0], ffn2_wd[0]]

        def src_tile(phase, n):
            return hid[:, n, :] if phase != "out" else y_T[:, n, :]

        block = ctx.enter_context(nc.Block())

        @block.sync
        def _(sp):
            sp.dma_start(h[:, :, :], x[0].rearrange("(t p) d -> p t d", p=P)).then_inc(x_in, 16)
            n_rows = 0
            for v in (ffn1_pre_g[0], mix_pre_g[0], ffn2_pre_g[0]):
                sp.dma_start(rows[n_rows:n_rows + ND, :], v.rearrange("(k p) -> k p", p=P)).then_inc(rows_in, 16)
                n_rows += ND
            sp.dma_start(rows[G_TAP:G_BIAS, :], conv_w[0].rearrange("j (k p) -> (j k) p", p=P)).then_inc(rows_in, 16)
            sp.dma_start(rows[G_BIAS:NROWS, :], conv_b[0].rearrange("(k p) -> k p", p=P)).then_inc(rows_in, 16)

            def load(c, slot, src, shape, first=False):
                if not first:
                    sp.wait_ge(lo_ready, 2 * c - 2 * RAW + 2)
                dst = raw[:, slot, :]
                if shape:
                    dst = dst.rearrange("p (k n) -> p k n", k=KC)
                sp.dma_start(dst, src).then_inc(raw_full[slot], 16)

            def by_columns(w, k0, col):
                return w.rearrange("(k p) n -> p k n", p=P)[:, k0:k0 + KC, bass.ds(col, COLS)]

            def up_block(e, i, first=False):
                for n, w in enumerate((WG[e], WU[e])):
                    for q in range(BLOCK_CHUNKS):
                        j = n * BLOCK_CHUNKS + q
                        load(C_UP[e] + i * 2 * BLOCK_CHUNKS + j, j % RAW, by_columns(w, KC * q, i * COLS), True,
                             first and j < RAW)

            def by_rows(w, base, n):
                with sp.Fori(0, n // RAW) as i:
                    for q in range(RAW):
                        load(base + i * RAW + q, q, w[bass.ds(i * (RAW * P) + q * P, P), :], False)

            for e in range(2):
                if e == 0:
                    up_block(0, 0, first=True)
                with sp.Fori(1 - e, NFB) as i:
                    up_block(e, i)
                by_rows(WD[e], C_DOWN[e], NF)
                if e == 0:
                    c = C_MIX
                    for _, _, col in IN_BLOCKS:
                        for q in range(BLOCK_CHUNKS):
                            load(c, c % RAW, by_columns(w_in[0], KC * q, col), True)
                            c += 1
                    for w in (w_attn_up[0], w_mlstm_up[0]):
                        with sp.Fori(0, NCB // 2) as i:
                            for b in range(2):
                                for q in range(UP_BLOCK_CHUNKS):
                                    j = b * UP_BLOCK_CHUNKS + q
                                    load(c + i * 2 * UP_BLOCK_CHUNKS + j, j % RAW,
                                         by_columns(w, KC * q, i * (2 * COLS) + b * COLS), True)
                        c += NCB * UP_BLOCK_CHUNKS
                    by_rows(w_out[0], C_OUT, ND)
            for cb in range(NCB):
                sp.wait_ge(h_ready, 2 * NCB + cb + 1)
                sp.dma_start(out[0].rearrange("(t p) d -> p t d", p=P)[:, :, cb * COLS:(cb + 1) * COLS],
                             h[:, :, cb * COLS:(cb + 1) * COLS]).then_inc(stored, 16)
            sp.wait_ge(stored, 16 * NCB)

        @block.gpsimd
        def _(pool):
            steps = [0]

            def step(ins):
                steps[0] += 1
                ins.then_inc(const_step, 1)
                pool.wait_ge(const_step, steps[0])

            step(pool.memset(ident[:, :], 0.0))
            step(pool.affine_select(out=ident[:, :], in_=ident[:, :], compare_op=ALU.not_equal, fill=1.0, base=0,
                                    pattern=[[-1, P]], channel_multiplier=1))
            pool.memset(neg_half[:, :], -0.5).then_inc(const_ready, 1)
            pool.memset(ones[:, :], 1.0).then_inc(const_ready, 1)
            pool.dma_start(gain[:, :], ffn1_post_g.to_broadcast([P, D])).then_inc(gain_in, 16)
            with nc.allow_non_contiguous_dma(reason="a few gate columns and biases"):
                pool.dma_start(wg_raw[:, :, :], w_in[0].rearrange("(k p) n -> p k n", p=P)[:, :, OFF_GATES:OFF_GA]).then_inc(wg_in, 16)
                pool.dma_start(gate_b[:, 0:1], m_igate_b.rearrange("a h -> h a")).then_inc(misc_in, 16)
                pool.dma_start(gate_b[:, 1:2], m_fgate_b.rearrange("a h -> h a")).then_inc(misc_in, 16)
            pool.dma_start(sinks[:, :], attn_sinks.to_broadcast([P, HEADS])).then_inc(misc_in, 16)
            pool.dma_start(head_g[:, :], m_head_g.to_broadcast([P, MV])).then_inc(misc_in, 16)
            step(pool.iota(dist[:, :], pattern=[[-1, 2 * P]], base=P, channel_multiplier=1,
                           allow_small_or_imprecise_dtypes=True))
            step(pool.affine_select(out=dist[:, :], in_=dist[:, :], compare_op=ALU.is_ge, fill=-MASKED, base=P,
                                    pattern=[[-1, 2 * P]], channel_multiplier=1))
            step(pool.affine_select(out=dist[:, :], in_=dist[:, :], compare_op=ALU.is_gt, fill=-MASKED, base=0,
                                    pattern=[[1, 2 * P]], channel_multiplier=-1))
            step(pool.memset(future[:, :], 0.0))
            step(pool.affine_select(out=future[:, :], in_=future[:, :], compare_op=ALU.is_ge, fill=MASKED, base=0,
                                    pattern=[[1, P]], channel_multiplier=-1))
            step(pool.memset(sel[:, :, :], 0.0))
            pool.affine_select(out=sel[:, :, :], in_=sel[:, :, :], compare_op=ALU.not_equal, fill=-1.0, base=0,
                               pattern=[[-1, MH], [0, P]], channel_multiplier=1).then_inc(const_ready, 1)

            def inverse_root(ms, dst, wait, count, done):
                pool.wait_ge(wait, count)
                pool.tensor_tensor(dst, ms, neg_half[:, 0:ms.shape[1]], ALU.pow).then_inc(done, 1)

            pool.wait_ge(const_ready, 3)
            inverse_root(ms_h, rs_h, h_ms, 1, h_rstd)
            inverse_root(ms_y, rs_y, y_ms, 1, y_rstd)
            pool.wait_ge(h_ready, NCB)
            pool.memset(mval[:, :, :, VD:VD + 1], 1.0).then_inc(ones_v, 1)
            pool.memset(conv_in[:, :, 0:CONV - 1], 0.0).then_inc(ones_v, 1)
            inverse_root(ms_h, rs_h, h_ms, 2, h_rstd)
            for b in range(NT):
                inverse_root(ms_m[:, b, :], rs_m[:, b, :], m_ms, b + 1, m_rstd)
            pool.wait_ge(att_split_lo, 4)
            pool.dma_start(gain[:, :], mix_post_g.to_broadcast([P, D])).then_inc(gain_in, 16)
            inverse_root(ms_y, rs_y, y_ms, 2, y_rstd)
            inverse_root(ms_h, rs_h, h_ms, 3, h_rstd)
            pool.wait_ge(h_ready, 2 * NCB)
            pool.dma_start(gain[:, :], ffn2_post_g.to_broadcast([P, D])).then_inc(gain_in, 16)
            inverse_root(ms_y, rs_y, y_ms, 3, y_rstd)

        @block.scalar
        def _(act):
            steps = [0]

            def step(ins):
                steps[0] += 1
                ins.then_inc(act_step, 1)
                act.wait_ge(act_step, steps[0])

            def split_hi(H, half, slot, hw, raw_wait, first=False):
                if half == 0:
                    act.wait_ge(raw_full[slot], raw_wait)
                if not first:
                    act.wait_ge(w_used, H - SPL + 1)
                act.activation(w_hi[:, hw, :], raw[:, slot, half * HALF:(half + 1) * HALF], ACT.Copy).then_inc(hi_ready, 1)

            def split_static(H, first=False):
                c = H // 2
                split_hi(H, H % 2, c % RAW, H % SPL, 16 * (c // RAW + 1), first)

            dropped = hid[:, 0:NT * D // SEQ, :].rearrange("p a b -> p (a b)")

            def turn_in(e):
                for u in range(ND // 2):
                    act.wait_ge(h_turned, e * ND // 2 + u + 1)
                    for kk in range(2):
                        k = 2 * u + kk
                        ins = act.activation(x_hi[:, k, :], ps[:, u % 4, kk * SEQ:(kk + 1) * SEQ], ACT.Identity,
                                             scale=cols[:, G_PRE[e] + k:G_PRE[e] + k + 1])
                    ins.then_inc(x_hi_ready, 1)
                if e == 0:
                    act.wait_ge(x_in, 16)
                for t in range(NT):
                    act.activation(dropped[:, t * D:(t + 1) * D], h[:, t, :], ACT.Square, accum_out=sq_h[:, t:t + 1]).then_inc(h_squared, 1)

            def silu_gate(e, i, base, started):
                act.wait_ge(w_used, 2 * C_UP[e] + i * 4 * BLOCK_CHUNKS + 2 * BLOCK_CHUNKS)
                if started:
                    act.wait_ge(prod_ready, e * NFB + i)
                for t in range(NT):
                    ins = act.activation(silu[:, t, :], ps[:, base + t, :], ACT.Silu, scale=rs_h[:, t:t + 1])
                ins.then_inc(silu_ready, 1)

            def copy_hidden(e, i, base):
                act.wait_ge(prod_turned, e * NFB + i + 1)
                act.activation(hid[:, bass.ds(i * 4, 2), :], ps[:, base, :].rearrange("p (a b) -> p a b", a=2),
                               ACT.Copy).then_inc(hid_a, 1)

            def up_block(e, i, even, first, very_first=False):
                base = 4 if even else 0
                for j in range(4 * BLOCK_CHUNKS):
                    c = j // 2
                    H = 2 * C_UP[e] + i * 4 * BLOCK_CHUNKS + j
                    split_hi(H, j % 2, c % RAW, j % SPL, (i * 2 + C_UP[e] // RAW + c // RAW + 1) * 16,
                             very_first and j < SPL)
                    if j == 7 and not first:
                        copy_hidden(e, i - 1, 4 - base)
                    if j == 10:
                        if first:
                            act.wait_ge(h_rstd, e * 2 + 1)
                        silu_gate(e, i, base, not first)

            def x_split(T, n, slot, phase):
                act.activation(x_hi[:, slot, :], src_tile(phase, n), ACT.Copy).then_inc(xs_hi_ready, 1)

            def rows_quad(base_c, T0, i, phase, e=None, tail=None):
                for q in range(RAW):
                    for half in range(2):
                        H = 2 * base_c + i * 2 * RAW + 2 * q + half
                        split_hi(H, half, q, (2 * q + half) % SPL, (i + base_c // RAW + 1) * 16)
                        if half == 0:
                            if phase == "down":
                                act.wait_ge(hid_a, e * NFB + i + 1)
                                act.wait_ge(hid_v, e * NFB + i + 1)
                            elif q == 0:
                                act.wait_ge(yt_a, NCB)
                                act.wait_ge(yt_v, NCB)
                            x_split(T0 + i * RAW + q, i * RAW + q, q, phase)
                        if tail and 2 * q + half == 3:
                            tail()

            def squares_of_y(p):
                for cb in range(NCB):
                    act.wait_ge(w_used, Y_END[p] - 1 + cb // 2)
                    for t in range(NT):
                        c = (2 * cb + t) * COLS
                        ins = act.activation(dropped[:, c:c + COLS], ps[:, 2 * cb + t, :], ACT.Square,
                                             accum_out=sq_y[:, t, cb:cb + 1])
                    ins.then_inc(y_squared, 1)

            def swiglu(e):
                up_block(e, 0, True, True, very_first=(e == 0))
                with act.Fori(0, NFB // 2) as it:
                    up_block(e, it * 2 + 1, False, False)
                    up_block(e, it * 2 + 2, True, False)
                rows_quad(C_DOWN[e], T_DOWN[e], 0, "down", e,
                          tail=lambda: copy_hidden(e, NFB - 1, 4))
                with act.Fori(1, NF // RAW) as i:
                    rows_quad(C_DOWN[e], T_DOWN[e], i, "down", e)

            act.wait_ge(rows_turned, 1)
            act.activation(cols[:, 0:NROWS], ps[:, 7, 0:NROWS], ACT.Copy).then_inc(cols_ready, 1)
            act.wait_ge(cols_ready, 1)
            act.wait_ge(wg_in, 16)
            act.activation(wg_hi[:, :, :], wg_raw[:, :, :], ACT.Copy).then_inc(wg_hi_ready, 1)
            turn_in(0)
            swiglu(0)
            squares_of_y(0)
            turn_in(1)
            act.wait_ge(h_rstd, 2)

            def evacuate(b):
                kind, j = kinds[b], IN_BLOCKS[b][1] if b < NIN else 0
                bank = 4 + 2 * (b % 2)
                if kind in ("A", "M"):
                    return
                act.wait_ge(w_used, H_MIX + ends(b) + 1)
                if kind == "k":
                    act.wait_ge(ones_v, 2)
                    act.activation(stage[:, 0, :].rearrange("p (h r d) -> p h r d", h=KVH, r=2),
                                   ps[:, bank, 0:ATT_KV].rearrange("p (h r d) -> p h r d", h=KVH, r=1).to_broadcast([P, KVH, 2, HD]),
                                   ACT.Identity, scale=rs_h[:, 0:1])
                    act.activation(att_v[:, 0, :], ps[:, bank, ATT_KV:2 * ATT_KV], ACT.Identity,
                                   scale=rs_h[:, 0:1]).then_inc(ev_a, 1)
                elif kind in ("q", "mqk"):
                    act.wait_ge(stage_turned, b)
                    if kind == "q":
                        act.wait_ge(q_scale, 1)
                    act.activation(stage[:, 0, :], ps[:, bank, :], ACT.Identity,
                                   scale=(rs_q if kind == "q" else rs_h)[:, 0:1]).then_inc(ev_a, 1)
                elif kind == "mv":
                    act.activation(mval[:, 0, 2 * j:2 * j + 2, 0:VD], ps[:, bank, :].rearrange("p (h d) -> p h d", h=2),
                                   ACT.Identity, scale=rs_h[:, 0:1]).then_inc(ev_a, 1)
                else:
                    for t in range(NT):
                        if kind == "mo":
                            dst = smo[:, t, j * COLS:(j + 1) * COLS]
                        elif kind == "ga":
                            dst = y[:, t, j * COLS:(j + 1) * COLS]
                        else:
                            dst = gm[:, j, t * COLS:(t + 1) * COLS]
                        ins = act.activation(dst, ps[:, bank + t, :], ACT.Sigmoid, scale=rs_h[:, t:t + 1])
                    ins.then_inc(ev_a, 1)

            def copy_y(j):
                act.wait_ge(y_turned, j + 1)
                act.activation(y_T[:, 4 * j:4 * j + 2, :], ps[:, 2 * (j % 2), :].rearrange("p (a n) -> p a n", a=2),
                               ACT.Copy).then_inc(yt_a, 1)

            def turned_tile(b, a):
                if b == 0:
                    return att_kT[:, 2 * a:2 * a + 2, :]
                if b < 3:
                    return att_qT[:, 4 * (b - 1) + 2 * a:4 * (b - 1) + 2 * a + 2, :]
                return conv_in[:, 4 * (b - 3) + 2 * a:4 * (b - 3) + 2 * a + 2, CONV - 1:CP]

            for s in range(END_SLOT):
                split_static(H_MIX + s)
                if s == 8:
                    act.wait_ge(gate_rows, 1)
                    act.wait_ge(const_ready, 3)
                    step(act.activation(rows4[:, 2, :], rows4[:, 1, :], ACT.Abs))
                    step(act.activation(rows4[:, 2, :], rows4[:, 2, :], ACT.Exp, scale=-1.0))
                    act.activation(rows4[:, 2, :], rows4[:, 2, :], ACT.Ln, bias=ones[0:MH, 0:1]).then_inc(log_ready, 1)
                if s == 16:
                    act.wait_ge(r_turned, 1)
                    act.activation(e_col, ps[:, 1, 0:16].rearrange("p (t k h) -> p t k h", t=NT, k=2)[:, :, 1, :],
                                   ACT.Exp, scale=-1.0).then_inc(e_cols, 1)
                if s in EVAC_AT:
                    evacuate(EVAC_AT[s])
                if s in TURN_COPY:
                    b = TURN_COPY[s]
                    act.wait_ge(stage_turned, b + 1)
                    act.activation(turned_tile(b, 0), ps[:, 0, :].rearrange("p (a n) -> p a n", a=2),
                                   ACT.Copy).then_inc(turn_a, 1)
                if s in SILU_AT:
                    q = SILU_AT[s]
                    act.wait_ge(conv_ready, 4 * q + 4)
                    for c in range(4 * q, 4 * q + 4):
                        ins = act.activation(conv_out[:, c, :], conv_out[:, c, :], ACT.Silu,
                                             bias=cols[:, G_BIAS + c:G_BIAS + c + 1])
                    ins.then_inc(conv_silu, 1)
                g = group_at(s, 4)
                if g is not None:
                    K = P * (g % 2 + 1)
                    st = a_stat[:, g % 2]
                    act.wait_ge(maxed, g + 1)
                    for hh in range(GROUP):
                        act.activation(probs[:, g % 2, hh * K:(hh + 1) * K], probs[:, g % 2, hh * K:(hh + 1) * K],
                                       ACT.Exp, bias=st[:, 2, hh:hh + 1], accum_out=st[:, 4, hh:hh + 1])
                    act.activation(st[:, 5, :], st[:, 3, :], ACT.Exp).then_inc(exped, 1)
                g = group_at(s, 7)
                if g is not None:
                    act.wait_ge(p_turned, g + 1)
                    act.activation(probs_T[:, g % 2, 0:COLS], ps[:, 2, :], ACT.Copy).then_inc(pt_a, 1)
                g = group_at(s, 9)
                if g is not None:
                    j, b = divmod(g, 2)
                    act.wait_ge(pv_done, g + 1)
                    act.activation(att[:, 2 * j:2 * j + 2, b * P:(b + 1) * P],
                                   ps[:, 2, 0:2 * P].rearrange("p (a n) -> p a n", a=2), ACT.Copy).then_inc(pv_out, 1)
                if s == 88:
                    act.wait_ge(wt_arg, 1)
                    act.wait_ge(r_cols, 1)
                    for hd in range(MH):
                        act.activation(wt[:, hd, 0:SEQ], wt[:, hd, 0:SEQ], ACT.Exp, bias=r_col[:, 0, hd:hd + 1])
                        ins = act.activation(wt[:, hd, SEQ:WTN], wt[:, hd, SEQ:WTN], ACT.Exp, bias=r_col[:, 1, hd:hd + 1])
                    ins.then_inc(wt_ready, 1)
                for b in range(NT):
                    if s == 97 + 6 * b:
                        act.wait_ge(rden_ready, b + 1)
                        for hd in range(2):
                            ins = act.activation(m_h[:, b, hd * VD:(hd + 1) * VD], ps[:, hd, 0:VD], ACT.Identity,
                                                 scale=rden[:, b, hd:hd + 1])
                        ins.then_inc(mh_a, 1)
                        act.wait_ge(mh_v, b + 1)
                        act.wait_ge(mh_a, b + 1)
                        for hd in range(MH):
                            ins = act.activation(gm[:, b, hd * VD:(hd + 1) * VD], m_h[:, b, hd * VD:(hd + 1) * VD], ACT.Square,
                                                 accum_out=sq_m[:, b, hd:hd + 1])
                        ins.then_inc(m_squared, 1)
                if s == 115:
                    act.wait_ge(m_turned, 1)
                    act.activation(m_T[:, 0:4, :], ps[:, 0:2, :].rearrange("p a (c n) -> p (a c) n", c=2),
                                   ACT.Copy).then_inc(mt_a, 1)
                if SPLIT_SLOT <= s < SPLIT_SLOT + 8:
                    q = s - SPLIT_SLOT
                    if q == 4:
                        act.wait_ge(mt_a, 1)
                        act.wait_ge(mt_v, 1)
                    src = att if q < 4 else m_T
                    act.activation(x_hi[:, 2 * q:2 * q + 2, :], src[:, 2 * (q % 4):2 * (q % 4) + 2, :],
                                   ACT.Copy).then_inc(att_split, 1)
                for j in range(NCB - 2):
                    if s == evac_slot(NIN + NCB + j) + 3:
                        copy_y(j)
            for j in range(NCB - 2, NCB):
                copy_y(j)
            with act.Fori(0, ND // RAW) as i:
                rows_quad(C_OUT, T_OUT, i, "out")
            squares_of_y(1)
            turn_in(2)
            swiglu(1)
            squares_of_y(2)

        @block.vector
        def _(dve):
            steps = [0]

            def step(ins):
                steps[0] += 1
                ins.then_inc(dve_step, 1)
                dve.wait_ge(dve_step, steps[0])

            def split_lo(H, half, slot, hw):
                dve.wait_ge(hi_ready, H + 1)
                dve.tensor_tensor(w_lo[:, hw, :], raw[:, slot, half * HALF:(half + 1) * HALF],
                                  w_hi[:, hw, :].bitcast(F32), ALU.subtract).then_inc(lo_ready, 1)

            def turn_in_pair(e, u):
                dve.wait_ge(x_hi_ready, e * ND // 2 + u + 1)
                for kk in range(2):
                    k = 2 * u + kk
                    ins = dve.scalar_tensor_tensor(out=x_lo[:, k, :], in0=ps[:, u % 4, kk * SEQ:(kk + 1) * SEQ],
                                                   scalar=cols[:, G_PRE[e] + k:G_PRE[e] + k + 1],
                                                   in1=x_hi[:, k, :].bitcast(F32), op0=ALU.mult, op1=ALU.subtract)
                ins.then_inc(x_lo_ready, 1)

            def mean_square_h(e):
                dve.wait_ge(h_squared, 2 * e + 2)
                dve.tensor_scalar(ms_h, sq_h, 1.0 / D, EPS, ALU.mult, ALU.add).then_inc(h_ms, 1)

            def post(p, factor):
                dve.wait_ge(y_squared, NCB * (p + 1))
                step(dve.tensor_reduce(ms_y, sq_y, AX.X, ALU.add))
                dve.tensor_scalar(ms_y, ms_y, 1.0 / D, EPS, ALU.mult, ALU.add).then_inc(y_ms, 1)
                dve.wait_ge(y_rstd, p + 1)
                dve.wait_ge(gain_in, 16 * (p + 1))
                step(dve.tensor_scalar(rs_yh, rs_y, factor, None, ALU.mult))
                for cb in range(NCB):
                    c = slice(cb * COLS, (cb + 1) * COLS)
                    normed_y = (prod, silu)[cb % 2]
                    if cb >= 2:
                        dve.wait_ge(h_ready, NCB * p + cb - 1)
                    for t in range(NT):
                        ins = dve.scalar_tensor_tensor(out=normed_y[:, t, :], in0=ps[:, 2 * cb + t, :],
                                                       scalar=rs_yh[:, t:t + 1], in1=gain[:, c],
                                                       op0=ALU.mult, op1=ALU.mult)
                    step(ins)
                    for t in range(NT):
                        ins = dve.tensor_tensor(h[:, t, c], h[:, t, c], normed_y[:, t, :], ALU.add)
                    ins.then_inc(h_ready, 1)
                    if p < 2 and cb >= 1:
                        turn_in_pair(p + 1, 2 * cb - 2)
                        turn_in_pair(p + 1, 2 * cb - 1)
                if p < 2:
                    turn_in_pair(p + 1, 2 * NCB - 2)
                    turn_in_pair(p + 1, 2 * NCB - 1)
                    mean_square_h(p + 1)

            def gated(e, i, base, first=False):
                dve.wait_ge(w_used, 2 * C_UP[e] + i * 4 * BLOCK_CHUNKS + 4 * BLOCK_CHUNKS)
                dve.wait_ge(silu_ready, e * NFB + i + 1)
                if not first:
                    dve.wait_ge(prod_turned, e * NFB + i)
                for t in range(NT):
                    ins = dve.scalar_tensor_tensor(out=prod[:, t, :], in0=ps[:, base + 2 + t, :],
                                                   scalar=rs_h[:, t:t + 1], in1=silu[:, t, :],
                                                   op0=ALU.mult, op1=ALU.mult)
                ins.then_inc(prod_ready, 1)

            def copy_hidden(e, i, base):
                dve.wait_ge(prod_turned, e * NFB + i + 1)
                dve.tensor_copy(hid[:, bass.ds(i * 4 + 2, 2), :],
                                ps[:, base + 1, :].rearrange("p (a b) -> p a b", a=2)).then_inc(hid_v, 1)

            def up_block(e, i, even, first):
                base = 4 if even else 0
                for j in range(4 * BLOCK_CHUNKS):
                    split_lo(2 * C_UP[e] + i * 4 * BLOCK_CHUNKS + j, j % 2, (j // 2) % RAW, j % SPL)
                    if j == 2 and not first:
                        gated(e, i - 1, 4 - base, first=isinstance(i, int) and i == 1)
                    if j == 7 and not first:
                        copy_hidden(e, i - 1, 4 - base)

            def rows_quad(base_c, T0, i, phase, e=None, tail=False):
                for q in range(RAW):
                    for half in range(2):
                        split_lo(2 * base_c + i * 2 * RAW + 2 * q + half, half, q, (2 * q + half) % SPL)
                        if half == 0:
                            dve.wait_ge(xs_hi_ready, T0 + i * RAW + q + 1)
                            dve.tensor_tensor(x_lo[:, q, :], src_tile(phase, i * RAW + q), x_hi[:, q, :].bitcast(F32),
                                              ALU.subtract).then_inc(xs_lo_ready, 1)
                        if tail and 2 * q + half == 2:
                            gated(e, NFB - 1, 4)
                        if tail and 2 * q + half == 3:
                            copy_hidden(e, NFB - 1, 4)

            def swiglu(e):
                up_block(e, 0, True, True)
                up_block(e, 1, False, False)
                up_block(e, 2, True, False)
                with dve.Fori(1, NFB // 2) as it:
                    up_block(e, it * 2 + 1, False, False)
                    up_block(e, it * 2 + 2, True, False)
                rows_quad(C_DOWN[e], T_DOWN[e], 0, "down", e, tail=True)
                with dve.Fori(1, NF // RAW) as i:
                    rows_quad(C_DOWN[e], T_DOWN[e], i, "down", e)

            dve.wait_ge(wg_hi_ready, 1)
            dve.tensor_tensor(wg_lo[:, :, :], wg_raw[:, :, :], wg_hi[:, :, :].bitcast(F32), ALU.subtract).then_inc(wg_lo_ready, 1)
            for u in range(ND // 2):
                turn_in_pair(0, u)
            mean_square_h(0)
            swiglu(0)
            post(0, 0.5)
            dve.wait_ge(h_rstd, 2)
            dve.tensor_scalar(rs_q, rs_h, HD ** -0.5, None, ALU.mult).then_inc(q_scale, 1)
            dve.wait_ge(q_scale, 1)

            def evacuate(b):
                kind, j = kinds[b], IN_BLOCKS[b][1] if b < NIN else (b - NIN) % NCB
                bank = 4 + 2 * (b % 2)
                if kind in ("mo", "ga", "gm"):
                    return
                dve.wait_ge(w_used, H_MIX + ends(b) + 1)
                if kind == "k":
                    dve.wait_ge(ones_v, 2)
                    dve.tensor_scalar(stage[:, 1, :].rearrange("p (h r d) -> p h r d", h=KVH, r=2),
                                      ps[:, bank + 1, 0:ATT_KV].rearrange("p (h r d) -> p h r d", h=KVH, r=1).to_broadcast([P, KVH, 2, HD]),
                                      rs_h[:, 1:2], None, ALU.mult)
                    dve.tensor_scalar(att_v[:, 1, :], ps[:, bank + 1, ATT_KV:2 * ATT_KV], rs_h[:, 1:2], None,
                                      ALU.mult).then_inc(ev_v, 1)
                elif kind in ("q", "mqk"):
                    dve.wait_ge(stage_turned, b)
                    dve.tensor_scalar(stage[:, 1, :], ps[:, bank + 1, :], (rs_q if kind == "q" else rs_h)[:, 1:2],
                                      None, ALU.mult).then_inc(ev_v, 1)
                elif kind == "mv":
                    dve.tensor_scalar(mval[:, 1, 2 * j:2 * j + 2, 0:VD], ps[:, bank + 1, :].rearrange("p (h d) -> p h d", h=2),
                                      rs_h[:, 1:2], None, ALU.mult).then_inc(ev_v, 1)
                else:
                    c = slice(j * COLS, (j + 1) * COLS)
                    if kind == "A":
                        dve.wait_ge(ev_a, act_evacs(8 + 1 + j))
                        for t in range(NT):
                            ins = dve.tensor_tensor(y[:, t, c], ps[:, bank + t, :], y[:, t, c], ALU.mult)
                        ins.then_inc(ev_v, 1)
                    else:
                        dve.wait_ge(ev_a, act_evacs(8 + 1 + 4 + j))
                        for t in range(NT):
                            g_t = gm[:, j, t * COLS:(t + 1) * COLS]
                            ins = dve.tensor_tensor(g_t, ps[:, bank + t, :], g_t, ALU.mult)
                        ins.then_inc(ev_v, 1)
                        dve.wait_ge(ev_v, dve_evacs(b))
                        for t in range(NT):
                            ins = dve.tensor_tensor(y[:, t, c], y[:, t, c], gm[:, j, t * COLS:(t + 1) * COLS], ALU.add)
                        ins.then_inc(y_ready, 1)

            def copy_y(j):
                dve.wait_ge(y_turned, j + 1)
                dve.tensor_copy(y_T[:, 4 * j + 2:4 * j + 4, :],
                                ps[:, 2 * (j % 2) + 1, :].rearrange("p (a n) -> p a n", a=2)).then_inc(yt_v, 1)

            def turned_tile(b, a):
                if b == 0:
                    return att_kT[:, 2 * a:2 * a + 2, :]
                if b < 3:
                    return att_qT[:, 4 * (b - 1) + 2 * a:4 * (b - 1) + 2 * a + 2, :]
                return conv_in[:, 4 * (b - 3) + 2 * a:4 * (b - 3) + 2 * a + 2, CONV - 1:CP]

            for s in range(END_SLOT):
                H = H_MIX + s
                split_lo(H, H % 2, (H // 2) % RAW, H % SPL)
                if s == 3:
                    dve.wait_ge(gates_done, 1)
                    for t in range(NT):
                        ins = dve.tensor_scalar(gates_tok[:, t, :], ps[:, 0, t * 2 * MH:(t + 1) * 2 * MH],
                                                rs_h[:, t:t + 1], None, ALU.mult)
                    ins.then_inc(gates_ready, 1)
                if s == 7:
                    dve.wait_ge(gates_turned, 1)
                    dve.wait_ge(misc_in, 64)
                    for n in range(2):
                        ins = dve.tensor_scalar(rows4[:, n, :], ps[0:MH, 1, n * SEQ:(n + 1) * SEQ],
                                                gate_b[:, n:n + 1], None, ALU.add)
                    ins.then_inc(gate_rows, 1)
                if s == 11:
                    dve.wait_ge(log_ready, 1)
                    dve.wait_ge(const_ready, 3)
                    i_r, f_R, l_m, F_ = (rows4[:, n, :] for n in range(4))
                    step(dve.scalar_tensor_tensor(out=l_m, in0=f_R, scalar=0.0, in1=l_m, op0=ALU.min, op1=ALU.subtract))
                    step(dve.tensor_tensor_scan(F_, ones[0:MH, :], l_m, 0.0, ALU.mult, ALU.add))
                    step(dve.tensor_tensor(i_r, i_r, F_, ALU.subtract))
                    step(dve.tensor_tensor_scan(f_R, ones[0:MH, :], i_r, 0.0, ALU.mult, ALU.max))
                    dve.tensor_tensor(l_m, F_, f_R, ALU.add).then_inc(rows_ready, 1)
                if s == 16:
                    dve.wait_ge(e_cols, 1)
                    dve.tensor_copy(r_col, ps[:, 1, 0:16].rearrange("p (t k h) -> p t k h", t=NT, k=2)[:, :, 0, :]).then_inc(r_cols, 1)
                if s in EVAC_AT:
                    evacuate(EVAC_AT[s])
                if s in TURN_COPY:
                    b = TURN_COPY[s]
                    dve.wait_ge(stage_turned, b + 1)
                    dve.tensor_copy(turned_tile(b, 1), ps[:, 1, :].rearrange("p (a n) -> p a n", a=2)).then_inc(turn_v, 1)
                if s in CONV_AT:
                    q, c4 = CONV_AT[s]
                    c = 4 * q + c4
                    dve.wait_ge(turn_a, 4 + q)
                    dve.wait_ge(turn_v, 4 + q)

                    def tap(j):
                        n = G_TAP + j * 2 * MQK // P + c
                        return cols[:, n:n + 1]

                    step(dve.tensor_scalar(conv_out[:, c, :], conv_in[:, c, 0:SEQ], tap(0), None, ALU.mult))
                    for j in range(1, CONV):
                        ins = dve.scalar_tensor_tensor(out=conv_out[:, c, :], in0=conv_in[:, c, j:j + SEQ], scalar=tap(j),
                                                       in1=conv_out[:, c, :], op0=ALU.mult, op1=ALU.add)
                        if j < CONV - 1:
                            step(ins)
                    ins.then_inc(conv_ready, 1)
                g = group_at(s, 3)
                if g is not None:
                    j, b = divmod(g, 2)
                    K = P * (b + 1)
                    st = a_stat[:, g % 2]
                    dve.wait_ge(scored, g + 1)
                    for hh in range(GROUP):
                        slope = float(np.exp2(np.float32(-8.0 * (GROUP * j + hh + 1) / HEADS)))
                        off = (hh // 2) * K
                        ins = dve.scalar_tensor_tensor(out=probs[:, g % 2, hh * K:(hh + 1) * K], in0=dist[:, 2 * P - K:2 * P],
                                                       scalar=-slope, in1=ps[:, hh % 2, off:off + K],
                                                       op0=ALU.mult, op1=ALU.add)
                    step(ins)
                    step(dve.tensor_reduce(st[:, 0, :], probs[:, g % 2, 0:GROUP * K].rearrange("p (h k) -> p h k", h=GROUP),
                                           AX.X, ALU.max))
                    sink = sinks[:, GROUP * j:GROUP * (j + 1)]
                    step(dve.tensor_tensor(st[:, 1, :], st[:, 0, :], sink, ALU.max))
                    dve.tensor_scalar(st[:, 2, :], st[:, 1, :], -1.0, None, ALU.mult)
                    dve.tensor_tensor(st[:, 3, :], sink, st[:, 1, :], ALU.subtract).then_inc(maxed, 1)
                g = group_at(s, 5)
                if g is not None:
                    K = P * (g % 2 + 1)
                    st = a_stat[:, g % 2]
                    dve.wait_ge(exped, g + 1)
                    step(dve.tensor_tensor(st[:, 6, :], st[:, 4, :], st[:, 5, :], ALU.add))
                    step(dve.reciprocal(st[:, 7, :], st[:, 6, :]))
                    pv = probs[:, g % 2, 0:GROUP * K].rearrange("p (h k) -> p h k", h=GROUP)
                    dve.tensor_tensor(pv, pv, st[:, 7, :].rearrange("p (h k) -> p h k", k=1).to_broadcast([P, GROUP, K]),
                                      ALU.mult).then_inc(normed, 1)
                g = group_at(s, 7)
                if g is not None and g % 2:
                    dve.wait_ge(p_turned, g + 1)
                    dve.tensor_copy(probs_T[:, g % 2, COLS:2 * COLS], ps[:, 3, :]).then_inc(pt_v, 1)
                if s == 80:
                    dve.wait_ge(ev_a, act_evacs(8))
                    for t in range(NT):
                        ins = dve.tensor_tensor(smo[:, t, :], smo[:, t, :], head_g[:, :], ALU.mult)
                    step(ins)
                if s == 87:
                    dve.wait_ge(neg_r, 1)
                    bc = ps[:, 0:2, :].rearrange("p a (c n) -> p (a c) n", c=2)
                    fut = future[:, :].rearrange("p (a n) -> p a n", a=1).to_broadcast([P, MH, P])
                    dve.tensor_tensor(wt[:, :, 0:P], bc[:, :, 0:P], fut, ALU.add)
                    dve.tensor_copy(wt[:, :, P:2 * P], bc[:, :, P:2 * P])
                    dve.tensor_tensor(wt[:, :, 2 * P:3 * P], bc[:, :, P:2 * P], fut, ALU.add).then_inc(wt_arg, 1)
                if s == 93:
                    dve.wait_ge(m_scored, 1)
                    dve.wait_ge(wt_ready, 1)
                    for hd in range(MH):
                        ins = dve.scalar_tensor_tensor(out=pt_m[:, hd, :], in0=ps[:, hd, 0:WTN], scalar=float(QKD) ** -0.5,
                                                       in1=wt[:, hd, :], op0=ALU.mult, op1=ALU.mult)
                    ins.then_inc(pt_m_ready, 1)
                for b in range(NT):
                    if s == 97 + 6 * b:
                        dve.wait_ge(num_done, b + 1)
                        dve.wait_ge(e_cols, 1)
                        d = den[:, b, :]
                        step(dve.tensor_copy(d, ps[:, 0:MH, VD]))
                        step(dve.scalar_tensor_tensor(out=d, in0=d, scalar=-1.0, in1=d, op0=ALU.mult, op1=ALU.max))
                        step(dve.tensor_tensor(d, d, e_col[:, b, :], ALU.max))
                        dve.reciprocal(rden[:, b, :], den[:, b, :]).then_inc(rden_ready, 1)
                        dve.wait_ge(rden_ready, b + 1)
                        for hd in range(2, MH):
                            ins = dve.tensor_scalar(m_h[:, b, hd * VD:(hd + 1) * VD], ps[:, hd, 0:VD], rden[:, b, hd:hd + 1],
                                                    None, ALU.mult)
                        ins.then_inc(mh_v, 1)
                    if s == 99 + 6 * b:
                        dve.wait_ge(m_squared, b + 1)
                        dve.tensor_scalar(ms_m[:, b, :], sq_m[:, b, :], 1.0 / VD, EPS, ALU.mult, ALU.add).then_inc(m_ms, 1)
                    if s == 101 + 6 * b:
                        dve.wait_ge(m_rstd, b + 1)
                        for hd in range(MH):
                            c = slice(hd * VD, (hd + 1) * VD)
                            ins = dve.scalar_tensor_tensor(out=smo[:, b, c], in0=m_h[:, b, c], scalar=rs_m[:, b, hd:hd + 1],
                                                           in1=smo[:, b, c], op0=ALU.mult, op1=ALU.mult)
                        ins.then_inc(m_rows, 1)
                if s == 115:
                    dve.wait_ge(m_turned, 1)
                    dve.tensor_copy(m_T[:, 4:8, :], ps[:, 2:4, :].rearrange("p a (c n) -> p (a c) n", c=2)).then_inc(mt_v, 1)
                if SPLIT_SLOT <= s < SPLIT_SLOT + 8:
                    q = s - SPLIT_SLOT
                    dve.wait_ge(att_split, q + 1)
                    src = att if q < 4 else m_T
                    dve.tensor_tensor(x_lo[:, 2 * q:2 * q + 2, :], src[:, 2 * (q % 4):2 * (q % 4) + 2, :],
                                      x_hi[:, 2 * q:2 * q + 2, :].bitcast(F32), ALU.subtract).then_inc(att_split_lo, 1)
                for j in range(NCB - 2):
                    if s == evac_slot(NIN + NCB + j) + 3:
                        copy_y(j)
            copy_y(NCB - 2)
            evacuate(NIN + 2 * NCB - 1)
            copy_y(NCB - 1)
            with dve.Fori(0, ND // RAW) as i:
                rows_quad(C_OUT, T_OUT, i, "out")
            post(1, 1.0)
            swiglu(1)
            post(2, 0.5)

        @block.tensor
        def _(pe):
            def three(dst, x_tile, t, w, n0, start, stop):
                xh = x_hi[:, x_tile, t * P:(t + 1) * P]
                pe.matmul(dst, xh, w_hi[:, w, n0:n0 + COLS], start=start, stop=False)
                pe.matmul(dst, xh, w_lo[:, w, n0:n0 + COLS], start=False, stop=False)
                return pe.matmul(dst, x_lo[:, x_tile, t * P:(t + 1) * P], w_hi[:, w, n0:n0 + COLS], start=False, stop=stop)

            def turn(dst, src):
                return pe.transpose(dst, src, ident[:, :])

            def turn_h(e):
                for cb in range(NCB):
                    if e:
                        pe.wait_ge(h_ready, (e - 1) * NCB + cb + 1)
                    for a in range(2):
                        u = 2 * cb + a
                        if u >= 4:
                            pe.wait_ge(x_lo_ready, e * ND // 2 + u - 3)
                        for kk in range(2):
                            for t in range(NT):
                                k = 2 * u + kk
                                ins = turn(ps[:, u % 4, kk * SEQ + t * P:kk * SEQ + (t + 1) * P], h[:, t, k * P:(k + 1) * P])
                        ins.then_inc(h_turned, 1)

            def turn_y(j):
                pe.wait_ge(y_ready, j + 1)
                if j >= 2:
                    pe.wait_ge(yt_a, j - 1)
                    pe.wait_ge(yt_v, j - 1)
                for c in range(4):
                    for t in range(NT):
                        n = (c % 2) * SEQ + t * P
                        ins = turn(ps[:, 2 * (j % 2) + c // 2, n:n + P], y[:, t, (4 * j + c) * P:(4 * j + c + 1) * P])
                ins.then_inc(y_turned, 1)

            def turn_hidden(e, i, base):
                pe.wait_ge(prod_ready, e * NFB + i + 1)
                pe.wait_ge(silu_ready, e * NFB + i + 1)
                for a in range(2):
                    for kk in range(2):
                        for t in range(NT):
                            c = (2 * a + kk) * P
                            ins = turn(ps[:, base + a, kk * SEQ + t * P:kk * SEQ + (t + 1) * P], prod[:, t, c:c + P])
                ins.then_inc(prod_turned, 1)

            def up_block(e, i, even, first, old):
                base = 4 if even else 0
                for j in range(4 * BLOCK_CHUNKS):
                    if old and j == 0:
                        pe.wait_ge(hid_a, e * NFB + i - 1)
                        pe.wait_ge(hid_v, e * NFB + i - 1)
                    if first and j < ND // 2:
                        pe.wait_ge(x_lo_ready, e * ND // 2 + j + 1)
                    n, q = divmod(j, 8)
                    H = 2 * C_UP[e] + i * 4 * BLOCK_CHUNKS + j
                    pe.wait_ge(lo_ready, H + 1)
                    for kk in range(2):
                        k = 2 * q + kk
                        for t in range(NT):
                            ins = three(ps[:, base + 2 * n + t, :], k, t, j % SPL, kk * COLS, k == 0, k == ND - 1)
                    ins.then_inc(w_used, 1)
                    if j == 4 and not first:
                        turn_hidden(e, i - 1, 4 - base)

            def row_half(H, T, slot, w, half, start, stop):
                pe.wait_ge(lo_ready, H + 1)
                pe.wait_ge(xs_lo_ready, T + 1)
                for t in range(NT):
                    for c in range(2):
                        ins = three(ps[:, 4 * half + 2 * c + t, :], slot, t, w, c * COLS, start, stop)
                ins.then_inc(w_used, 1)

            def rows_quad(base_c, T0, i, first, tail=None, last=False):
                for q in range(RAW):
                    for half in range(2):
                        j = 2 * q + half
                        if tail and j == 1:
                            tail()
                        row_half(2 * base_c + i * 2 * RAW + j, T0 + i * RAW + q, q, j % SPL, half,
                                 first and q == 0, last and q == RAW - 1)

            def by_rows(base_c, T0, n, tail=None):
                rows_quad(base_c, T0, 0, True, tail)
                if n > 2 * RAW:
                    with pe.Fori(1, n // RAW - 1) as i:
                        rows_quad(base_c, T0, i, False)
                rows_quad(base_c, T0, n // RAW - 1, False, last=True)

            def swiglu(e):
                up_block(e, 0, True, True, False)
                up_block(e, 1, False, False, False)
                up_block(e, 2, True, False, True)
                with pe.Fori(1, NFB // 2) as it:
                    up_block(e, it * 2 + 1, False, False, True)
                    up_block(e, it * 2 + 2, True, False, True)
                pe.wait_ge(hid_a, e * NFB + NFB - 1)
                pe.wait_ge(hid_v, e * NFB + NFB - 1)

                def tail():
                    turn_hidden(e, NFB - 1, 4)
                    pe.wait_ge(hid_a, (e + 1) * NFB)
                    pe.wait_ge(hid_v, (e + 1) * NFB)

                by_rows(C_DOWN[e], T_DOWN[e], NF, tail)

            pe.wait_ge(const_step, 2)
            pe.wait_ge(rows_in, 80)
            pe.transpose(ps[:, 7, 0:NROWS], rows[0:NROWS, :], ident[0:NROWS, 0:NROWS]).then_inc(rows_turned, 1)
            pe.wait_ge(x_in, 16)
            turn_h(0)
            swiglu(0)
            turn_h(1)

            pe.wait_ge(x_lo_ready, ND)
            pe.wait_ge(wg_lo_ready, 1)
            for t in range(NT):
                dst = ps[:, 0, t * 2 * MH:(t + 1) * 2 * MH]
                for k in range(ND):
                    xh = x_hi[:, k, t * P:(t + 1) * P]
                    pe.matmul(dst, xh, wg_hi[:, k, :], start=(k == 0), stop=False)
                    pe.matmul(dst, xh, wg_lo[:, k, :], start=False, stop=False)
                    ins = pe.matmul(dst, x_lo[:, k, t * P:(t + 1) * P], wg_hi[:, k, :], start=False, stop=(k == ND - 1))
            ins.then_inc(gates_done, 1)

            for s in range(END_SLOT):
                H = H_MIX + s
                if s < A_SLOT:
                    b, q = divmod(s, 8)
                    K, x0 = ND, 0
                else:
                    b, q = divmod(s - A_SLOT, 4)
                    b += NIN
                    K, x0 = UPK, 0 if s < M_SLOT else UPK
                    if b == NIN:
                        pe.wait_ge(att_split_lo, q + 1)
                    if b == NIN + NCB:
                        pe.wait_ge(att_split_lo, 4 + q + 1)
                banks = 4 + 2 * (b % 2)
                if q == 0 and b >= 2:
                    pe.wait_ge(ev_a, act_evacs(b - 2))
                    if dve_evacs(b - 2):
                        pe.wait_ge(ev_v, dve_evacs(b - 2))
                pe.wait_ge(lo_ready, H + 1)
                for kk in range(2):
                    k = 2 * q + kk
                    for t in range(NT):
                        ins = three(ps[:, banks + t, :], x0 + k, t, H % SPL, kk * COLS, k == 0, k == K - 1)
                ins.then_inc(w_used, 1)

                if s == 4:
                    pe.wait_ge(gates_ready, 1)
                    for n in range(2):
                        for t in range(NT):
                            ins = turn(ps[0:MH, 1, n * SEQ + t * P:n * SEQ + (t + 1) * P],
                                       gates_tok[:, t, n * MH:(n + 1) * MH])
                    ins.then_inc(gates_turned, 1)
                if s == 14:
                    pe.wait_ge(rows_ready, 1)
                    pe.wait_ge(turn_v, 1)
                    for t in range(NT):
                        for n, row in enumerate((0, 2)):
                            c = t * 2 * MH + n * MH
                            ins = pe.transpose(ps[:, 1, c:c + MH], rows4[:, row, t * P:(t + 1) * P], ident[0:MH, 0:MH])
                    ins.then_inc(r_turned, 1)
                if s in TURN_B:
                    b = TURN_B[s]
                    pe.wait_ge(ev_a, act_evacs(b))
                    pe.wait_ge(ev_v, dve_evacs(b))
                    if b == 0:
                        pe.wait_ge(gate_rows, 1)
                    if b == 1:
                        pe.wait_ge(r_cols, 1)
                    if b >= 2:
                        pe.wait_ge(maxed, b - 1)
                    if b:
                        pe.wait_ge(turn_a, b)
                        pe.wait_ge(turn_v, b)
                    for c in range(4):
                        for t in range(NT):
                            n = (c % 2) * SEQ + t * P
                            ins = turn(ps[:, c // 2, n:n + P], stage[:, t, c * P:(c + 1) * P])
                    ins.then_inc(stage_turned, 1)
                g = group_at(s, 0)
                if g is not None:
                    j, b = divmod(g, 2)
                    K = P * (b + 1)
                    turns = min(2 + g, 5)
                    pe.wait_ge(turn_a, turns)
                    pe.wait_ge(turn_v, turns)
                    if g:
                        pe.wait_ge(maxed, g)
                    for i in range(2):
                        for par in range(2):
                            lo, hi = par * HD, (par + 1) * HD
                            ins = pe.matmul(ps[:, par, i * K:(i + 1) * K], att_qT[lo:hi, 2 * j + i, b * P:(b + 1) * P],
                                            att_kT[lo:hi, j, 0:K], start=(i == 0), stop=(i == 1), skip_group_check=True)
                    ins.then_inc(scored, 1)
                g = group_at(s, 4)
                if g is not None:
                    j, b = divmod(g, 2)
                    K = P * (b + 1)
                    pe.wait_ge(normed, g + 1)
                    if g:
                        pe.wait_ge(pv_out, g)
                    if g >= 2:
                        pe.wait_ge(pt_v, g // 2)
                    for kt in range(b + 1):
                        for hh in range(GROUP):
                            n = ((hh % 2) * 2 + hh // 2) * P
                            ins = turn(ps[:, 2 + kt, n:n + P], probs[:, g % 2, hh * K + kt * P:hh * K + (kt + 1) * P])
                    ins.then_inc(p_turned, 1)
                g = group_at(s, 6)
                if g is not None:
                    j, b = divmod(g, 2)
                    pe.wait_ge(pt_a, g + 1)
                    if b:
                        pe.wait_ge(pt_v, g // 2 + 1)
                    for par in range(2):
                        for kt in range(b + 1):
                            n = kt * COLS + par * 2 * P
                            ins = pe.matmul(ps[par * HD:(par + 1) * HD, 2, 0:2 * P], att_v[:, kt, j * HD:(j + 1) * HD],
                                            probs_T[:, g % 2, n:n + 2 * P], start=(kt == 0), stop=(kt == b))
                    ins.then_inc(pv_done, 1)
                if s == 84:
                    pe.wait_ge(maxed, NG)
                    pe.wait_ge(const_ready, 3)
                    for hd in range(MH):
                        ins = pe.matmul(ps[:, hd // 2, (hd % 2) * SEQ:(hd % 2 + 1) * SEQ], sel[:, hd, :], rows4[:, 1, :],
                                        start=(hd % 2 == 0), stop=(hd % 2 == 1), skip_group_check=True)
                    ins.then_inc(neg_r, 1)
                if s == 90:
                    pe.wait_ge(conv_silu, 2)
                    pe.wait_ge(wt_arg, 1)
                    pe.wait_ge(pv_out, NG)
                    pe.wait_ge(pt_v, NG // 2)
                    for hd in range(MH):
                        pe.matmul(ps[:, hd, 0:SEQ], conv_out[:, MH + hd, 0:P], conv_out[:, hd, :], start=True, stop=False,
                                  skip_group_check=True)
                        ins = pe.matmul(ps[:, hd, SEQ:WTN], conv_out[:, MH + hd, P:SEQ], conv_out[:, hd, P:SEQ],
                                        start=False, stop=True, skip_group_check=True)
                    ins.then_inc(m_scored, 1)
                for b in range(NT):
                    if s == 94 + 6 * b:
                        if b:
                            pe.wait_ge(mh_a, 1)
                            pe.wait_ge(mh_v, 1)
                        else:
                            pe.wait_ge(pt_m_ready, 1)
                            pe.wait_ge(ones_v, 1)
                            pe.wait_ge(ev_a, act_evacs(6))
                            pe.wait_ge(ev_v, dve_evacs(6))
                        for hd in range(MH):
                            for a in range(b + 1):
                                c = (b if a == 0 else 2) * P
                                ins = pe.matmul(ps[:, hd, 0:VD + 1], pt_m[:, hd, c:c + P], mval[:, a, hd, :],
                                                start=(a == 0), stop=(a == b))
                        ins.then_inc(num_done, 1)
                if s == 112:
                    pe.wait_ge(m_rows, NT)
                    pe.wait_ge(mh_a, NT)
                    pe.wait_ge(mh_v, NT)
                    for c in range(2 * MH):
                        for t in range(NT):
                            n = (c % 2) * SEQ + t * P
                            ins = turn(ps[:, c // 2, n:n + P], smo[:, t, c * P:(c + 1) * P])
                    ins.then_inc(m_turned, 1)
                for j in range(NCB - 1):
                    if s == evac_slot(NIN + NCB + j):
                        turn_y(j)
            turn_y(NCB - 1)
            pe.wait_ge(yt_a, NCB)
            pe.wait_ge(yt_v, NCB)
            by_rows(C_OUT, T_OUT, ND)
            turn_h(2)
            swiglu(1)


_INS = ["x", "ffn1_pre_g", "ffn1_wg", "ffn1_wu", "ffn1_wd", "ffn1_post_g", "mix_pre_g", "w_in", "conv_w", "conv_b",
        "attn_sinks", "m_igate_b", "m_fgate_b", "m_head_g", "w_attn_up", "w_mlstm_up", "w_out", "mix_post_g",
        "ffn2_pre_g", "ffn2_wg", "ffn2_wu", "ffn2_wd", "ffn2_post_g"]


def kernel(**inputs):
    import concourse.bacc as bacc
    from concourse.bass_utils import run_bass_kernel_spmd

    nc = bacc.Bacc("TRN2", target_bir_lowering=False, num_devices=1)
    arrays, args = {}, []
    for name in _INS:
        a = np.ascontiguousarray(inputs[name])
        arrays[f"in_{name}"] = a
        args.append(nc.dram_tensor(f"in_{name}", a.shape, mybir.dt.from_np(a.dtype), kind="ExternalInput").ap())
    shape = np.shape(inputs["x"])
    args.append(nc.dram_tensor("out_y", shape, F32, kind="ExternalOutput").ap())
    hybrid_layer(nc, *args)
    r = run_bass_kernel_spmd(nc, [arrays], core_ids=[0])
    return r.results[0]["out_y"]
```

```python
from contextlib import ExitStack

import numpy as np

import concourse.bass as bass
from concourse import mybir

F32 = mybir.dt.float32
F32R = mybir.dt.float32r
ALU = mybir.AluOpType
ACT = mybir.ActivationFunctionType
AX = mybir.AxisListType

P = 128
EPS = 1e-6
MASKED = -1e30


def hybrid_layer(nc: bass.Bass, x, ffn1_pre_g, ffn1_wg, ffn1_wu, ffn1_wd, ffn1_post_g, mix_pre_g,
                 w_in, conv_w, conv_b, attn_sinks, m_igate_b, m_fgate_b, m_head_g, w_attn_up,
                 w_mlstm_up, w_out, mix_post_g, ffn2_pre_g, ffn2_wg, ffn2_wu, ffn2_wd, ffn2_post_g,
                 out):
    _, SEQ, D = x.shape
    F = ffn1_wg.shape[2]
    NT = SEQ // P
    ND = D // P
    NF = F // P
    COLS = 512
    NCB = D // COLS
    HEADS = attn_sinks.shape[1]
    KVH = 4
    GROUP = HEADS // KVH
    HD = 64
    MH = m_igate_b.shape[1]
    CONV = conv_w.shape[1]
    MQK = conv_w.shape[2] // 2
    QKD = MQK // MH
    MV = m_head_g.shape[1]
    VD = MV // MH
    ATT_Q, ATT_KV = HEADS * HD, KVH * HD
    assert NT == 2 and ND == 16 and NCB == 4 and QKD == P and VD == 2 * P and ATT_Q == MV == 1024

    HALF = 1024
    RAW = 4
    SPL = 4
    KC = 4
    BLOCK_CHUNKS = ND // KC
    NFB = F // COLS
    UP_CHUNKS = NFB * 2 * BLOCK_CHUNKS
    UPK = ATT_Q // P
    UP_BLOCK_CHUNKS = UPK // KC
    OFF_K = ATT_Q
    OFF_MQ = ATT_Q + 2 * ATT_KV
    OFF_MK = OFF_MQ + MQK
    OFF_MV = OFF_MK + MQK
    OFF_MO = OFF_MV + MV
    OFF_GATES = OFF_MO + MV
    OFF_GA = OFF_GATES + 2 * MH
    OFF_GM = OFF_GA + D
    IN_BLOCKS = ([("k", 0, OFF_K)] + [("q", j, j * COLS) for j in range(2)]
                 + [("mqk", 0, OFF_MQ), ("mqk", 1, OFF_MK)]
                 + [("mv", j, OFF_MV + j * COLS) for j in range(2)]
                 + [("mo", j, OFF_MO + j * COLS) for j in range(2)]
                 + [("ga", j, OFF_GA + j * COLS) for j in range(4)]
                 + [("gm", j, OFF_GM + j * COLS) for j in range(4)])
    NIN = len(IN_BLOCKS)
    A_SLOT = NIN * 8
    M_SLOT = A_SLOT + NCB * 2 * UP_BLOCK_CHUNKS
    END_SLOT = M_SLOT + NCB * 2 * UP_BLOCK_CHUNKS
    C_UP = [0, 0]
    C_DOWN = [C_UP[0] + UP_CHUNKS, 0]
    C_MIX = C_DOWN[0] + NF
    C_OUT = C_MIX + END_SLOT // 2
    C_UP[1] = C_OUT + ND
    C_DOWN[1] = C_UP[1] + UP_CHUNKS
    H_MIX = 2 * C_MIX
    CBO = (3, 2, 0, 1)
    assert NCB == BLOCK_CHUNKS == 4

    def k_tile(q):
        return KC * CBO[q // 2] + 2 * (q % 2)

    QUAD = [(q, half) for q in range(RAW) for half in range(2)]
    LAST_QUAD = [(q, half) for half in range(2) for q in range(RAW)]
    Y_END = [2 * (C_DOWN[0] + NF), 2 * (C_OUT + ND), 2 * (C_DOWN[1] + NF)]
    assert all(c % RAW == 0 for c in C_UP + C_DOWN + [C_MIX, C_OUT])
    T_DOWN = [0, NF + ND]
    T_OUT = NF

    def ends(b):
        return 8 * b + 7 if b < NIN else A_SLOT + 4 * (b - NIN) + 3

    def evac_slot(b):
        return ends(b) + 3

    EVAC_AT = {evac_slot(b): b for b in range(NIN + 2 * NCB)}
    kinds = [k for k, _, _ in IN_BLOCKS] + ["A"] * NCB + ["M"] * NCB

    def act_evacs(b):
        return sum(k not in ("A", "M") for k in kinds[:b + 1])

    def dve_evacs(b):
        return sum(k not in ("mo", "ga", "gm") for k in kinds[:b + 1])

    TURN_B = {8 * b + 9: b for b in (0, 1, 2, 3, 4)}
    TURN_COPY = {8 * b + 13: b for b in (0, 1, 2, 3, 4)}
    CONV_AT = {38 + 8 * q + c: (q, c) for q in range(2) for c in range(4)}
    SILU_AT = {43 + 8 * q: q for q in range(2)}
    G0 = 22
    NG = 2 * KVH
    SPLIT_SLOT = A_SLOT - SPL
    Y_BANK = (0, 2, 0, 6)

    def group_at(s, offset):
        g, rest = divmod(s - G0 - offset, 8)
        return g if rest == 0 and 0 <= g < NG else None

    ctx = ExitStack()
    with ctx:
        def sb(name, shape, dt=F32, where=ctx):
            return where.enter_context(nc.sbuf_tensor(name, shape, dt))

        def sem(name):
            return ctx.enter_context(nc.semaphore(name))

        raw = sb("raw", [P, RAW, 2 * HALF])
        w_hi = sb("w_hi", [P, SPL, HALF], F32R)
        w_lo = sb("w_lo", [P, SPL, HALF], F32R)
        x_hi = sb("x_hi", [P, ND, SEQ], F32R)
        x_lo = sb("x_lo", [P, ND, SEQ], F32R)
        h = sb("h", [P, NT, D])
        gain = sb("gain", [P, D])
        att = gain[:, :].rearrange("p (c t) -> p c t", t=SEQ)
        rows = sb("rows", [P, P])
        cols = sb("cols", [P, P])
        ident = sb("ident", [P, P])
        dist = sb("dist", [P, 2 * P])
        future = sb("future", [P, P])
        sel = sb("sel", [MH, MH, P])
        ones = sb("ones", [P, SEQ])
        neg_half = sb("neg_half", [P, 4])
        sinks = sb("sinks", [P, HEADS])
        head_g = sb("head_g", [P, MV])
        gate_b = sb("gate_b", [MH, 2])
        wg_raw = sb("wg_raw", [P, ND, 2 * MH])
        wg_hi = sb("wg_hi", [P, ND, 2 * MH], F32R)
        wg_lo = sb("wg_lo", [P, ND, 2 * MH], F32R)
        stat = sb("stat", [P, 64])
        sq_y = stat[:, 0:8].rearrange("p (t c) -> p t c", t=NT)
        ms_y = stat[:, 8:10]
        rs_y = stat[:, 10:12]
        rs_yh = stat[:, 12:14]
        sq_h = stat[:, 14:16]
        ms_h = stat[:, 16:18]
        rs_h = stat[:, 18:20]
        rs_q = stat[:, 20:22]
        m_stat = sb("m_stat", [P, 64])
        r_col = m_stat[:, 0:8].rearrange("p (t h) -> p t h", t=NT)
        e_col = m_stat[:, 8:16].rearrange("p (t h) -> p t h", t=NT)
        den = m_stat[:, 16:24].rearrange("p (t h) -> p t h", t=NT)
        rden = m_stat[:, 24:32].rearrange("p (t h) -> p t h", t=NT)
        sq_m = m_stat[:, 32:40].rearrange("p (t h) -> p t h", t=NT)
        ms_m = m_stat[:, 40:48].rearrange("p (t h) -> p t h", t=NT)
        rs_m = m_stat[:, 48:56].rearrange("p (t h) -> p t h", t=NT)
        a_stat = sb("a_stat", [P, 2, 8, 4])
        gates_tok = sb("gates_tok", [P, NT, 2 * MH])
        G_PRE = [0, ND, 2 * ND]
        G_TAP = 3 * ND
        G_BIAS = G_TAP + CONV * 2 * MQK // P
        NROWS = G_BIAS + 2 * MQK // P

        with ExitStack() as part:
            hid = sb("hid", [P, NF, SEQ], F32, part)
            silu = sb("silu", [P, NT, COLS], F32, part)
            prod = sb("prod", [P, NT, COLS], F32, part)
        with ExitStack() as part:
            attn_in = sb("attn_in", [P, 3584], F32, part)
            m_in = sb("m_in", [P, 2 * MH * SEQ + NT * MH * (VD + 1)], F32, part)
            smo = sb("smo", [P, NT, MV], F32, part)
            y = sb("y", [P, NT, D], F32, part)
            gm = sb("gm", [P, NCB, NT * COLS], F32, part)
            rows4 = sb("rows4", [MH, 4, SEQ], F32, part)
        conv_out = m_in[:, 0:2 * MH * SEQ].rearrange("p (c t) -> p c t", t=SEQ)
        mval = m_in[:, 2 * MH * SEQ:].rearrange("p (t h d) -> p t h d", t=NT, h=MH)
        y_T = m_in[:, 0:ND * SEQ].rearrange("p (c t) -> p c t", t=SEQ)
        att_qT = attn_in[:, 0:2048].rearrange("p (c t) -> p c t", t=SEQ)
        att_kT = attn_in[:, 2048:3072].rearrange("p (c t) -> p c t", t=SEQ)
        att_v = attn_in[:, 3072:3584].rearrange("p (t d) -> p t d", t=NT)
        WTN = 3 * P
        wt = attn_in[:, 0:MH * WTN].rearrange("p (h n) -> p h n", h=MH)
        pt_m = attn_in[:, MH * WTN:2 * MH * WTN].rearrange("p (h n) -> p h n", h=MH)
        y_flat = y[:, :, :].rearrange("p t d -> p (t d)")
        CP = SEQ + CONV - 1
        conv_in = y_flat[:, 0:8 * CP].rearrange("p (c n) -> p c n", n=CP)
        stage = y_flat[:, 8 * CP:8 * CP + NT * COLS].rearrange("p (t n) -> p t n", t=NT)
        probs = gm[:, 0:2, :]
        probs_T = gm[:, 2:4, :]
        m_h = gm[:, 2:4, :]
        m_T = conv_out

        ps = ctx.enter_context(nc.psum_tensor("ps", [P, 8, COLS], F32))

        x_in = [sem(f"x_in{i}") for i in range(NCB)]
        rows_in = sem("rows_in")
        misc_in = sem("misc_in")
        wg_in = sem("wg_in")
        gain_in = sem("gain_in")
        raw_full = [sem(f"raw_full{i}") for i in range(RAW)]
        hi_ready = sem("hi_ready")
        lo_ready = sem("lo_ready")
        w_used = sem("w_used")
        const_step = sem("const_step")
        const_ready = sem("const_ready")
        rows_turned = sem("rows_turned")
        cols_ready = sem("cols_ready")
        h_turned = sem("h_turned")
        x_hi_ready = sem("x_hi_ready")
        x_lo_ready = sem("x_lo_ready")
        xs_hi_ready = sem("xs_hi_ready")
        xs_lo_ready = sem("xs_lo_ready")
        y_bank = sem("y_bank")
        y_scaled = sem("y_scaled")
        h_squared = sem("h_squared")
        h_ms = sem("h_ms")
        h_rstd = sem("h_rstd")
        y_squared = sem("y_squared")
        y_ms = sem("y_ms")
        y_rstd = sem("y_rstd")
        h_ready = sem("h_ready")
        silu_ready = sem("silu_ready")
        prod_ready = sem("prod_ready")
        prod_turned = sem("prod_turned")
        hid_a = sem("hid_a")
        hid_v = sem("hid_v")
        act_step = sem("act_step")
        dve_step = sem("dve_step")
        wg_hi_ready = sem("wg_hi_ready")
        wg_lo_ready = sem("wg_lo_ready")
        gates_done = sem("gates_done")
        gates_ready = sem("gates_ready")
        gates_turned = sem("gates_turned")
        gate_rows = sem("gate_rows")
        log_ready = sem("log_ready")
        rows_ready = sem("rows_ready")
        r_turned = sem("r_turned")
        r_cols = sem("r_cols")
        e_cols = sem("e_cols")
        ev_a = sem("ev_a")
        ev_v = sem("ev_v")
        stage_turned = sem("stage_turned")
        turn_a = sem("turn_a")
        turn_v = sem("turn_v")
        conv_ready = sem("conv_ready")
        conv_silu = sem("conv_silu")
        scored = sem("scored")
        maxed = sem("maxed")
        exped = sem("exped")
        normed = sem("normed")
        p_turned = sem("p_turned")
        pt_a = sem("pt_a")
        pt_v = sem("pt_v")
        pv_done = sem("pv_done")
        pv_out = sem("pv_out")
        neg_r = sem("neg_r")
        wt_arg = sem("wt_arg")
        wt_ready = sem("wt_ready")
        m_scored = sem("m_scored")
        pt_m_ready = sem("pt_m_ready")
        num_done = sem("num_done")
        rden_ready = sem("rden_ready")
        mh_a = sem("mh_a")
        mh_v = sem("mh_v")
        m_squared = sem("m_squared")
        m_ms = sem("m_ms")
        m_rstd = sem("m_rstd")
        m_rows = sem("m_rows")
        m_turned = sem("m_turned")
        mt_a = sem("mt_a")
        mt_v = sem("mt_v")
        att_split = sem("att_split")
        att_split_lo = sem("att_split_lo")
        ones_v = sem("ones_v")
        q_scale = sem("q_scale")
        y_ready = sem("y_ready")
        y_turned = sem("y_turned")
        yt_a = sem("yt_a")
        yt_v = sem("yt_v")
        stored = sem("stored")

        WG = [ffn1_wg[0], ffn2_wg[0]]
        WU = [ffn1_wu[0], ffn2_wu[0]]
        WD = [ffn1_wd[0], ffn2_wd[0]]

        def src_tile(phase, n):
            return hid[:, n, :] if phase != "out" else y_T[:, n, :]

        block = ctx.enter_context(nc.Block())

        @block.sync
        def _(sp):
            def load_x(cb):
                c = slice(cb * COLS, (cb + 1) * COLS)
                sp.dma_start(h[:, :, c], x[0].rearrange("(t p) d -> p t d", p=P)[:, :, c]).then_inc(x_in[cb], 16)

            def load(c, slot, src, shape, first=False, after_rows=False):
                if after_rows:
                    sp.wait_ge(lo_ready, 2 * (c - slot) - RAW + 1 + slot)
                elif not first:
                    sp.wait_ge(lo_ready, 2 * c - 2 * RAW + 2)
                dst = raw[:, slot, :]
                if shape:
                    dst = dst.rearrange("p (k n) -> p k n", k=KC)
                sp.dma_start(dst, src).then_inc(raw_full[slot], 16)

            def by_columns(w, k0, col):
                return w.rearrange("(k p) n -> p k n", p=P)[:, k0:k0 + KC, bass.ds(col, COLS)]

            def up_block(e, i, col, first=False):
                for n, w in enumerate((WG[e], WU[e])):
                    for q in range(BLOCK_CHUNKS):
                        j = n * BLOCK_CHUNKS + q
                        if first and e == 0 and j < NCB:
                            load_x(CBO[j])
                        load(C_UP[e] + i * 2 * BLOCK_CHUNKS + j, j % RAW, by_columns(w, KC * CBO[q], col), True,
                             first and j < RAW and e == 0, first and j < RAW and e == 1)

            def by_rows(w, base, n):
                with sp.Fori(0, n // RAW) as i:
                    for q in range(RAW):
                        load(base + i * RAW + q, q, w[bass.ds(i * (RAW * P) + q * P, P), :], False)

            for e in range(2):
                up_block(e, 0, 0, first=True)
                with sp.Fori(0, NFB - 1) as i:
                    up_block(e, i + 1, i * COLS + COLS)
                by_rows(WD[e], C_DOWN[e], NF)
                if e == 0:
                    c = C_MIX
                    for _, _, col in IN_BLOCKS:
                        for q in range(BLOCK_CHUNKS):
                            load(c, c % RAW, by_columns(w_in[0], KC * CBO[q], col), True, after_rows=c < C_MIX + RAW)
                            c += 1
                    for w in (w_attn_up[0], w_mlstm_up[0]):
                        with sp.Fori(0, NCB // 2) as i:
                            for b in range(2):
                                for q in range(UP_BLOCK_CHUNKS):
                                    j = b * UP_BLOCK_CHUNKS + q
                                    load(c + i * 2 * UP_BLOCK_CHUNKS + j, j % RAW,
                                         by_columns(w, KC * q, i * (2 * COLS) + b * COLS), True)
                        c += NCB * UP_BLOCK_CHUNKS
                    by_rows(w_out[0], C_OUT, ND)
            for i, cb in enumerate(CBO):
                sp.wait_ge(h_ready, 2 * NCB + i + 1)
                sp.dma_start(out[0].rearrange("(t p) d -> p t d", p=P)[:, :, cb * COLS:(cb + 1) * COLS],
                             h[:, :, cb * COLS:(cb + 1) * COLS]).then_inc(stored, 16)
            sp.wait_ge(stored, 16 * NCB)

        @block.gpsimd
        def _(pool):
            steps = [0]

            def step(ins):
                steps[0] += 1
                ins.then_inc(const_step, 1)
                pool.wait_ge(const_step, steps[0])

            step(pool.memset(ident[:, :], 0.0))
            step(pool.affine_select(out=ident[:, :], in_=ident[:, :], compare_op=ALU.not_equal, fill=1.0, base=0,
                                    pattern=[[-1, P]], channel_multiplier=1))
            pool.memset(neg_half[:, :], -0.5).then_inc(const_ready, 1)
            pool.memset(ones[:, :], 1.0).then_inc(const_ready, 1)
            pool.dma_start(gain[:, :], ffn1_post_g.to_broadcast([P, D])).then_inc(gain_in, 16)
            with nc.allow_non_contiguous_dma(reason="a few gate columns and biases"):
                pool.dma_start(wg_raw[:, :, :], w_in[0].rearrange("(k p) n -> p k n", p=P)[:, :, OFF_GATES:OFF_GA]).then_inc(wg_in, 16)
                pool.dma_start(gate_b[:, 0:1], m_igate_b.rearrange("a h -> h a")).then_inc(misc_in, 16)
                pool.dma_start(gate_b[:, 1:2], m_fgate_b.rearrange("a h -> h a")).then_inc(misc_in, 16)
            pool.dma_start(sinks[:, :], attn_sinks.to_broadcast([P, HEADS])).then_inc(misc_in, 16)
            pool.dma_start(head_g[:, :], m_head_g.to_broadcast([P, MV])).then_inc(misc_in, 16)
            step(pool.iota(dist[:, :], pattern=[[-1, 2 * P]], base=P, channel_multiplier=1,
                           allow_small_or_imprecise_dtypes=True))
            step(pool.affine_select(out=dist[:, :], in_=dist[:, :], compare_op=ALU.is_ge, fill=-MASKED, base=P,
                                    pattern=[[-1, 2 * P]], channel_multiplier=1))
            step(pool.affine_select(out=dist[:, :], in_=dist[:, :], compare_op=ALU.is_gt, fill=-MASKED, base=0,
                                    pattern=[[1, 2 * P]], channel_multiplier=-1))
            step(pool.memset(future[:, :], 0.0))
            step(pool.affine_select(out=future[:, :], in_=future[:, :], compare_op=ALU.is_ge, fill=MASKED, base=0,
                                    pattern=[[1, P]], channel_multiplier=-1))
            step(pool.memset(sel[:, :, :], 0.0))
            pool.affine_select(out=sel[:, :, :], in_=sel[:, :, :], compare_op=ALU.not_equal, fill=-1.0, base=0,
                               pattern=[[-1, MH], [0, P]], channel_multiplier=1).then_inc(const_ready, 1)

            def inverse_root(ms, dst, wait, count, done):
                pool.wait_ge(wait, count)
                pool.tensor_tensor(dst, ms, neg_half[:, 0:ms.shape[1]], ALU.pow).then_inc(done, 1)

            def post(p):
                inverse_root(ms_y, rs_y, y_ms, p + 1, y_rstd)
                for i, cb in enumerate(CBO):
                    c = slice(cb * COLS, (cb + 1) * COLS)
                    pool.wait_ge(y_scaled, NCB * p + i + 1)
                    for t in range(NT):
                        ins = pool.tensor_tensor(h[:, t, c], h[:, t, c], (prod, silu)[i % 2][:, t, :], ALU.add)
                    ins.then_inc(h_ready, 1)

            pool.wait_ge(const_ready, 3)
            inverse_root(ms_h, rs_h, h_ms, 1, h_rstd)
            post(0)
            pool.wait_ge(h_ready, NCB)
            pool.memset(mval[:, :, :, VD:VD + 1], 1.0).then_inc(ones_v, 1)
            pool.memset(conv_in[:, :, 0:CONV - 1], 0.0).then_inc(ones_v, 1)
            inverse_root(ms_h, rs_h, h_ms, 2, h_rstd)
            for b in range(NT):
                inverse_root(ms_m[:, b, :], rs_m[:, b, :], m_ms, b + 1, m_rstd)
            pool.wait_ge(att_split_lo, 4)
            pool.dma_start(gain[:, :], mix_post_g.to_broadcast([P, D])).then_inc(gain_in, 16)
            post(1)
            inverse_root(ms_h, rs_h, h_ms, 3, h_rstd)
            pool.wait_ge(h_ready, 2 * NCB)
            pool.dma_start(gain[:, :], ffn2_post_g.to_broadcast([P, D])).then_inc(gain_in, 16)
            post(2)

        @block.scalar
        def _(act):
            steps = [0]

            def step(ins):
                steps[0] += 1
                ins.then_inc(act_step, 1)
                act.wait_ge(act_step, steps[0])

            def split_hi(H, half, slot, hw, raw_wait, first=False):
                if half == 0:
                    act.wait_ge(raw_full[slot], raw_wait)
                if not first:
                    act.wait_ge(w_used, H - SPL + 1)
                act.activation(w_hi[:, hw, :], raw[:, slot, half * HALF:(half + 1) * HALF], ACT.Copy).then_inc(hi_ready, 1)

            def split_static(H, first=False):
                c = H // 2
                split_hi(H, H % 2, c % RAW, H % SPL, 16 * (c // RAW + 1), first)

            dropped = hid[:, 0:NT * D // SEQ, :].rearrange("p a b -> p (a b)")

            def turn_in(e, u):
                act.wait_ge(h_turned, e * ND // 2 + u + 1)
                for kk in range(2):
                    k = k_tile(u) + kk
                    ins = act.activation(x_hi[:, k, :], ps[:, 6 + u % 2, kk * SEQ:(kk + 1) * SEQ], ACT.Identity,
                                         scale=cols[:, G_PRE[e] + k:G_PRE[e] + k + 1])
                ins.then_inc(x_hi_ready, 1)

            def square_h(e, t):
                if e == 0 and t == 0:
                    for cb in range(NCB):
                        act.wait_ge(x_in[cb], 16)
                if e and t == 0:
                    act.wait_ge(h_ready, e * NCB)
                act.activation(dropped[:, t * D:(t + 1) * D], h[:, t, :], ACT.Square,
                               accum_out=sq_h[:, t:t + 1]).then_inc(h_squared, 1)

            def begin(e, H0, split):
                split(0)
                split(1)
                for u in range(ND // 2):
                    turn_in(e, u)
                    split(u + 2)
                    if u >= ND // 2 - NT:
                        square_h(e, u - (ND // 2 - NT))

            def silu_gate(e, i, base, started):
                act.wait_ge(w_used, 2 * C_UP[e] + i * 4 * BLOCK_CHUNKS + 2 * BLOCK_CHUNKS)
                if started:
                    act.wait_ge(prod_ready, e * NFB + i)
                for t in range(NT):
                    ins = act.activation(silu[:, t, :], ps[:, base + t, :], ACT.Silu, scale=rs_h[:, t:t + 1])
                ins.then_inc(silu_ready, 1)

            def copy_hidden(e, i, base):
                act.wait_ge(prod_turned, e * NFB + i + 1)
                act.activation(hid[:, bass.ds(i * 4, 2), :], ps[:, base, :].rearrange("p (a b) -> p a b", a=2),
                               ACT.Copy).then_inc(hid_a, 1)

            def up_block(e, i, even, first, very_first=False):
                base = 4 if even else 0

                def split(j):
                    H = 2 * C_UP[e] + i * 4 * BLOCK_CHUNKS + j
                    split_hi(H, j % 2, (j // 2) % RAW, j % SPL, (i * 2 + C_UP[e] // RAW + j // 2 // RAW + 1) * 16,
                             very_first and j < SPL)

                if first:
                    begin(e and 2, 2 * C_UP[e], split)
                for j in range(ND // 2 + 2 if first else 0, 4 * BLOCK_CHUNKS):
                    split(j)
                    if j == 7 and not first:
                        copy_hidden(e, i - 1, 4 - base)
                    if j == 10:
                        if first:
                            act.wait_ge(h_rstd, e * 2 + 1)
                        silu_gate(e, i, base, not first)

            def x_split(T, n, slot, phase):
                act.activation(x_hi[:, slot, :], src_tile(phase, n), ACT.Copy).then_inc(xs_hi_ready, 1)

            def rows_quad(base_c, T0, i, phase, e=None, tail=None, last=False):
                for j, (q, half) in enumerate(LAST_QUAD if last else QUAD):
                    split_hi(2 * base_c + i * 2 * RAW + j, half, q, j % SPL, (i + base_c // RAW + 1) * 16)
                    if half == 0:
                        if q == 0 and phase == "down":
                            act.wait_ge(hid_a, e * NFB + i + 1)
                            act.wait_ge(hid_v, e * NFB + i + 1)
                        elif q == 0:
                            act.wait_ge(yt_a, i + 1)
                            act.wait_ge(yt_v, i + 1)
                        x_split(T0 + i * RAW + q, i * RAW + q, q, phase)
                    if tail and j == 3:
                        tail()

            def squares_of_y(p):
                for bank in range(NCB * NT):
                    if bank == 0:
                        act.wait_ge(w_used, Y_END[p] - RAW)
                    elif bank == NCB * NT - 1:
                        act.wait_ge(w_used, Y_END[p])
                    elif bank >= NCB:
                        act.wait_ge(y_bank, 3 * p + bank - NCB + 1)
                    ins = act.activation(dropped[:, bank * COLS:(bank + 1) * COLS], ps[:, bank, :], ACT.Square,
                                         accum_out=sq_y[:, bank % NT, bank // NT:bank // NT + 1])
                ins.then_inc(y_squared, 1)

            def swiglu(e):
                up_block(e, 0, True, True, very_first=(e == 0))
                with act.Fori(0, NFB // 2) as it:
                    up_block(e, it * 2 + 1, False, False)
                    up_block(e, it * 2 + 2, True, False)
                if e == 0:
                    act.wait_ge(wg_in, 16)
                    act.activation(wg_hi[:, :, :], wg_raw[:, :, :], ACT.Copy).then_inc(wg_hi_ready, 1)
                rows_quad(C_DOWN[e], T_DOWN[e], 0, "down", e,
                          tail=lambda: copy_hidden(e, NFB - 1, 4))
                with act.Fori(1, NF // RAW - 1) as i:
                    rows_quad(C_DOWN[e], T_DOWN[e], i, "down", e)
                rows_quad(C_DOWN[e], T_DOWN[e], NF // RAW - 1, "down", e, last=True)
                squares_of_y(2 * e)

            n_rows = 0
            for v in (ffn1_pre_g[0], mix_pre_g[0], ffn2_pre_g[0]):
                act.dma_start(rows[n_rows:n_rows + ND, :], v.rearrange("(k p) -> k p", p=P)).then_inc(rows_in, 16)
                n_rows += ND
            act.dma_start(rows[G_TAP:G_BIAS, :], conv_w[0].rearrange("j (k p) -> (j k) p", p=P)).then_inc(rows_in, 16)
            act.dma_start(rows[G_BIAS:NROWS, :], conv_b[0].rearrange("(k p) -> k p", p=P)).then_inc(rows_in, 16)
            act.wait_ge(rows_turned, 1)
            act.activation(cols[:, 0:NROWS], ps[:, 5, 0:NROWS], ACT.Copy).then_inc(cols_ready, 1)
            act.wait_ge(cols_ready, 1)
            swiglu(0)

            def evacuate(b):
                kind, j = kinds[b], IN_BLOCKS[b][1] if b < NIN else 0
                bank = 4 + 2 * (b % 2)
                if kind in ("A", "M"):
                    return
                act.wait_ge(w_used, H_MIX + ends(b) + 1)
                if kind == "k":
                    act.wait_ge(ones_v, 2)
                    act.activation(stage[:, 0, :].rearrange("p (h r d) -> p h r d", h=KVH, r=2),
                                   ps[:, bank, 0:ATT_KV].rearrange("p (h r d) -> p h r d", h=KVH, r=1).to_broadcast([P, KVH, 2, HD]),
                                   ACT.Identity, scale=rs_h[:, 0:1])
                    act.activation(att_v[:, 0, :], ps[:, bank, ATT_KV:2 * ATT_KV], ACT.Identity,
                                   scale=rs_h[:, 0:1]).then_inc(ev_a, 1)
                elif kind in ("q", "mqk"):
                    act.wait_ge(stage_turned, b)
                    if kind == "q":
                        act.wait_ge(q_scale, 1)
                    act.activation(stage[:, 0, :], ps[:, bank, :], ACT.Identity,
                                   scale=(rs_q if kind == "q" else rs_h)[:, 0:1]).then_inc(ev_a, 1)
                elif kind == "mv":
                    act.activation(mval[:, 0, 2 * j:2 * j + 2, 0:VD], ps[:, bank, :].rearrange("p (h d) -> p h d", h=2),
                                   ACT.Identity, scale=rs_h[:, 0:1]).then_inc(ev_a, 1)
                else:
                    for t in range(NT):
                        if kind == "mo":
                            dst = smo[:, t, j * COLS:(j + 1) * COLS]
                        elif kind == "ga":
                            dst = y[:, t, j * COLS:(j + 1) * COLS]
                        else:
                            dst = gm[:, j, t * COLS:(t + 1) * COLS]
                        ins = act.activation(dst, ps[:, bank + t, :], ACT.Sigmoid, scale=rs_h[:, t:t + 1])
                    ins.then_inc(ev_a, 1)

            def copy_y(j):
                act.wait_ge(y_turned, j + 1)
                act.activation(y_T[:, 4 * j:4 * j + 2, :], ps[:, Y_BANK[j], :].rearrange("p (a n) -> p a n", a=2),
                               ACT.Copy).then_inc(yt_a, 1)

            def turned_tile(b, a):
                if b == 0:
                    return att_kT[:, 2 * a:2 * a + 2, :]
                if b < 3:
                    return att_qT[:, 4 * (b - 1) + 2 * a:4 * (b - 1) + 2 * a + 2, :]
                return conv_in[:, 4 * (b - 3) + 2 * a:4 * (b - 3) + 2 * a + 2, CONV - 1:CP]

            def split(s):
                split_static(H_MIX + s)

            begin(1, H_MIX, split)
            act.wait_ge(h_rstd, 2)
            for s in range(END_SLOT):
                if s >= ND // 2 + 2:
                    split(s)
                if s == 16:
                    act.wait_ge(gate_rows, 1)
                    act.wait_ge(const_ready, 3)
                    step(act.activation(rows4[:, 2, :], rows4[:, 1, :], ACT.Abs))
                    step(act.activation(rows4[:, 2, :], rows4[:, 2, :], ACT.Exp, scale=-1.0))
                    act.activation(rows4[:, 2, :], rows4[:, 2, :], ACT.Ln, bias=ones[0:MH, 0:1]).then_inc(log_ready, 1)
                if s == 24:
                    act.wait_ge(r_turned, 1)
                    act.activation(e_col, ps[:, 3, 0:16].rearrange("p (t k h) -> p t k h", t=NT, k=2)[:, :, 1, :],
                                   ACT.Exp, scale=-1.0).then_inc(e_cols, 1)
                if s in EVAC_AT:
                    evacuate(EVAC_AT[s])
                if s in TURN_COPY:
                    b = TURN_COPY[s]
                    act.wait_ge(stage_turned, b + 1)
                    act.activation(turned_tile(b, 0), ps[:, 0, :].rearrange("p (a n) -> p a n", a=2),
                                   ACT.Copy).then_inc(turn_a, 1)
                if s in SILU_AT:
                    q = SILU_AT[s]
                    act.wait_ge(conv_ready, 4 * q + 4)
                    for c in range(4 * q, 4 * q + 4):
                        ins = act.activation(conv_out[:, c, :], conv_out[:, c, :], ACT.Silu,
                                             bias=cols[:, G_BIAS + c:G_BIAS + c + 1])
                    ins.then_inc(conv_silu, 1)
                g = group_at(s, 4)
                if g is not None:
                    K = P * (g % 2 + 1)
                    st = a_stat[:, g % 2]
                    act.wait_ge(maxed, g + 1)
                    for hh in range(GROUP):
                        act.activation(probs[:, g % 2, hh * K:(hh + 1) * K], probs[:, g % 2, hh * K:(hh + 1) * K],
                                       ACT.Exp, bias=st[:, 2, hh:hh + 1], accum_out=st[:, 4, hh:hh + 1])
                    act.activation(st[:, 5, :], st[:, 3, :], ACT.Exp).then_inc(exped, 1)
                g = group_at(s, 7)
                if g is not None:
                    act.wait_ge(p_turned, g + 1)
                    act.activation(probs_T[:, g % 2, 0:COLS], ps[:, 2, :], ACT.Copy).then_inc(pt_a, 1)
                g = group_at(s, 9)
                if g is not None:
                    j, b = divmod(g, 2)
                    act.wait_ge(pv_done, g + 1)
                    act.activation(att[:, 2 * j:2 * j + 2, b * P:(b + 1) * P],
                                   ps[:, 2, 0:2 * P].rearrange("p (a n) -> p a n", a=2), ACT.Copy).then_inc(pv_out, 1)
                if s == 88:
                    act.wait_ge(wt_arg, 1)
                    act.wait_ge(r_cols, 1)
                    for hd in range(MH):
                        act.activation(wt[:, hd, 0:SEQ], wt[:, hd, 0:SEQ], ACT.Exp, bias=r_col[:, 0, hd:hd + 1])
                        ins = act.activation(wt[:, hd, SEQ:WTN], wt[:, hd, SEQ:WTN], ACT.Exp, bias=r_col[:, 1, hd:hd + 1])
                    ins.then_inc(wt_ready, 1)
                for b in range(NT):
                    if s == 97 + 6 * b:
                        act.wait_ge(rden_ready, b + 1)
                        for hd in range(2):
                            ins = act.activation(m_h[:, b, hd * VD:(hd + 1) * VD], ps[:, hd, 0:VD], ACT.Identity,
                                                 scale=rden[:, b, hd:hd + 1])
                        ins.then_inc(mh_a, 1)
                        act.wait_ge(mh_v, b + 1)
                        act.wait_ge(mh_a, b + 1)
                        for hd in range(MH):
                            ins = act.activation(gm[:, b, hd * VD:(hd + 1) * VD], m_h[:, b, hd * VD:(hd + 1) * VD], ACT.Square,
                                                 accum_out=sq_m[:, b, hd:hd + 1])
                        ins.then_inc(m_squared, 1)
                if s == 115:
                    act.wait_ge(m_turned, 1)
                    act.activation(m_T[:, 0:4, :], ps[:, 0:2, :].rearrange("p a (c n) -> p (a c) n", c=2),
                                   ACT.Copy).then_inc(mt_a, 1)
                if SPLIT_SLOT <= s < SPLIT_SLOT + 8:
                    q = s - SPLIT_SLOT
                    if q == 4:
                        act.wait_ge(mt_a, 1)
                        act.wait_ge(mt_v, 1)
                    src = att if q < 4 else m_T
                    k = k_tile(q)
                    act.activation(x_hi[:, k:k + 2, :], src[:, 2 * (q % 4):2 * (q % 4) + 2, :],
                                   ACT.Copy).then_inc(att_split, 1)
                for j in range(NCB - 2):
                    if s == evac_slot(NIN + NCB + j) + 3:
                        copy_y(j)
            copy_y(NCB - 2)
            rows_quad(C_OUT, T_OUT, 0, "out", tail=lambda: copy_y(NCB - 1))
            with act.Fori(1, ND // RAW - 1) as i:
                rows_quad(C_OUT, T_OUT, i, "out")
            rows_quad(C_OUT, T_OUT, ND // RAW - 1, "out", last=True)
            squares_of_y(1)
            swiglu(1)

        @block.vector
        def _(dve):
            steps = [0]

            def step(ins):
                steps[0] += 1
                ins.then_inc(dve_step, 1)
                dve.wait_ge(dve_step, steps[0])

            def split_lo(H, half, slot, hw):
                dve.wait_ge(hi_ready, H + 1)
                dve.tensor_tensor(w_lo[:, hw, :], raw[:, slot, half * HALF:(half + 1) * HALF],
                                  w_hi[:, hw, :].bitcast(F32), ALU.subtract).then_inc(lo_ready, 1)

            def turn_in_pair(e, u):
                dve.wait_ge(x_hi_ready, e * ND // 2 + u + 1)
                for kk in range(2):
                    k = k_tile(u) + kk
                    ins = dve.scalar_tensor_tensor(out=x_lo[:, k, :], in0=ps[:, 6 + u % 2, kk * SEQ:(kk + 1) * SEQ],
                                                   scalar=cols[:, G_PRE[e] + k:G_PRE[e] + k + 1],
                                                   in1=x_hi[:, k, :].bitcast(F32), op0=ALU.mult, op1=ALU.subtract)
                ins.then_inc(x_lo_ready, 1)

            def mean_square_h(e):
                dve.wait_ge(h_squared, 2 * e + 2)
                dve.tensor_scalar(ms_h, sq_h, 1.0 / D, EPS, ALU.mult, ALU.add).then_inc(h_ms, 1)

            def scale_y(p, i):
                cb = CBO[i]
                if i >= 2:
                    dve.wait_ge(h_ready, NCB * p + i - 1)
                for t in range(NT):
                    ins = dve.scalar_tensor_tensor(out=(prod, silu)[i % 2][:, t, :], in0=ps[:, 2 * cb + t, :],
                                                   scalar=rs_y[:, t:t + 1], in1=gain[:, cb * COLS:(cb + 1) * COLS],
                                                   op0=ALU.mult, op1=ALU.mult)
                ins.then_inc(y_scaled, 1)

            def norm_y(p, factor):
                dve.wait_ge(y_squared, p + 1)
                step(dve.tensor_reduce(ms_y, sq_y, AX.X, ALU.add))
                dve.tensor_scalar(ms_y, ms_y, 1.0 / (D * factor * factor), EPS / (factor * factor), ALU.mult,
                                  ALU.add).then_inc(y_ms, 1)
                dve.wait_ge(y_rstd, p + 1)
                dve.wait_ge(gain_in, 16 * (p + 1))

            def begin(e, split, factor):
                if e:
                    norm_y(e - 1, factor)
                    scale_y(e - 1, 0)
                    scale_y(e - 1, 1)
                for u in range(ND // 2):
                    if e and u in (2, 4):
                        scale_y(e - 1, 1 + u // 2)
                    turn_in_pair(e, u)
                    split(u)
                mean_square_h(e)

            def gated(e, i, base, first=False):
                dve.wait_ge(w_used, 2 * C_UP[e] + i * 4 * BLOCK_CHUNKS + 4 * BLOCK_CHUNKS)
                dve.wait_ge(silu_ready, e * NFB + i + 1)
                if not first:
                    dve.wait_ge(prod_turned, e * NFB + i)
                for t in range(NT):
                    ins = dve.scalar_tensor_tensor(out=prod[:, t, :], in0=ps[:, base + 2 + t, :],
                                                   scalar=rs_h[:, t:t + 1], in1=silu[:, t, :],
                                                   op0=ALU.mult, op1=ALU.mult)
                ins.then_inc(prod_ready, 1)

            def copy_hidden(e, i, base):
                dve.wait_ge(prod_turned, e * NFB + i + 1)
                dve.tensor_copy(hid[:, bass.ds(i * 4 + 2, 2), :],
                                ps[:, base + 1, :].rearrange("p (a b) -> p a b", a=2)).then_inc(hid_v, 1)

            def up_block(e, i, even, first):
                base = 4 if even else 0

                def split(j):
                    split_lo(2 * C_UP[e] + i * 4 * BLOCK_CHUNKS + j, j % 2, (j // 2) % RAW, j % SPL)

                if first:
                    begin(e and 2, split, 1.0)
                for j in range(ND // 2 if first else 0, 4 * BLOCK_CHUNKS):
                    split(j)
                    if j == 2 and not first:
                        gated(e, i - 1, 4 - base, first=isinstance(i, int) and i == 1)
                    if j == 7 and not first:
                        copy_hidden(e, i - 1, 4 - base)

            def rows_quad(base_c, T0, i, phase, e=None, tail=(), last=False):
                for j, (q, half) in enumerate(LAST_QUAD if last else QUAD):
                    split_lo(2 * base_c + i * 2 * RAW + j, half, q, j % SPL)
                    if half == 0:
                        dve.wait_ge(xs_hi_ready, T0 + i * RAW + q + 1)
                        dve.tensor_tensor(x_lo[:, q, :], src_tile(phase, i * RAW + q), x_hi[:, q, :].bitcast(F32),
                                          ALU.subtract).then_inc(xs_lo_ready, 1)
                    if tail and j in (2, 3):
                        tail[j - 2]()

            def swiglu(e):
                up_block(e, 0, True, True)
                up_block(e, 1, False, False)
                up_block(e, 2, True, False)
                with dve.Fori(1, NFB // 2) as it:
                    up_block(e, it * 2 + 1, False, False)
                    up_block(e, it * 2 + 2, True, False)
                if e == 0:
                    dve.wait_ge(wg_hi_ready, 1)
                    dve.tensor_tensor(wg_lo[:, :, :], wg_raw[:, :, :], wg_hi[:, :, :].bitcast(F32),
                                      ALU.subtract).then_inc(wg_lo_ready, 1)
                rows_quad(C_DOWN[e], T_DOWN[e], 0, "down", e,
                          tail=(lambda: gated(e, NFB - 1, 4), lambda: copy_hidden(e, NFB - 1, 4)))
                with dve.Fori(1, NF // RAW - 1) as i:
                    rows_quad(C_DOWN[e], T_DOWN[e], i, "down", e)
                rows_quad(C_DOWN[e], T_DOWN[e], NF // RAW - 1, "down", e, last=True)

            swiglu(0)

            def split(s):
                split_lo(H_MIX + s, s % 2, (s // 2) % RAW, s % SPL)

            begin(1, split, 0.5)
            dve.wait_ge(h_rstd, 2)
            dve.tensor_scalar(rs_q, rs_h, HD ** -0.5, None, ALU.mult).then_inc(q_scale, 1)
            dve.wait_ge(q_scale, 1)

            def evacuate(b):
                kind, j = kinds[b], IN_BLOCKS[b][1] if b < NIN else (b - NIN) % NCB
                bank = 4 + 2 * (b % 2)
                if kind in ("mo", "ga", "gm"):
                    return
                dve.wait_ge(w_used, H_MIX + ends(b) + 1)
                if kind == "k":
                    dve.wait_ge(ones_v, 2)
                    dve.tensor_scalar(stage[:, 1, :].rearrange("p (h r d) -> p h r d", h=KVH, r=2),
                                      ps[:, bank + 1, 0:ATT_KV].rearrange("p (h r d) -> p h r d", h=KVH, r=1).to_broadcast([P, KVH, 2, HD]),
                                      rs_h[:, 1:2], None, ALU.mult)
                    dve.tensor_scalar(att_v[:, 1, :], ps[:, bank + 1, ATT_KV:2 * ATT_KV], rs_h[:, 1:2], None,
                                      ALU.mult).then_inc(ev_v, 1)
                elif kind in ("q", "mqk"):
                    dve.wait_ge(stage_turned, b)
                    dve.tensor_scalar(stage[:, 1, :], ps[:, bank + 1, :], (rs_q if kind == "q" else rs_h)[:, 1:2],
                                      None, ALU.mult).then_inc(ev_v, 1)
                elif kind == "mv":
                    dve.tensor_scalar(mval[:, 1, 2 * j:2 * j + 2, 0:VD], ps[:, bank + 1, :].rearrange("p (h d) -> p h d", h=2),
                                      rs_h[:, 1:2], None, ALU.mult).then_inc(ev_v, 1)
                else:
                    c = slice(j * COLS, (j + 1) * COLS)
                    if kind == "A":
                        dve.wait_ge(ev_a, act_evacs(8 + 1 + j))
                        for t in range(NT):
                            ins = dve.tensor_tensor(y[:, t, c], ps[:, bank + t, :], y[:, t, c], ALU.mult)
                        ins.then_inc(ev_v, 1)
                    else:
                        dve.wait_ge(ev_a, act_evacs(8 + 1 + 4 + j))
                        for t in range(NT):
                            g_t = gm[:, j, t * COLS:(t + 1) * COLS]
                            ins = dve.tensor_tensor(g_t, ps[:, bank + t, :], g_t, ALU.mult)
                        ins.then_inc(ev_v, 1)
                        dve.wait_ge(ev_v, dve_evacs(b))
                        for t in range(NT):
                            ins = dve.tensor_tensor(y[:, t, c], y[:, t, c], gm[:, j, t * COLS:(t + 1) * COLS], ALU.add)
                        ins.then_inc(y_ready, 1)

            def copy_y(j):
                dve.wait_ge(y_turned, j + 1)
                dve.tensor_copy(y_T[:, 4 * j + 2:4 * j + 4, :],
                                ps[:, Y_BANK[j] + 1, :].rearrange("p (a n) -> p a n", a=2)).then_inc(yt_v, 1)

            def turned_tile(b, a):
                if b == 0:
                    return att_kT[:, 2 * a:2 * a + 2, :]
                if b < 3:
                    return att_qT[:, 4 * (b - 1) + 2 * a:4 * (b - 1) + 2 * a + 2, :]
                return conv_in[:, 4 * (b - 3) + 2 * a:4 * (b - 3) + 2 * a + 2, CONV - 1:CP]

            for s in range(END_SLOT):
                if s >= ND // 2:
                    split(s)
                if s == 10:
                    dve.wait_ge(gates_done, 1)
                    for t in range(NT):
                        ins = dve.tensor_scalar(gates_tok[:, t, :], ps[:, 2, t * 2 * MH:(t + 1) * 2 * MH],
                                                rs_h[:, t:t + 1], None, ALU.mult)
                    ins.then_inc(gates_ready, 1)
                if s == 15:
                    dve.wait_ge(gates_turned, 1)
                    dve.wait_ge(misc_in, 64)
                    for n in range(2):
                        ins = dve.tensor_scalar(rows4[:, n, :], ps[0:MH, 3, n * SEQ:(n + 1) * SEQ],
                                                gate_b[:, n:n + 1], None, ALU.add)
                    ins.then_inc(gate_rows, 1)
                if s == 19:
                    dve.wait_ge(log_ready, 1)
                    dve.wait_ge(const_ready, 3)
                    i_r, f_R, l_m, F_ = (rows4[:, n, :] for n in range(4))
                    step(dve.scalar_tensor_tensor(out=l_m, in0=f_R, scalar=0.0, in1=l_m, op0=ALU.min, op1=ALU.subtract))
                    step(dve.tensor_tensor_scan(F_, ones[0:MH, :], l_m, 0.0, ALU.mult, ALU.add))
                    step(dve.tensor_tensor(i_r, i_r, F_, ALU.subtract))
                    step(dve.tensor_tensor_scan(f_R, ones[0:MH, :], i_r, 0.0, ALU.mult, ALU.max))
                    dve.tensor_tensor(l_m, F_, f_R, ALU.add).then_inc(rows_ready, 1)
                if s == 24:
                    dve.wait_ge(e_cols, 1)
                    dve.tensor_copy(r_col, ps[:, 3, 0:16].rearrange("p (t k h) -> p t k h", t=NT, k=2)[:, :, 0, :]).then_inc(r_cols, 1)
                if s in EVAC_AT:
                    evacuate(EVAC_AT[s])
                if s in TURN_COPY:
                    b = TURN_COPY[s]
                    dve.wait_ge(stage_turned, b + 1)
                    dve.tensor_copy(turned_tile(b, 1), ps[:, 1, :].rearrange("p (a n) -> p a n", a=2)).then_inc(turn_v, 1)
                if s in CONV_AT:
                    q, c4 = CONV_AT[s]
                    c = 4 * q + c4
                    dve.wait_ge(turn_a, 4 + q)
                    dve.wait_ge(turn_v, 4 + q)

                    def tap(j):
                        n = G_TAP + j * 2 * MQK // P + c
                        return cols[:, n:n + 1]

                    step(dve.tensor_scalar(conv_out[:, c, :], conv_in[:, c, 0:SEQ], tap(0), None, ALU.mult))
                    for j in range(1, CONV):
                        ins = dve.scalar_tensor_tensor(out=conv_out[:, c, :], in0=conv_in[:, c, j:j + SEQ], scalar=tap(j),
                                                       in1=conv_out[:, c, :], op0=ALU.mult, op1=ALU.add)
                        if j < CONV - 1:
                            step(ins)
                    ins.then_inc(conv_ready, 1)
                g = group_at(s, 3)
                if g is not None:
                    j, b = divmod(g, 2)
                    K = P * (b + 1)
                    st = a_stat[:, g % 2]
                    dve.wait_ge(scored, g + 1)
                    for hh in range(GROUP):
                        slope = float(np.exp2(np.float32(-8.0 * (GROUP * j + hh + 1) / HEADS)))
                        off = (hh // 2) * K
                        ins = dve.scalar_tensor_tensor(out=probs[:, g % 2, hh * K:(hh + 1) * K], in0=dist[:, 2 * P - K:2 * P],
                                                       scalar=-slope, in1=ps[:, hh % 2, off:off + K],
                                                       op0=ALU.mult, op1=ALU.add)
                    step(ins)
                    step(dve.tensor_reduce(st[:, 0, :], probs[:, g % 2, 0:GROUP * K].rearrange("p (h k) -> p h k", h=GROUP),
                                           AX.X, ALU.max))
                    sink = sinks[:, GROUP * j:GROUP * (j + 1)]
                    step(dve.tensor_tensor(st[:, 1, :], st[:, 0, :], sink, ALU.max))
                    dve.tensor_scalar(st[:, 2, :], st[:, 1, :], -1.0, None, ALU.mult)
                    dve.tensor_tensor(st[:, 3, :], sink, st[:, 1, :], ALU.subtract).then_inc(maxed, 1)
                g = group_at(s, 5)
                if g is not None:
                    K = P * (g % 2 + 1)
                    st = a_stat[:, g % 2]
                    dve.wait_ge(exped, g + 1)
                    step(dve.tensor_tensor(st[:, 6, :], st[:, 4, :], st[:, 5, :], ALU.add))
                    step(dve.reciprocal(st[:, 7, :], st[:, 6, :]))
                    pv = probs[:, g % 2, 0:GROUP * K].rearrange("p (h k) -> p h k", h=GROUP)
                    dve.tensor_tensor(pv, pv, st[:, 7, :].rearrange("p (h k) -> p h k", k=1).to_broadcast([P, GROUP, K]),
                                      ALU.mult).then_inc(normed, 1)
                g = group_at(s, 7)
                if g is not None and g % 2:
                    dve.wait_ge(p_turned, g + 1)
                    dve.tensor_copy(probs_T[:, g % 2, COLS:2 * COLS], ps[:, 3, :]).then_inc(pt_v, 1)
                if s == 80:
                    dve.wait_ge(ev_a, act_evacs(8))
                    for t in range(NT):
                        ins = dve.tensor_tensor(smo[:, t, :], smo[:, t, :], head_g[:, :], ALU.mult)
                    step(ins)
                if s == 87:
                    dve.wait_ge(neg_r, 1)
                    bc = ps[:, 0:2, :].rearrange("p a (c n) -> p (a c) n", c=2)
                    fut = future[:, :].rearrange("p (a n) -> p a n", a=1).to_broadcast([P, MH, P])
                    dve.tensor_tensor(wt[:, :, 0:P], bc[:, :, 0:P], fut, ALU.add)
                    dve.tensor_copy(wt[:, :, P:2 * P], bc[:, :, P:2 * P])
                    dve.tensor_tensor(wt[:, :, 2 * P:3 * P], bc[:, :, P:2 * P], fut, ALU.add).then_inc(wt_arg, 1)
                if s == 93:
                    dve.wait_ge(m_scored, 1)
                    dve.wait_ge(wt_ready, 1)
                    for hd in range(MH):
                        ins = dve.scalar_tensor_tensor(out=pt_m[:, hd, :], in0=ps[:, hd, 0:WTN], scalar=float(QKD) ** -0.5,
                                                       in1=wt[:, hd, :], op0=ALU.mult, op1=ALU.mult)
                    ins.then_inc(pt_m_ready, 1)
                for b in range(NT):
                    if s == 97 + 6 * b:
                        dve.wait_ge(num_done, b + 1)
                        dve.wait_ge(e_cols, 1)
                        d = den[:, b, :]
                        step(dve.tensor_copy(d, ps[:, 0:MH, VD]))
                        step(dve.scalar_tensor_tensor(out=d, in0=d, scalar=-1.0, in1=d, op0=ALU.mult, op1=ALU.max))
                        step(dve.tensor_tensor(d, d, e_col[:, b, :], ALU.max))
                        dve.reciprocal(rden[:, b, :], den[:, b, :]).then_inc(rden_ready, 1)
                        dve.wait_ge(rden_ready, b + 1)
                        for hd in range(2, MH):
                            ins = dve.tensor_scalar(m_h[:, b, hd * VD:(hd + 1) * VD], ps[:, hd, 0:VD], rden[:, b, hd:hd + 1],
                                                    None, ALU.mult)
                        ins.then_inc(mh_v, 1)
                    if s == 99 + 6 * b:
                        dve.wait_ge(m_squared, b + 1)
                        dve.tensor_scalar(ms_m[:, b, :], sq_m[:, b, :], 1.0 / VD, EPS, ALU.mult, ALU.add).then_inc(m_ms, 1)
                    if s == 101 + 6 * b:
                        dve.wait_ge(m_rstd, b + 1)
                        for hd in range(MH):
                            c = slice(hd * VD, (hd + 1) * VD)
                            ins = dve.scalar_tensor_tensor(out=smo[:, b, c], in0=m_h[:, b, c], scalar=rs_m[:, b, hd:hd + 1],
                                                           in1=smo[:, b, c], op0=ALU.mult, op1=ALU.mult)
                        ins.then_inc(m_rows, 1)
                if s == 115:
                    dve.wait_ge(m_turned, 1)
                    dve.tensor_copy(m_T[:, 4:8, :], ps[:, 2:4, :].rearrange("p a (c n) -> p (a c) n", c=2)).then_inc(mt_v, 1)
                if SPLIT_SLOT <= s < SPLIT_SLOT + 8:
                    q = s - SPLIT_SLOT
                    dve.wait_ge(att_split, q + 1)
                    src = att if q < 4 else m_T
                    k = k_tile(q)
                    dve.tensor_tensor(x_lo[:, k:k + 2, :], src[:, 2 * (q % 4):2 * (q % 4) + 2, :],
                                      x_hi[:, k:k + 2, :].bitcast(F32), ALU.subtract).then_inc(att_split_lo, 1)
                for j in range(NCB - 2):
                    if s == evac_slot(NIN + NCB + j) + 3:
                        copy_y(j)
            copy_y(NCB - 2)
            rows_quad(C_OUT, T_OUT, 0, "out", tail=(lambda: evacuate(NIN + 2 * NCB - 1), lambda: copy_y(NCB - 1)))
            with dve.Fori(1, ND // RAW - 1) as i:
                rows_quad(C_OUT, T_OUT, i, "out")
            rows_quad(C_OUT, T_OUT, ND // RAW - 1, "out", last=True)
            swiglu(1)
            norm_y(2, 0.5)
            for i in range(NCB):
                scale_y(2, i)

        @block.tensor
        def _(pe):
            def three(dst, x_tile, t, w, n0, start, stop):
                xh = x_hi[:, x_tile, t * P:(t + 1) * P]
                pe.matmul(dst, xh, w_hi[:, w, n0:n0 + COLS], start=start, stop=False)
                pe.matmul(dst, xh, w_lo[:, w, n0:n0 + COLS], start=False, stop=False)
                return pe.matmul(dst, x_lo[:, x_tile, t * P:(t + 1) * P], w_hi[:, w, n0:n0 + COLS], start=False, stop=stop)

            def turn(dst, src):
                return pe.transpose(dst, src, ident[:, :])

            def turn_h(e, u):
                if e:
                    pe.wait_ge(h_ready, (e - 1) * NCB + u // 2 + 1)
                elif u % 2 == 0:
                    pe.wait_ge(x_in[CBO[u // 2]], 16)
                if u >= 2:
                    pe.wait_ge(x_lo_ready, e * ND // 2 + u - 1)
                for kk in range(2):
                    for t in range(NT):
                        k = k_tile(u) + kk
                        n = kk * SEQ + t * P
                        ins = turn(ps[:, 6 + u % 2, n:n + P], h[:, t, k * P:(k + 1) * P])
                ins.then_inc(h_turned, 1)

            def begin(e, halves):
                turn_h(e, 0)
                turn_h(e, 1)
                for j in range(ND // 2):
                    pe.wait_ge(x_lo_ready, e * ND // 2 + j + 1)
                    if e and j == 0:
                        pe.wait_ge(y_scaled, (e - 1) * NCB + 2)
                    halves(j)
                    if j + 2 < ND // 2:
                        turn_h(e, j + 2)

            def turn_y(j):
                pe.wait_ge(y_ready, j + 1)
                if j == 2:
                    pe.wait_ge(yt_a, 1)
                    pe.wait_ge(yt_v, 1)
                for c in range(4):
                    for t in range(NT):
                        n = (c % 2) * SEQ + t * P
                        ins = turn(ps[:, Y_BANK[j] + c // 2, n:n + P], y[:, t, (4 * j + c) * P:(4 * j + c + 1) * P])
                ins.then_inc(y_turned, 1)

            def turn_hidden(e, i, base):
                pe.wait_ge(prod_ready, e * NFB + i + 1)
                pe.wait_ge(silu_ready, e * NFB + i + 1)
                for a in range(2):
                    for kk in range(2):
                        for t in range(NT):
                            c = (2 * a + kk) * P
                            ins = turn(ps[:, base + a, kk * SEQ + t * P:kk * SEQ + (t + 1) * P], prod[:, t, c:c + P])
                ins.then_inc(prod_turned, 1)

            def up_block(e, i, even, first, old):
                base = 4 if even else 0

                def halves(j):
                    n, q = divmod(j, 8)
                    pe.wait_ge(lo_ready, 2 * C_UP[e] + i * 4 * BLOCK_CHUNKS + j + 1)
                    for kk in range(2):
                        for t in range(NT):
                            ins = three(ps[:, base + 2 * n + t, :], k_tile(q) + kk, t, j % SPL, kk * COLS,
                                        q == kk == 0, q == 7 and kk == 1)
                    ins.then_inc(w_used, 1)

                if first:
                    begin(e and 2, halves)
                for j in range(ND // 2 if first else 0, 4 * BLOCK_CHUNKS):
                    if old and j == 0:
                        pe.wait_ge(hid_a, e * NFB + i - 1)
                        pe.wait_ge(hid_v, e * NFB + i - 1)
                    if isinstance(i, int) and i == 1 and e and j == 0:
                        pe.wait_ge(y_scaled, 2 * NCB)
                    halves(j)
                    if j == 4 and not first:
                        turn_hidden(e, i - 1, 4 - base)

            def row_half(H, T, slot, w, half, start, stop):
                pe.wait_ge(lo_ready, H + 1)
                pe.wait_ge(xs_lo_ready, T + 1)
                for t in range(NT):
                    for c in range(2):
                        ins = three(ps[:, 4 * half + 2 * c + t, :], slot, t, w, c * COLS, start, stop)
                ins.then_inc(w_used, 1)

            def rows_quad(base_c, T0, i, first, tail=None):
                for j, (q, half) in enumerate(QUAD):
                    if tail and j == 1:
                        tail()
                    row_half(2 * base_c + i * 2 * RAW + j, T0 + i * RAW + q, q, j % SPL, half,
                             first and q == 0, False)

            def last_rows_quad(base_c, T0, i):
                H = 2 * base_c + i * 2 * RAW
                for j, (q, half) in enumerate(LAST_QUAD[:RAW]):
                    row_half(H + j, T0 + i * RAW + q, q, j % SPL, half, False, q == RAW - 1)
                pe.wait_ge(lo_ready, H + 2 * RAW)
                for c in range(2):
                    for t in range(NT):
                        for q in range(RAW):
                            ins = three(ps[:, 4 + 2 * c + t, :], q, t, q, c * COLS, False, q == RAW - 1)
                            if c == t == 1:
                                ins.then_inc(w_used, 1)
                        if not c == t == 1:
                            ins.then_inc(y_bank, 1)

            def by_rows(base_c, T0, n, tail=None):
                rows_quad(base_c, T0, 0, True, tail)
                if n > 2 * RAW:
                    with pe.Fori(1, n // RAW - 1) as i:
                        rows_quad(base_c, T0, i, False)
                last_rows_quad(base_c, T0, n // RAW - 1)

            def swiglu(e):
                up_block(e, 0, True, True, False)
                up_block(e, 1, False, False, False)
                up_block(e, 2, True, False, True)
                with pe.Fori(1, NFB // 2) as it:
                    up_block(e, it * 2 + 1, False, False, True)
                    up_block(e, it * 2 + 2, True, False, True)
                pe.wait_ge(hid_a, e * NFB + NFB - 1)
                pe.wait_ge(hid_v, e * NFB + NFB - 1)

                def tail():
                    turn_hidden(e, NFB - 1, 4)
                    pe.wait_ge(hid_a, (e + 1) * NFB)
                    pe.wait_ge(hid_v, (e + 1) * NFB)

                by_rows(C_DOWN[e], T_DOWN[e], NF, tail)

            pe.wait_ge(const_step, 2)
            pe.wait_ge(rows_in, 80)
            pe.transpose(ps[:, 5, 0:NROWS], rows[0:NROWS, :], ident[0:NROWS, 0:NROWS]).then_inc(rows_turned, 1)
            swiglu(0)

            def gates(s):
                if s == 4:
                    pe.wait_ge(y_scaled, NCB)
                    pe.wait_ge(wg_lo_ready, 1)
                for q in (2 * s - 8, 2 * s - 7):
                    for kk in range(2):
                        k = k_tile(q) + kk
                        for t in range(NT):
                            dst = ps[:, 2, t * 2 * MH:(t + 1) * 2 * MH]
                            first, last = q == kk == t == 0, q == 7 and kk == t == 1
                            xh = x_hi[:, k, t * P:(t + 1) * P]
                            pe.matmul(dst, xh, wg_hi[:, k, :], start=first, stop=False, skip_group_check=True)
                            pe.matmul(dst, xh, wg_lo[:, k, :], start=False, stop=False, skip_group_check=True)
                            ins = pe.matmul(dst, x_lo[:, k, t * P:(t + 1) * P], wg_hi[:, k, :], start=False, stop=last,
                                            skip_group_check=True)
                if s == 7:
                    ins.then_inc(gates_done, 1)

            def in_half(s):
                if s < A_SLOT:
                    b, q = divmod(s, 8)
                    last, k = q == 7, k_tile(q)
                else:
                    b, q = divmod(s - A_SLOT, 4)
                    b += NIN
                    last, k = q == 3, k_tile(q if s < M_SLOT else 4 + q)
                    if b == NIN:
                        pe.wait_ge(att_split_lo, q + 1)
                    if b == NIN + NCB:
                        pe.wait_ge(att_split_lo, 4 + q + 1)
                if q == 0 and b >= 2:
                    pe.wait_ge(ev_a, act_evacs(b - 2))
                    if dve_evacs(b - 2):
                        pe.wait_ge(ev_v, dve_evacs(b - 2))
                pe.wait_ge(lo_ready, H_MIX + s + 1)
                for kk in range(2):
                    for t in range(NT):
                        ins = three(ps[:, 4 + 2 * (b % 2) + t, :], k + kk, t, s % SPL, kk * COLS, q == kk == 0,
                                    last and kk == 1)
                ins.then_inc(w_used, 1)
                if 4 <= s < 8:
                    gates(s)

            begin(1, in_half)
            for s in range(ND // 2, END_SLOT):
                in_half(s)
                if s == 12:
                    pe.wait_ge(gates_ready, 1)
                    for n in range(2):
                        for t in range(NT):
                            ins = turn(ps[0:MH, 3, n * SEQ + t * P:n * SEQ + (t + 1) * P],
                                       gates_tok[:, t, n * MH:(n + 1) * MH])
                    ins.then_inc(gates_turned, 1)
                if s == 22:
                    pe.wait_ge(rows_ready, 1)
                    for t in range(NT):
                        for n, row in enumerate((0, 2)):
                            c = t * 2 * MH + n * MH
                            ins = pe.transpose(ps[:, 3, c:c + MH], rows4[:, row, t * P:(t + 1) * P], ident[0:MH, 0:MH])
                    ins.then_inc(r_turned, 1)
                if s in TURN_B:
                    b = TURN_B[s]
                    pe.wait_ge(ev_a, act_evacs(b))
                    pe.wait_ge(ev_v, dve_evacs(b))
                    if b >= 2:
                        pe.wait_ge(maxed, b - 1)
                    if b:
                        pe.wait_ge(turn_a, b)
                        pe.wait_ge(turn_v, b)
                    for c in range(4):
                        for t in range(NT):
                            n = (c % 2) * SEQ + t * P
                            ins = turn(ps[:, c // 2, n:n + P], stage[:, t, c * P:(c + 1) * P])
                    ins.then_inc(stage_turned, 1)
                g = group_at(s, 0)
                if g is not None:
                    j, b = divmod(g, 2)
                    K = P * (b + 1)
                    turns = min(2 + g, 5)
                    pe.wait_ge(turn_a, turns)
                    pe.wait_ge(turn_v, turns)
                    if g:
                        pe.wait_ge(maxed, g)
                    for i in range(2):
                        for par in range(2):
                            lo, hi = par * HD, (par + 1) * HD
                            ins = pe.matmul(ps[:, par, i * K:(i + 1) * K], att_qT[lo:hi, 2 * j + i, b * P:(b + 1) * P],
                                            att_kT[lo:hi, j, 0:K], start=(i == 0), stop=(i == 1), skip_group_check=True)
                    ins.then_inc(scored, 1)
                g = group_at(s, 4)
                if g is not None:
                    j, b = divmod(g, 2)
                    K = P * (b + 1)
                    pe.wait_ge(normed, g + 1)
                    if g == 0:
                        pe.wait_ge(r_cols, 1)
                    if g:
                        pe.wait_ge(pv_out, g)
                    if g >= 2:
                        pe.wait_ge(pt_v, g // 2)
                    for kt in range(b + 1):
                        for hh in range(GROUP):
                            n = ((hh % 2) * 2 + hh // 2) * P
                            ins = turn(ps[:, 2 + kt, n:n + P], probs[:, g % 2, hh * K + kt * P:hh * K + (kt + 1) * P])
                    ins.then_inc(p_turned, 1)
                g = group_at(s, 6)
                if g is not None:
                    j, b = divmod(g, 2)
                    pe.wait_ge(pt_a, g + 1)
                    if b:
                        pe.wait_ge(pt_v, g // 2 + 1)
                    for par in range(2):
                        for kt in range(b + 1):
                            n = kt * COLS + par * 2 * P
                            ins = pe.matmul(ps[par * HD:(par + 1) * HD, 2, 0:2 * P], att_v[:, kt, j * HD:(j + 1) * HD],
                                            probs_T[:, g % 2, n:n + 2 * P], start=(kt == 0), stop=(kt == b))
                    ins.then_inc(pv_done, 1)
                if s == 84:
                    pe.wait_ge(maxed, NG)
                    pe.wait_ge(const_ready, 3)
                    for hd in range(MH):
                        ins = pe.matmul(ps[:, hd // 2, (hd % 2) * SEQ:(hd % 2 + 1) * SEQ], sel[:, hd, :], rows4[:, 1, :],
                                        start=(hd % 2 == 0), stop=(hd % 2 == 1), skip_group_check=True)
                    ins.then_inc(neg_r, 1)
                if s == 90:
                    pe.wait_ge(conv_silu, 2)
                    pe.wait_ge(wt_arg, 1)
                    pe.wait_ge(pv_out, NG)
                    pe.wait_ge(pt_v, NG // 2)
                    for hd in range(MH):
                        pe.matmul(ps[:, hd, 0:SEQ], conv_out[:, MH + hd, 0:P], conv_out[:, hd, :], start=True, stop=False,
                                  skip_group_check=True)
                        ins = pe.matmul(ps[:, hd, SEQ:WTN], conv_out[:, MH + hd, P:SEQ], conv_out[:, hd, P:SEQ],
                                        start=False, stop=True, skip_group_check=True)
                    ins.then_inc(m_scored, 1)
                for b in range(NT):
                    if s == 94 + 6 * b:
                        if b:
                            pe.wait_ge(mh_a, 1)
                            pe.wait_ge(mh_v, 1)
                        else:
                            pe.wait_ge(pt_m_ready, 1)
                            pe.wait_ge(ones_v, 1)
                            pe.wait_ge(ev_a, act_evacs(6))
                            pe.wait_ge(ev_v, dve_evacs(6))
                        for hd in range(MH):
                            for a in range(b + 1):
                                c = (b if a == 0 else 2) * P
                                ins = pe.matmul(ps[:, hd, 0:VD + 1], pt_m[:, hd, c:c + P], mval[:, a, hd, :],
                                                start=(a == 0), stop=(a == b))
                        ins.then_inc(num_done, 1)
                if s == 112:
                    pe.wait_ge(m_rows, NT)
                    pe.wait_ge(mh_a, NT)
                    pe.wait_ge(mh_v, NT)
                    for c in range(2 * MH):
                        for t in range(NT):
                            n = (c % 2) * SEQ + t * P
                            ins = turn(ps[:, c // 2, n:n + P], smo[:, t, c * P:(c + 1) * P])
                    ins.then_inc(m_turned, 1)
                for j in range(NCB - 1):
                    if s == evac_slot(NIN + NCB + j):
                        turn_y(j)
            pe.wait_ge(yt_a, NCB - 1)
            pe.wait_ge(yt_v, NCB - 1)

            def tail():
                turn_y(NCB - 1)
                pe.wait_ge(yt_a, NCB)
                pe.wait_ge(yt_v, NCB)

            by_rows(C_OUT, T_OUT, ND, tail)
            swiglu(1)


_INS = ["x", "ffn1_pre_g", "ffn1_wg", "ffn1_wu", "ffn1_wd", "ffn1_post_g", "mix_pre_g", "w_in", "conv_w", "conv_b",
        "attn_sinks", "m_igate_b", "m_fgate_b", "m_head_g", "w_attn_up", "w_mlstm_up", "w_out", "mix_post_g",
        "ffn2_pre_g", "ffn2_wg", "ffn2_wu", "ffn2_wd", "ffn2_post_g"]


def kernel(**inputs):
    import concourse.bacc as bacc
    from concourse.bass_utils import run_bass_kernel_spmd

    nc = bacc.Bacc("TRN2", target_bir_lowering=False, num_devices=1)
    arrays, args = {}, []
    for name in _INS:
        a = np.ascontiguousarray(inputs[name])
        arrays[f"in_{name}"] = a
        args.append(nc.dram_tensor(f"in_{name}", a.shape, mybir.dt.from_np(a.dtype), kind="ExternalInput").ap())
    shape = np.shape(inputs["x"])
    args.append(nc.dram_tensor("out_y", shape, F32, kind="ExternalOutput").ap())
    hybrid_layer(nc, *args)
    r = run_bass_kernel_spmd(nc, [arrays], core_ids=[0])
    return r.results[0]["out_y"]
```

```python
from contextlib import ExitStack

import numpy as np

import concourse.bass as bass
from concourse import mybir

F32 = mybir.dt.float32
F32R = mybir.dt.float32r
ALU = mybir.AluOpType
ACT = mybir.ActivationFunctionType
AX = mybir.AxisListType

P = 128
EPS = 1e-6
MASKED = -1e30


def hybrid_layer(nc: bass.Bass, x, ffn1_pre_g, ffn1_wg, ffn1_wu, ffn1_wd, ffn1_post_g, mix_pre_g,
                 w_in, conv_w, conv_b, attn_sinks, m_igate_b, m_fgate_b, m_head_g, w_attn_up,
                 w_mlstm_up, w_out, mix_post_g, ffn2_pre_g, ffn2_wg, ffn2_wu, ffn2_wd, ffn2_post_g,
                 out):
    _, SEQ, D = x.shape
    F = ffn1_wg.shape[2]
    NT = SEQ // P
    ND = D // P
    NF = F // P
    COLS = 512
    NCB = D // COLS
    HEADS = attn_sinks.shape[1]
    KVH = 4
    GROUP = HEADS // KVH
    HD = 64
    MH = m_igate_b.shape[1]
    CONV = conv_w.shape[1]
    MQK = conv_w.shape[2] // 2
    QKD = MQK // MH
    MV = m_head_g.shape[1]
    VD = MV // MH
    ATT_Q, ATT_KV = HEADS * HD, KVH * HD
    assert NT == 2 and ND == 16 and NCB == 4 and QKD == P and VD == 2 * P and ATT_Q == MV == 1024

    HALF = 1024
    RAW = 4
    SPL = 4
    KC = 4
    BLOCK_CHUNKS = ND // KC
    NFB = F // COLS
    UP_CHUNKS = NFB * 2 * BLOCK_CHUNKS
    UPK = ATT_Q // P
    UP_BLOCK_CHUNKS = UPK // KC
    OFF_K = ATT_Q
    OFF_MQ = ATT_Q + 2 * ATT_KV
    OFF_MK = OFF_MQ + MQK
    OFF_MV = OFF_MK + MQK
    OFF_MO = OFF_MV + MV
    OFF_GATES = OFF_MO + MV
    OFF_GA = OFF_GATES + 2 * MH
    OFF_GM = OFF_GA + D
    IN_BLOCKS = ([("k", 0, OFF_K)] + [("q", j, j * COLS) for j in range(2)]
                 + [("mqk", 0, OFF_MQ), ("mqk", 1, OFF_MK)]
                 + [("mv", j, OFF_MV + j * COLS) for j in range(2)]
                 + [("mo", j, OFF_MO + j * COLS) for j in range(2)]
                 + [("ga", j, OFF_GA + j * COLS) for j in range(4)]
                 + [("gm", j, OFF_GM + j * COLS) for j in range(4)])
    NIN = len(IN_BLOCKS)
    A_SLOT = NIN * 8
    M_SLOT = A_SLOT + NCB * 2 * UP_BLOCK_CHUNKS
    END_SLOT = M_SLOT + NCB * 2 * UP_BLOCK_CHUNKS
    C_UP = [0, 0]
    C_DOWN = [C_UP[0] + UP_CHUNKS, 0]
    C_MIX = C_DOWN[0] + NF
    C_OUT = C_MIX + END_SLOT // 2
    C_UP[1] = C_OUT + ND
    C_DOWN[1] = C_UP[1] + UP_CHUNKS
    H_MIX = 2 * C_MIX
    CBO = (3, 2, 0, 1)
    assert NCB == BLOCK_CHUNKS == 4
    Y_BANKS = (0, 1, 2, 3, 4, 6, 5, 7)
    assert NT == 2

    def k_tile(q):
        return KC * CBO[q // 2] + 2 * (q % 2)

    QUAD = [(q, half) for q in range(RAW) for half in range(2)]
    EDGE_QUAD = [(q, half) for half in range(2) for q in range(RAW)]
    Y_END = [2 * (C_DOWN[0] + NF), 2 * (C_OUT + ND), 2 * (C_DOWN[1] + NF)]
    assert all(c % RAW == 0 for c in C_UP + C_DOWN + [C_MIX, C_OUT])
    T_DOWN = [0, NF + ND]
    T_OUT = NF

    def ends(b):
        return 8 * b + 7 if b < NIN else A_SLOT + 4 * (b - NIN) + 3

    def evac_slot(b):
        return ends(b) + 3

    EVAC_AT = {evac_slot(b): b for b in range(NIN + 2 * NCB)}
    kinds = [k for k, _, _ in IN_BLOCKS] + ["A"] * NCB + ["M"] * NCB

    def act_evacs(b):
        return sum(k not in ("A", "M") for k in kinds[:b + 1])

    def dve_evacs(b):
        return sum(k not in ("mo", "ga", "gm") for k in kinds[:b + 1])

    TURN_B = {8 * b + 9: b for b in (0, 1, 2, 3, 4)}
    TURN_COPY = {8 * b + 13: b for b in (0, 1, 2, 3, 4)}
    CONV_AT = {38 + 8 * q + c: (q, c) for q in range(2) for c in range(4)}
    SILU_AT = {43 + 8 * q: q for q in range(2)}
    G0 = 22
    NG = 2 * KVH
    SPLIT_SLOT = A_SLOT - SPL
    Y_BANK = (0, 2, 0, 6)

    def group_at(s, offset):
        g, rest = divmod(s - G0 - offset, 8)
        return g if rest == 0 and 0 <= g < NG else None

    ctx = ExitStack()
    with ctx:
        def sb(name, shape, dt=F32, where=ctx):
            return where.enter_context(nc.sbuf_tensor(name, shape, dt))

        def sem(name):
            return ctx.enter_context(nc.semaphore(name))

        raw = sb("raw", [P, RAW, 2 * HALF])
        w_hi = sb("w_hi", [P, SPL, HALF], F32R)
        w_lo = sb("w_lo", [P, SPL, HALF], F32R)
        x_hi = sb("x_hi", [P, ND, SEQ], F32R)
        x_lo = sb("x_lo", [P, ND, SEQ], F32R)
        h = sb("h", [P, NT, D])
        gain = sb("gain", [P, D])
        att = gain[:, :].rearrange("p (c t) -> p c t", t=SEQ)
        rows = sb("rows", [P, P])
        cols = sb("cols", [P, P])
        ident = sb("ident", [P, P])
        dist = sb("dist", [P, 2 * P])
        future = sb("future", [P, P])
        sel = sb("sel", [MH, MH, P])
        ones = sb("ones", [P, SEQ])
        neg_half = sb("neg_half", [P, 4])
        sinks = sb("sinks", [P, HEADS])
        head_g = sb("head_g", [P, MV])
        gate_b = sb("gate_b", [MH, 2])
        wg_raw = sb("wg_raw", [P, ND, 2 * MH])
        wg_hi = sb("wg_hi", [P, ND, 2 * MH], F32R)
        wg_lo = sb("wg_lo", [P, ND, 2 * MH], F32R)
        stat = sb("stat", [P, 64])
        sq_y = stat[:, 0:8].rearrange("p (t c) -> p t c", t=NT)
        ms_y = stat[:, 8:10]
        rs_y = stat[:, 10:12]
        sq_h = stat[:, 14:16]
        ms_h = stat[:, 16:18]
        rs_h = stat[:, 18:20]
        rs_q = stat[:, 20:22]
        m_stat = sb("m_stat", [P, 64])
        r_col = m_stat[:, 0:8].rearrange("p (t h) -> p t h", t=NT)
        e_col = m_stat[:, 8:16].rearrange("p (t h) -> p t h", t=NT)
        den = m_stat[:, 16:24].rearrange("p (t h) -> p t h", t=NT)
        rden = m_stat[:, 24:32].rearrange("p (t h) -> p t h", t=NT)
        sq_m = m_stat[:, 32:40].rearrange("p (t h) -> p t h", t=NT)
        ms_m = m_stat[:, 40:48].rearrange("p (t h) -> p t h", t=NT)
        rs_m = m_stat[:, 48:56].rearrange("p (t h) -> p t h", t=NT)
        a_stat = sb("a_stat", [P, 2, 8, 4])
        G_PRE = [0, ND, 2 * ND]
        G_TAP = 3 * ND
        G_BIAS = G_TAP + CONV * 2 * MQK // P
        NROWS = G_BIAS + 2 * MQK // P

        with ExitStack() as part:
            hid = sb("hid", [P, NF, SEQ], F32, part)
            silu = sb("silu", [P, NT, COLS], F32, part)
            prod = sb("prod", [P, NT, COLS], F32, part)
        dropped = hid[:, 0:NT * D // SEQ, :].rearrange("p a b -> p (a b)")
        z = hid[:, NT * D // SEQ:2 * NT * D // SEQ, :].rearrange("p (a c) b -> p a (c b)", a=NCB * NT)
        with ExitStack() as part:
            attn_in = sb("attn_in", [P, 3584], F32, part)
            m_in = sb("m_in", [P, 2 * MH * SEQ + NT * MH * (VD + 1)], F32, part)
            smo = sb("smo", [P, NT, MV], F32, part)
            y = sb("y", [P, NT, D], F32, part)
            gm = sb("gm", [P, NCB, NT * COLS], F32, part)
            rows4 = sb("rows4", [MH, 4, SEQ], F32, part)
        conv_out = m_in[:, 0:2 * MH * SEQ].rearrange("p (c t) -> p c t", t=SEQ)
        mval = m_in[:, 2 * MH * SEQ:].rearrange("p (t h d) -> p t h d", t=NT, h=MH)
        y_T = m_in[:, 0:ND * SEQ].rearrange("p (c t) -> p c t", t=SEQ)
        att_qT = attn_in[:, 0:2048].rearrange("p (c t) -> p c t", t=SEQ)
        att_kT = attn_in[:, 2048:3072].rearrange("p (c t) -> p c t", t=SEQ)
        att_v = attn_in[:, 3072:3584].rearrange("p (t d) -> p t d", t=NT)
        WTN = 3 * P
        wt = attn_in[:, 0:MH * WTN].rearrange("p (h n) -> p h n", h=MH)
        pt_m = attn_in[:, MH * WTN:2 * MH * WTN].rearrange("p (h n) -> p h n", h=MH)
        y_flat = y[:, :, :].rearrange("p t d -> p (t d)")
        CP = SEQ + CONV - 1
        conv_in = y_flat[:, 0:8 * CP].rearrange("p (c n) -> p c n", n=CP)
        stage = y_flat[:, 8 * CP:8 * CP + NT * COLS].rearrange("p (t n) -> p t n", t=NT)
        gates8 = smo[0:2 * MH, 0, 0:SEQ]
        probs = gm[:, 0:2, :]
        probs_T = gm[:, 2:4, :]
        m_h = gm[:, 2:4, :]
        m_T = conv_out

        ps = ctx.enter_context(nc.psum_tensor("ps", [P, 8, COLS], F32))

        x_in = [sem(f"x_in{i}") for i in range(NCB)]
        gain_rows_in = sem("gain_rows_in")
        rows_in = sem("rows_in")
        misc_in = sem("misc_in")
        wg_in = sem("wg_in")
        gain_in = sem("gain_in")
        first_half_in = sem("first_half_in")
        raw_full = [sem(f"raw_full{i}") for i in range(RAW)]
        hi_ready = sem("hi_ready")
        lo_ready = sem("lo_ready")
        w_used = sem("w_used")
        const_step = sem("const_step")
        const_ready = sem("const_ready")
        rows_turned = sem("rows_turned")
        cols_ready = sem("cols_ready")
        h_turned = sem("h_turned")
        x_hi_ready = sem("x_hi_ready")
        x_lo_ready = sem("x_lo_ready")
        xs_hi_ready = sem("xs_hi_ready")
        xs_lo_ready = sem("xs_lo_ready")
        y_bank = sem("y_bank")
        z_ready = sem("z_ready")
        z_scaled = sem("z_scaled")
        h_squared = sem("h_squared")
        h_ms = sem("h_ms")
        h_rstd = sem("h_rstd")
        y_squared = sem("y_squared")
        y_ms = sem("y_ms")
        y_rstd = sem("y_rstd")
        h_ready_0 = sem("h_ready_0")
        h_ready_1 = sem("h_ready_1")
        h_ready_pool = sem("h_ready_pool")
        silu_ready = sem("silu_ready")
        prod_ready = sem("prod_ready")
        prod_turned = sem("prod_turned")
        hid_a = sem("hid_a")
        hid_v = sem("hid_v")
        act_step = sem("act_step")
        dve_step = sem("dve_step")
        wg_hi_ready = sem("wg_hi_ready")
        wg_lo_ready = sem("wg_lo_ready")
        gates_done = sem("gates_done")
        gates_ready = sem("gates_ready")
        gates_turned = sem("gates_turned")
        gate_rows = sem("gate_rows")
        log_ready = sem("log_ready")
        rows_ready = sem("rows_ready")
        r_turned = sem("r_turned")
        r_cols = sem("r_cols")
        e_cols = sem("e_cols")
        ev_a = sem("ev_a")
        ev_v = sem("ev_v")
        stage_turned = sem("stage_turned")
        turn_a = sem("turn_a")
        turn_v = sem("turn_v")
        conv_ready = sem("conv_ready")
        conv_silu = sem("conv_silu")
        scored = sem("scored")
        maxed = sem("maxed")
        exped = sem("exped")
        normed = sem("normed")
        p_turned = sem("p_turned")
        pt_a = sem("pt_a")
        pt_v = sem("pt_v")
        pv_done = sem("pv_done")
        pv_out = sem("pv_out")
        neg_r = sem("neg_r")
        wt_arg = sem("wt_arg")
        wt_ready = sem("wt_ready")
        m_scored = sem("m_scored")
        pt_m_ready = sem("pt_m_ready")
        num_done = sem("num_done")
        rden_ready = sem("rden_ready")
        mh_a = sem("mh_a")
        mh_v = sem("mh_v")
        m_squared = sem("m_squared")
        m_ms = sem("m_ms")
        m_rstd = sem("m_rstd")
        m_rows = sem("m_rows")
        m_turned = sem("m_turned")
        mt_a = sem("mt_a")
        mt_v = sem("mt_v")
        att_split = sem("att_split")
        att_split_lo = sem("att_split_lo")
        ones_v = sem("ones_v")
        q_scale = sem("q_scale")
        y_ready = sem("y_ready")
        y_turned = sem("y_turned")
        yt_a = sem("yt_a")
        yt_v = sem("yt_v")
        stored = sem("stored")

        WG = [ffn1_wg[0], ffn2_wg[0]]
        WU = [ffn1_wu[0], ffn2_wu[0]]
        WD = [ffn1_wd[0], ffn2_wd[0]]

        def src_tile(phase, n):
            return hid[:, n, :] if phase != "out" else y_T[:, n, :]

        block = ctx.enter_context(nc.Block())

        @block.sync
        def _(sp):
            def load_x(cb):
                c = slice(cb * COLS, (cb + 1) * COLS)
                sp.dma_start(h[:, :, c], x[0].rearrange("(t p) d -> p t d", p=P)[:, :, c]).then_inc(x_in[cb], 16)

            def load(c, slot, src, by_k, first=False, after_rows=False):
                if after_rows:
                    sp.wait_ge(lo_ready, 2 * (c - slot) - RAW + 1 + slot)
                elif not first:
                    sp.wait_ge(lo_ready, 2 * c - 2 * RAW + 2)
                dst = raw[:, slot, :]
                if by_k:
                    dst = dst.rearrange("p (k n) -> p k n", k=KC)
                if isinstance(c, int) and c == 0:
                    sp.dma_start(dst[:, 0:KC // 2, :], src[:, 0:KC // 2, :]).then_inc(first_half_in, 16)
                    dst, src = dst[:, KC // 2:, :], src[:, KC // 2:, :]
                sp.dma_start(dst, src).then_inc(raw_full[slot], 16)

            def by_columns(w, k0, col):
                return w.rearrange("(k p) n -> p k n", p=P)[:, k0:k0 + KC, bass.ds(col, COLS)]

            def up_block(e, i, col, first=False):
                for n, w in enumerate((WG[e], WU[e])):
                    for q in range(BLOCK_CHUNKS):
                        j = n * BLOCK_CHUNKS + q
                        if first and e == 0 and j < NCB:
                            load_x(CBO[j])
                        load(C_UP[e] + i * 2 * BLOCK_CHUNKS + j, j % RAW, by_columns(w, KC * CBO[q], col), True,
                             first=first and j < RAW and e == 0, after_rows=first and j < RAW and e == 1)

            def by_rows(w, base, n):
                for c in range(2 * RAW):
                    load(base + c, c % RAW, w[c * P:(c + 1) * P, :], False, after_rows=c >= RAW)
                with sp.Fori(2, n // RAW) as i:
                    for q in range(RAW):
                        load(base + i * RAW + q, q, w[bass.ds(i * (RAW * P) + q * P, P), :], False)

            sp.dma_start(rows[0:ND, :], ffn1_pre_g[0].rearrange("(k p) -> k p", p=P)).then_inc(gain_rows_in, 16)
            for e in range(2):
                up_block(e, 0, 0, first=True)
                with sp.Fori(0, NFB - 1) as i:
                    up_block(e, i + 1, i * COLS + COLS)
                by_rows(WD[e], C_DOWN[e], NF)
                if e == 0:
                    c = C_MIX
                    for _, _, col in IN_BLOCKS:
                        for q in range(BLOCK_CHUNKS):
                            load(c, c % RAW, by_columns(w_in[0], KC * CBO[q], col), True, after_rows=c < C_MIX + RAW)
                            c += 1
                    for w in (w_attn_up[0], w_mlstm_up[0]):
                        with sp.Fori(0, NCB // 2) as i:
                            for b in range(2):
                                for q in range(UP_BLOCK_CHUNKS):
                                    j = b * UP_BLOCK_CHUNKS + q
                                    load(c + i * 2 * UP_BLOCK_CHUNKS + j, j % RAW,
                                         by_columns(w, KC * q, i * (2 * COLS) + b * COLS), True)
                        c += NCB * UP_BLOCK_CHUNKS
                    by_rows(w_out[0], C_OUT, ND)
            for t in range(NT):
                for i, cb in enumerate(CBO):
                    if t == 0:
                        sp.wait_ge(h_ready_0, 2 * NCB + i + 1)
                    elif i < NCB - 1:
                        sp.wait_ge(h_ready_1, 2 * 2 + i + 2)
                    else:
                        sp.wait_ge(h_ready_pool, 2 * (NCB - 1) + 1)
                    c = slice(cb * COLS, (cb + 1) * COLS)
                    sp.dma_start(out[0, t * P:(t + 1) * P, c], h[:, t, c]).then_inc(stored, 16)
            sp.wait_ge(stored, 16 * NT * NCB)

        @block.gpsimd
        def _(pool):
            steps = [0]

            def step(ins):
                steps[0] += 1
                ins.then_inc(const_step, 1)
                pool.wait_ge(const_step, steps[0])

            step(pool.memset(ident[:, :], 0.0))
            step(pool.affine_select(out=ident[:, :], in_=ident[:, :], compare_op=ALU.not_equal, fill=1.0, base=0,
                                    pattern=[[-1, P]], channel_multiplier=1))
            pool.memset(neg_half[:, :], -0.5).then_inc(const_ready, 1)
            pool.memset(ones[:, :], 1.0).then_inc(const_ready, 1)
            pool.wait_ge(hi_ready, 4)
            pool.dma_start(gain[:, :], ffn1_post_g.to_broadcast([P, D])).then_inc(gain_in, 16)
            with nc.allow_non_contiguous_dma(reason="a few gate columns and biases"):
                pool.dma_start(wg_raw[:, :, :], w_in[0].rearrange("(k p) n -> p k n", p=P)[:, :, OFF_GATES:OFF_GA]).then_inc(wg_in, 16)
                pool.dma_start(gate_b[:, 0:1], m_igate_b.rearrange("a h -> h a")).then_inc(misc_in, 16)
                pool.dma_start(gate_b[:, 1:2], m_fgate_b.rearrange("a h -> h a")).then_inc(misc_in, 16)
            pool.dma_start(sinks[:, :], attn_sinks.to_broadcast([P, HEADS])).then_inc(misc_in, 16)
            pool.dma_start(head_g[:, :], m_head_g.to_broadcast([P, MV])).then_inc(misc_in, 16)
            step(pool.iota(dist[:, :], pattern=[[-1, 2 * P]], base=P, channel_multiplier=1,
                           allow_small_or_imprecise_dtypes=True))
            step(pool.affine_select(out=dist[:, :], in_=dist[:, :], compare_op=ALU.is_ge, fill=-MASKED, base=P,
                                    pattern=[[-1, 2 * P]], channel_multiplier=1))
            step(pool.affine_select(out=dist[:, :], in_=dist[:, :], compare_op=ALU.is_gt, fill=-MASKED, base=0,
                                    pattern=[[1, 2 * P]], channel_multiplier=-1))
            step(pool.memset(future[:, :], 0.0))
            step(pool.affine_select(out=future[:, :], in_=future[:, :], compare_op=ALU.is_ge, fill=MASKED, base=0,
                                    pattern=[[1, P]], channel_multiplier=-1))
            step(pool.memset(sel[:, :, :], 0.0))
            pool.affine_select(out=sel[:, :, :], in_=sel[:, :, :], compare_op=ALU.not_equal, fill=-1.0, base=0,
                               pattern=[[-1, MH], [0, P]], channel_multiplier=1).then_inc(const_ready, 1)

            def inverse_root(ms, dst, wait, count, done):
                pool.wait_ge(wait, count)
                pool.tensor_tensor(dst, ms, neg_half[:, 0:ms.shape[1]], ALU.pow).then_inc(done, 1)

            def post(p):
                for t in range(NT):
                    inverse_root(ms_y[:, t:t + 1], rs_y[:, t:t + 1], y_ms, NT * p + t + 1, y_rstd)
                pool.wait_ge(y_rstd, NT * (p + 1))
                pool.wait_ge(z_ready, (p + 1) * NCB * NT)
                for cb in CBO[1:] if p < 2 else CBO[-1:]:
                    c = slice(cb * COLS, (cb + 1) * COLS)
                    z_1 = z[:, 2 * cb + 1, :]
                    if p == 2:
                        pool.wait_ge(z_scaled, 1)
                    else:
                        step(pool.tensor_tensor(z_1, z_1, rs_y[:, 1:2].to_broadcast([P, COLS]), ALU.mult))
                    pool.tensor_tensor(h[:, 1, c], z_1, h[:, 1, c], ALU.add).then_inc(h_ready_pool, 1)

            pool.wait_ge(const_ready, 3)
            inverse_root(ms_h, rs_h, h_ms, 1, h_rstd)
            post(0)
            pool.wait_ge(h_ready_0, NCB)
            pool.wait_ge(h_ready_1, 2)
            pool.wait_ge(h_ready_pool, NCB - 1)
            pool.memset(mval[:, :, :, VD:VD + 1], 1.0).then_inc(ones_v, 1)
            pool.memset(conv_in[:, :, 0:CONV - 1], 0.0).then_inc(ones_v, 1)
            inverse_root(ms_h, rs_h, h_ms, 2, h_rstd)
            for b in range(NT):
                inverse_root(ms_m[:, b, :], rs_m[:, b, :], m_ms, b + 1, m_rstd)
            pool.wait_ge(att_split_lo, 4)
            pool.dma_start(gain[:, :], mix_post_g.to_broadcast([P, D])).then_inc(gain_in, 16)
            post(1)
            inverse_root(ms_h, rs_h, h_ms, 3, h_rstd)
            pool.wait_ge(z_ready, 2 * NCB * NT)
            pool.dma_start(gain[:, :], ffn2_post_g.to_broadcast([P, D])).then_inc(gain_in, 16)
            post(2)

        @block.scalar
        def _(act):
            steps = [0]

            def step(ins):
                steps[0] += 1
                ins.then_inc(act_step, 1)
                act.wait_ge(act_step, steps[0])

            def split_hi(H, half, slot, hw, raw_wait, first=False):
                if isinstance(H, int) and H < 2:
                    act.wait_ge((first_half_in, raw_full[0])[H], 16)
                elif half == 0:
                    act.wait_ge(raw_full[slot], raw_wait)
                if not first:
                    act.wait_ge(w_used, H - SPL + 1)
                act.activation(w_hi[:, hw, :], raw[:, slot, half * HALF:(half + 1) * HALF], ACT.Copy).then_inc(hi_ready, 1)

            def split_static(H, first=False):
                c = H // 2
                split_hi(H, H % 2, c % RAW, H % SPL, 16 * (c // RAW + 1), first)

            def turn_in(e, u):
                act.wait_ge(h_turned, e * ND // 2 + u + 1)
                for kk in range(2):
                    k = k_tile(u) + kk
                    ins = act.activation(x_hi[:, k, :], ps[:, 6 + u % 2, kk * SEQ:(kk + 1) * SEQ], ACT.Identity,
                                         scale=cols[:, G_PRE[e] + k:G_PRE[e] + k + 1])
                ins.then_inc(x_hi_ready, 1)

            def square_h(e, t):
                if e == 0 and t == 0:
                    for cb in range(NCB):
                        act.wait_ge(x_in[cb], 16)
                if e and t == 0:
                    act.wait_ge(h_ready_0, e * NCB)
                    act.wait_ge(h_ready_1, e * 2)
                    act.wait_ge(h_ready_pool, e * (NCB - 1))
                act.activation(dropped[:, t * D:(t + 1) * D], h[:, t, :], ACT.Square,
                               accum_out=sq_h[:, t:t + 1]).then_inc(h_squared, 1)

            def squares_of_y(p, before_last=None):
                for bank in Y_BANKS:
                    if bank == 0:
                        act.wait_ge(w_used, Y_END[p] - RAW)
                    elif bank == 7:
                        if before_last:
                            before_last()
                        act.wait_ge(w_used, Y_END[p])
                    elif bank in (4, 5):
                        act.wait_ge(y_bank, 2 * p + bank - 3)
                    act.activation(dropped[:, bank * COLS:(bank + 1) * COLS], ps[:, bank, :], ACT.Square,
                                   accum_out=sq_y[:, bank % NT, bank // NT:bank // NT + 1]).then_inc(y_squared, 1)

            def begin(e, H0, split):
                if e:
                    squares_of_y(e - 1, lambda: split(0))
                else:
                    turn_in(e, 0)
                    split(0)
                    turn_in(e, 1)
                split(1)
                for u in range(ND // 2):
                    if e or u >= 2:
                        turn_in(e, u)
                    split(u + 2)
                    if u >= ND // 2 - NT:
                        square_h(e, u - (ND // 2 - NT))

            def silu_gate(e, i, base, started):
                act.wait_ge(w_used, 2 * C_UP[e] + i * 4 * BLOCK_CHUNKS + 2 * BLOCK_CHUNKS)
                if started:
                    act.wait_ge(prod_ready, e * NFB + i)
                for t in range(NT):
                    ins = act.activation(silu[:, t, :], ps[:, base + t, :], ACT.Silu, scale=rs_h[:, t:t + 1])
                ins.then_inc(silu_ready, 1)

            def copy_hidden(e, i, base):
                act.wait_ge(prod_turned, e * NFB + i + 1)
                act.activation(hid[:, bass.ds(i * 4, 2), :], ps[:, base, :].rearrange("p (a b) -> p a b", a=2),
                               ACT.Copy).then_inc(hid_a, 1)

            def up_block(e, i, even, first, very_first=False):
                base = 4 if even else 0

                def split(j):
                    H = 2 * C_UP[e] + i * 4 * BLOCK_CHUNKS + j
                    split_hi(H, j % 2, (j // 2) % RAW, j % SPL, (i * 2 + C_UP[e] // RAW + j // 2 // RAW + 1) * 16,
                             very_first and j < SPL)

                if first:
                    begin(e and 2, 2 * C_UP[e], split)
                for j in range(ND // 2 + 2 if first else 0, 4 * BLOCK_CHUNKS):
                    split(j)
                    if j == 7 and not first:
                        copy_hidden(e, i - 1, 4 - base)
                    if j == 10 and first and e == 0:
                        act.wait_ge(rows_turned, 2)
                        act.activation(cols[:, ND:NROWS], ps[:, 0, ND:NROWS], ACT.Copy).then_inc(cols_ready, 1)
                    if j == 10:
                        if first:
                            act.wait_ge(h_rstd, e * 2 + 1)
                        silu_gate(e, i, base, not first)

            def x_split(T, n, slot, phase):
                act.activation(x_hi[:, slot, :], src_tile(phase, n), ACT.Copy).then_inc(xs_hi_ready, 1)

            def rows_quad(base_c, T0, i, phase, e=None, beside=(), edge=False):
                for j, (q, half) in enumerate(EDGE_QUAD if edge else QUAD):
                    split_hi(2 * base_c + i * 2 * RAW + j, half, q, j % SPL, (i + base_c // RAW + 1) * 16)
                    if half == 0:
                        if q == 0 and phase == "down":
                            act.wait_ge(hid_a, e * NFB + i + 1)
                            act.wait_ge(hid_v, e * NFB + i + 1)
                        elif q == 0:
                            act.wait_ge(yt_a, i + 1)
                            act.wait_ge(yt_v, i + 1)
                        x_split(T0 + i * RAW + q, i * RAW + q, q, phase)
                    if j in beside:
                        beside[j]()

            def swiglu(e):
                up_block(e, 0, True, True, very_first=(e == 0))
                with act.Fori(0, NFB // 2) as it:
                    up_block(e, it * 2 + 1, False, False)
                    up_block(e, it * 2 + 2, True, False)
                if e == 0:
                    act.wait_ge(wg_in, 16)
                    act.activation(wg_hi[:, :, :], wg_raw[:, :, :], ACT.Copy).then_inc(wg_hi_ready, 1)
                rows_quad(C_DOWN[e], T_DOWN[e], 0, "down", e, {5: lambda: copy_hidden(e, NFB - 1, 4)}, edge=True)
                with act.Fori(1, NF // RAW - 1) as i:
                    rows_quad(C_DOWN[e], T_DOWN[e], i, "down", e)
                rows_quad(C_DOWN[e], T_DOWN[e], NF // RAW - 1, "down", e, edge=True)

            act.wait_ge(rows_turned, 1)
            act.activation(cols[:, 0:ND], ps[:, 5, 0:ND], ACT.Copy).then_inc(cols_ready, 1)
            act.wait_ge(cols_ready, 1)
            n_rows = ND
            for v in (mix_pre_g[0], ffn2_pre_g[0]):
                act.dma_start(rows[n_rows:n_rows + ND, :], v.rearrange("(k p) -> k p", p=P)).then_inc(rows_in, 16)
                n_rows += ND
            act.dma_start(rows[G_TAP:G_BIAS, :], conv_w[0].rearrange("j (k p) -> (j k) p", p=P)).then_inc(rows_in, 16)
            act.dma_start(rows[G_BIAS:NROWS, :], conv_b[0].rearrange("(k p) -> k p", p=P)).then_inc(rows_in, 16)
            swiglu(0)

            def evacuate(b):
                kind, j = kinds[b], IN_BLOCKS[b][1] if b < NIN else 0
                bank = 4 + 2 * (b % 2)
                if kind in ("A", "M"):
                    return
                act.wait_ge(w_used, H_MIX + ends(b) + 1)
                if kind == "k":
                    act.wait_ge(ones_v, 2)
                    act.activation(stage[:, 0, :].rearrange("p (h r d) -> p h r d", h=KVH, r=2),
                                   ps[:, bank, 0:ATT_KV].rearrange("p (h r d) -> p h r d", h=KVH, r=1).to_broadcast([P, KVH, 2, HD]),
                                   ACT.Identity, scale=rs_h[:, 0:1])
                    act.activation(att_v[:, 0, :], ps[:, bank, ATT_KV:2 * ATT_KV], ACT.Identity,
                                   scale=rs_h[:, 0:1]).then_inc(ev_a, 1)
                elif kind in ("q", "mqk"):
                    act.wait_ge(stage_turned, b)
                    if kind == "q":
                        act.wait_ge(q_scale, 1)
                    act.activation(stage[:, 0, :], ps[:, bank, :], ACT.Identity,
                                   scale=(rs_q if kind == "q" else rs_h)[:, 0:1]).then_inc(ev_a, 1)
                elif kind == "mv":
                    act.activation(mval[:, 0, 2 * j:2 * j + 2, 0:VD], ps[:, bank, :].rearrange("p (h d) -> p h d", h=2),
                                   ACT.Identity, scale=rs_h[:, 0:1]).then_inc(ev_a, 1)
                else:
                    for t in range(NT):
                        if kind == "mo":
                            dst = smo[:, t, j * COLS:(j + 1) * COLS]
                        elif kind == "ga":
                            dst = y[:, t, j * COLS:(j + 1) * COLS]
                        else:
                            dst = gm[:, j, t * COLS:(t + 1) * COLS]
                        ins = act.activation(dst, ps[:, bank + t, :], ACT.Sigmoid, scale=rs_h[:, t:t + 1])
                    ins.then_inc(ev_a, 1)

            def copy_y(j):
                act.wait_ge(y_turned, j + 1)
                act.activation(y_T[:, 4 * j:4 * j + 2, :], ps[:, Y_BANK[j], :].rearrange("p (a n) -> p a n", a=2),
                               ACT.Copy).then_inc(yt_a, 1)

            def turned_tile(b, a):
                if b == 0:
                    return att_kT[:, 2 * a:2 * a + 2, :]
                if b < 3:
                    return att_qT[:, 4 * (b - 1) + 2 * a:4 * (b - 1) + 2 * a + 2, :]
                return conv_in[:, 4 * (b - 3) + 2 * a:4 * (b - 3) + 2 * a + 2, CONV - 1:CP]

            def split(s):
                split_static(H_MIX + s)

            begin(1, H_MIX, split)
            act.wait_ge(h_rstd, 2)
            for s in range(END_SLOT):
                if s >= ND // 2 + 2:
                    split(s)
                if s == 18:
                    act.wait_ge(gate_rows, 1)
                    act.wait_ge(const_ready, 3)
                    step(act.activation(rows4[:, 2, :], rows4[:, 1, :], ACT.Abs))
                    step(act.activation(rows4[:, 2, :], rows4[:, 2, :], ACT.Exp, scale=-1.0))
                    act.activation(rows4[:, 2, :], rows4[:, 2, :], ACT.Ln, bias=ones[0:MH, 0:1]).then_inc(log_ready, 1)
                if s == 27:
                    act.wait_ge(r_turned, 1)
                    act.activation(e_col, ps[:, 3, 0:16].rearrange("p (t k h) -> p t k h", t=NT, k=2)[:, :, 1, :],
                                   ACT.Exp, scale=-1.0).then_inc(e_cols, 1)
                if s in EVAC_AT:
                    evacuate(EVAC_AT[s])
                if s in TURN_COPY:
                    b = TURN_COPY[s]
                    act.wait_ge(stage_turned, b + 1)
                    act.activation(turned_tile(b, 0), ps[:, 0, :].rearrange("p (a n) -> p a n", a=2),
                                   ACT.Copy).then_inc(turn_a, 1)
                if s in SILU_AT:
                    q = SILU_AT[s]
                    act.wait_ge(conv_ready, 4 * q + 4)
                    for c in range(4 * q, 4 * q + 4):
                        ins = act.activation(conv_out[:, c, :], conv_out[:, c, :], ACT.Silu,
                                             bias=cols[:, G_BIAS + c:G_BIAS + c + 1])
                    ins.then_inc(conv_silu, 1)
                g = group_at(s, 4)
                if g is not None:
                    K = P * (g % 2 + 1)
                    st = a_stat[:, g % 2]
                    act.wait_ge(maxed, g + 1)
                    for hh in range(GROUP):
                        act.activation(probs[:, g % 2, hh * K:(hh + 1) * K], probs[:, g % 2, hh * K:(hh + 1) * K],
                                       ACT.Exp, bias=st[:, 2, hh:hh + 1], accum_out=st[:, 4, hh:hh + 1])
                    act.activation(st[:, 5, :], st[:, 3, :], ACT.Exp).then_inc(exped, 1)
                g = group_at(s, 7)
                if g is not None:
                    act.wait_ge(p_turned, g + 1)
                    act.activation(probs_T[:, g % 2, 0:COLS], ps[:, 2, :], ACT.Copy).then_inc(pt_a, 1)
                g = group_at(s, 9)
                if g is not None:
                    j, b = divmod(g, 2)
                    act.wait_ge(pv_done, g + 1)
                    act.activation(att[:, 2 * j:2 * j + 2, b * P:(b + 1) * P],
                                   ps[:, 2, 0:2 * P].rearrange("p (a n) -> p a n", a=2), ACT.Copy).then_inc(pv_out, 1)
                if s == 88:
                    act.wait_ge(wt_arg, 1)
                    act.wait_ge(r_cols, 1)
                    for hd in range(MH):
                        act.activation(wt[:, hd, 0:SEQ], wt[:, hd, 0:SEQ], ACT.Exp, bias=r_col[:, 0, hd:hd + 1])
                        ins = act.activation(wt[:, hd, SEQ:WTN], wt[:, hd, SEQ:WTN], ACT.Exp, bias=r_col[:, 1, hd:hd + 1])
                    ins.then_inc(wt_ready, 1)
                for b in range(NT):
                    if s == 97 + 6 * b:
                        act.wait_ge(rden_ready, b + 1)
                        for hd in range(2):
                            ins = act.activation(m_h[:, b, hd * VD:(hd + 1) * VD], ps[:, hd, 0:VD], ACT.Identity,
                                                 scale=rden[:, b, hd:hd + 1])
                        ins.then_inc(mh_a, 1)
                        act.wait_ge(mh_v, b + 1)
                        act.wait_ge(mh_a, b + 1)
                        for hd in range(MH):
                            ins = act.activation(gm[:, b, hd * VD:(hd + 1) * VD], m_h[:, b, hd * VD:(hd + 1) * VD], ACT.Square,
                                                 accum_out=sq_m[:, b, hd:hd + 1])
                        ins.then_inc(m_squared, 1)
                if s == 115:
                    act.wait_ge(m_turned, 1)
                    act.activation(m_T[:, 0:4, :], ps[:, 0:2, :].rearrange("p a (c n) -> p (a c) n", c=2),
                                   ACT.Copy).then_inc(mt_a, 1)
                if SPLIT_SLOT <= s < SPLIT_SLOT + 8:
                    q = s - SPLIT_SLOT
                    if q == 4:
                        act.wait_ge(mt_a, 1)
                        act.wait_ge(mt_v, 1)
                    src = att if q < 4 else m_T
                    k = k_tile(q)
                    act.activation(x_hi[:, k:k + 2, :], src[:, 2 * (q % 4):2 * (q % 4) + 2, :],
                                   ACT.Copy).then_inc(att_split, 1)
                for j in range(NCB - 2):
                    if s == evac_slot(NIN + NCB + j) + 3:
                        copy_y(j)
            rows_quad(C_OUT, T_OUT, 0, "out", beside={0: lambda: copy_y(NCB - 2), 5: lambda: copy_y(NCB - 1)}, edge=True)
            with act.Fori(1, ND // RAW - 1) as i:
                rows_quad(C_OUT, T_OUT, i, "out")
            rows_quad(C_OUT, T_OUT, ND // RAW - 1, "out", edge=True)
            swiglu(1)
            squares_of_y(2)
            act.wait_ge(y_rstd, 3 * NT)
            act.wait_ge(z_ready, 3 * NCB * NT)
            z_1 = z[:, 2 * CBO[-1] + 1, :]
            act.activation(z_1, z_1, ACT.Identity, scale=rs_y[:, 1:2]).then_inc(z_scaled, 1)

        @block.vector
        def _(dve):
            steps = [0]

            def step(ins):
                steps[0] += 1
                ins.then_inc(dve_step, 1)
                dve.wait_ge(dve_step, steps[0])

            def split_lo(H, half, slot, hw):
                dve.wait_ge(hi_ready, H + 1)
                dve.tensor_tensor(w_lo[:, hw, :], raw[:, slot, half * HALF:(half + 1) * HALF],
                                  w_hi[:, hw, :].bitcast(F32), ALU.subtract).then_inc(lo_ready, 1)

            def turn_in_pair(e, u):
                dve.wait_ge(x_hi_ready, e * ND // 2 + u + 1)
                for kk in range(2):
                    k = k_tile(u) + kk
                    ins = dve.scalar_tensor_tensor(out=x_lo[:, k, :], in0=ps[:, 6 + u % 2, kk * SEQ:(kk + 1) * SEQ],
                                                   scalar=cols[:, G_PRE[e] + k:G_PRE[e] + k + 1],
                                                   in1=x_hi[:, k, :].bitcast(F32), op0=ALU.mult, op1=ALU.subtract)
                ins.then_inc(x_lo_ready, 1)

            def mean_square_h(e):
                dve.wait_ge(h_squared, 2 * e + 2)
                dve.tensor_scalar(ms_h, sq_h, 1.0 / D, EPS, ALU.mult, ALU.add).then_inc(h_ms, 1)

            def gain_y(p, n):
                bank = Y_BANKS[n]
                dve.wait_ge(y_squared, p * NCB * NT + n + 1)
                c = bank // NT * COLS
                dve.tensor_tensor(z[:, bank, :], ps[:, bank, :], gain[:, c:c + COLS], ALU.mult).then_inc(z_ready, 1)

            def mean_square_y(p, t, factor):
                dve.wait_ge(y_squared, p * NCB * NT + (6, 8)[t])
                ms = ms_y[:, t:t + 1]
                step(dve.tensor_reduce(ms, sq_y[:, t, :], AX.X, ALU.add))
                dve.tensor_scalar(ms, ms, 1.0 / (D * factor * factor), EPS / (factor * factor), ALU.mult,
                                  ALU.add).then_inc(y_ms, 1)

            def add_y(t, c0, n):
                cb, off = divmod(c0, COLS)
                return dve.scalar_tensor_tensor(out=h[:, t, c0:c0 + n], in0=z[:, 2 * cb + t, off:off + n],
                                                scalar=rs_y[:, t:t + 1], in1=h[:, t, c0:c0 + n],
                                                op0=ALU.mult, op1=ALU.add)

            def add_block(t, i):
                add_y(t, CBO[i] * COLS, COLS).then_inc((h_ready_0, h_ready_1)[t], 1)

            def norm_y(p, factor, early, before_last=None):
                dve.wait_ge(gain_in, 16 * (p + 1))
                for n in range(6):
                    gain_y(p, n)
                mean_square_y(p, 0, factor)
                dve.wait_ge(z_ready, p * NCB * NT + 6)
                dve.wait_ge(y_rstd, NT * p + 1)
                add_block(0, 0)
                gain_y(p, 6)
                for i in range(1, early):
                    add_block(0, i)
                if before_last:
                    before_last()
                mean_square_y(p, 1, factor)
                gain_y(p, 7)
                for i in range(early, NCB) if p == 2 else ():
                    add_block(0, i)
                dve.wait_ge(z_ready, (p + 1) * NCB * NT)
                dve.wait_ge(y_rstd, NT * (p + 1))
                for half in range(2):
                    add_y(1, CBO[0] * COLS + half * COLS // 2, COLS // 2).then_inc(h_ready_1, 1)

            def begin(e, split, factor):
                if e:
                    norm_y(e - 1, factor, 1, lambda: split(0))
                for u in range(ND // 2):
                    turn_in_pair(e, u)
                    if e and u < NCB - 1:
                        add_block(0, 1 + u)
                    if e and u == 0:
                        split(1)
                    if not e or u >= 2:
                        split(u)
                mean_square_h(e)

            def gated(e, i, base, first=False):
                dve.wait_ge(w_used, 2 * C_UP[e] + i * 4 * BLOCK_CHUNKS + 4 * BLOCK_CHUNKS)
                dve.wait_ge(silu_ready, e * NFB + i + 1)
                if not first:
                    dve.wait_ge(prod_turned, e * NFB + i)
                for t in range(NT):
                    ins = dve.scalar_tensor_tensor(out=prod[:, t, :], in0=ps[:, base + 2 + t, :],
                                                   scalar=rs_h[:, t:t + 1], in1=silu[:, t, :],
                                                   op0=ALU.mult, op1=ALU.mult)
                ins.then_inc(prod_ready, 1)

            def copy_hidden(e, i, base):
                dve.wait_ge(prod_turned, e * NFB + i + 1)
                dve.tensor_copy(hid[:, bass.ds(i * 4 + 2, 2), :],
                                ps[:, base + 1, :].rearrange("p (a b) -> p a b", a=2)).then_inc(hid_v, 1)

            def up_block(e, i, even, first):
                base = 4 if even else 0

                def split(j):
                    split_lo(2 * C_UP[e] + i * 4 * BLOCK_CHUNKS + j, j % 2, (j // 2) % RAW, j % SPL)

                if first:
                    begin(e and 2, split, 1.0)
                for j in range(ND // 2 if first else 0, 4 * BLOCK_CHUNKS):
                    split(j)
                    if j == 2 and not first:
                        gated(e, i - 1, 4 - base, first=isinstance(i, int) and i == 1)
                    if j == 7 and not first:
                        copy_hidden(e, i - 1, 4 - base)

            def rows_quad(base_c, T0, i, phase, e=None, beside=(), edge=False):
                for j, (q, half) in enumerate(EDGE_QUAD if edge else QUAD):
                    split_lo(2 * base_c + i * 2 * RAW + j, half, q, j % SPL)
                    if half == 0:
                        dve.wait_ge(xs_hi_ready, T0 + i * RAW + q + 1)
                        dve.tensor_tensor(x_lo[:, q, :], src_tile(phase, i * RAW + q), x_hi[:, q, :].bitcast(F32),
                                          ALU.subtract).then_inc(xs_lo_ready, 1)
                    if j in beside:
                        beside[j]()

            def swiglu(e):
                up_block(e, 0, True, True)
                up_block(e, 1, False, False)
                up_block(e, 2, True, False)
                with dve.Fori(1, NFB // 2) as it:
                    up_block(e, it * 2 + 1, False, False)
                    up_block(e, it * 2 + 2, True, False)
                if e == 0:
                    dve.wait_ge(wg_hi_ready, 1)
                    dve.tensor_tensor(wg_lo[:, :, :], wg_raw[:, :, :], wg_hi[:, :, :].bitcast(F32),
                                      ALU.subtract).then_inc(wg_lo_ready, 1)
                rows_quad(C_DOWN[e], T_DOWN[e], 0, "down", e,
                          {2: lambda: gated(e, NFB - 1, 4), 5: lambda: copy_hidden(e, NFB - 1, 4)}, edge=True)
                with dve.Fori(1, NF // RAW - 1) as i:
                    rows_quad(C_DOWN[e], T_DOWN[e], i, "down", e)
                rows_quad(C_DOWN[e], T_DOWN[e], NF // RAW - 1, "down", e, edge=True)

            swiglu(0)

            def split(s):
                split_lo(H_MIX + s, s % 2, (s // 2) % RAW, s % SPL)

            begin(1, split, 0.5)
            dve.wait_ge(h_rstd, 2)
            dve.tensor_scalar(rs_q, rs_h, HD ** -0.5, None, ALU.mult).then_inc(q_scale, 1)
            dve.wait_ge(q_scale, 1)

            def evacuate(b):
                kind, j = kinds[b], IN_BLOCKS[b][1] if b < NIN else (b - NIN) % NCB
                bank = 4 + 2 * (b % 2)
                if kind in ("mo", "ga", "gm"):
                    return
                dve.wait_ge(w_used, H_MIX + ends(b) + 1)
                if kind == "k":
                    dve.wait_ge(ones_v, 2)
                    dve.tensor_scalar(stage[:, 1, :].rearrange("p (h r d) -> p h r d", h=KVH, r=2),
                                      ps[:, bank + 1, 0:ATT_KV].rearrange("p (h r d) -> p h r d", h=KVH, r=1).to_broadcast([P, KVH, 2, HD]),
                                      rs_h[:, 1:2], None, ALU.mult)
                    dve.tensor_scalar(att_v[:, 1, :], ps[:, bank + 1, ATT_KV:2 * ATT_KV], rs_h[:, 1:2], None,
                                      ALU.mult).then_inc(ev_v, 1)
                elif kind in ("q", "mqk"):
                    dve.wait_ge(stage_turned, b)
                    dve.tensor_scalar(stage[:, 1, :], ps[:, bank + 1, :], (rs_q if kind == "q" else rs_h)[:, 1:2],
                                      None, ALU.mult).then_inc(ev_v, 1)
                elif kind == "mv":
                    dve.tensor_scalar(mval[:, 1, 2 * j:2 * j + 2, 0:VD], ps[:, bank + 1, :].rearrange("p (h d) -> p h d", h=2),
                                      rs_h[:, 1:2], None, ALU.mult).then_inc(ev_v, 1)
                else:
                    c = slice(j * COLS, (j + 1) * COLS)
                    if kind == "A":
                        dve.wait_ge(ev_a, act_evacs(8 + 1 + j))
                        for t in range(NT):
                            ins = dve.tensor_tensor(y[:, t, c], ps[:, bank + t, :], y[:, t, c], ALU.mult)
                        ins.then_inc(ev_v, 1)
                    else:
                        dve.wait_ge(ev_a, act_evacs(8 + 1 + 4 + j))
                        for t in range(NT):
                            g_t = gm[:, j, t * COLS:(t + 1) * COLS]
                            ins = dve.tensor_tensor(g_t, ps[:, bank + t, :], g_t, ALU.mult)
                        ins.then_inc(ev_v, 1)
                        dve.wait_ge(ev_v, dve_evacs(b))
                        for t in range(NT):
                            ins = dve.tensor_tensor(y[:, t, c], y[:, t, c], gm[:, j, t * COLS:(t + 1) * COLS], ALU.add)
                        ins.then_inc(y_ready, 1)

            def copy_y(j):
                dve.wait_ge(y_turned, j + 1)
                dve.tensor_copy(y_T[:, 4 * j + 2:4 * j + 4, :],
                                ps[:, Y_BANK[j] + 1, :].rearrange("p (a n) -> p a n", a=2)).then_inc(yt_v, 1)

            def turned_tile(b, a):
                if b == 0:
                    return att_kT[:, 2 * a:2 * a + 2, :]
                if b < 3:
                    return att_qT[:, 4 * (b - 1) + 2 * a:4 * (b - 1) + 2 * a + 2, :]
                return conv_in[:, 4 * (b - 3) + 2 * a:4 * (b - 3) + 2 * a + 2, CONV - 1:CP]

            for s in range(END_SLOT):
                if s >= ND // 2:
                    split(s)
                if s == 13:
                    dve.wait_ge(gates_done, 1)
                    step(dve.tensor_copy(gates8, ps[0:2 * MH, 2, SEQ:2 * SEQ]))
                    dve.tensor_tensor(gates8, ps[0:2 * MH, 2, 0:SEQ], gates8, ALU.mult).then_inc(gates_ready, 1)
                if s == 17:
                    dve.wait_ge(gates_turned, 1)
                    dve.wait_ge(misc_in, 64)
                    for n in range(2):
                        ins = dve.tensor_scalar(rows4[:, n, :], ps[0:MH, 3, n * SEQ:(n + 1) * SEQ],
                                                gate_b[:, n:n + 1], None, ALU.add)
                    ins.then_inc(gate_rows, 1)
                if s == 21:
                    dve.wait_ge(log_ready, 1)
                    dve.wait_ge(const_ready, 3)
                    i_r, f_R, l_m, F_ = (rows4[:, n, :] for n in range(4))
                    step(dve.scalar_tensor_tensor(out=l_m, in0=f_R, scalar=0.0, in1=l_m, op0=ALU.min, op1=ALU.subtract))
                    step(dve.tensor_tensor_scan(F_, ones[0:MH, :], l_m, 0.0, ALU.mult, ALU.add))
                    step(dve.tensor_tensor(i_r, i_r, F_, ALU.subtract))
                    step(dve.tensor_tensor_scan(f_R, ones[0:MH, :], i_r, 0.0, ALU.mult, ALU.max))
                    dve.tensor_tensor(l_m, F_, f_R, ALU.add).then_inc(rows_ready, 1)
                if s == 27:
                    dve.wait_ge(e_cols, 1)
                    dve.tensor_copy(r_col, ps[:, 3, 0:16].rearrange("p (t k h) -> p t k h", t=NT, k=2)[:, :, 0, :]).then_inc(r_cols, 1)
                if s in EVAC_AT:
                    evacuate(EVAC_AT[s])
                if s in TURN_COPY:
                    b = TURN_COPY[s]
                    dve.wait_ge(stage_turned, b + 1)
                    dve.tensor_copy(turned_tile(b, 1), ps[:, 1, :].rearrange("p (a n) -> p a n", a=2)).then_inc(turn_v, 1)
                if s in CONV_AT:
                    q, c4 = CONV_AT[s]
                    c = 4 * q + c4
                    dve.wait_ge(turn_a, 4 + q)
                    dve.wait_ge(turn_v, 4 + q)

                    def tap(j):
                        n = G_TAP + j * 2 * MQK // P + c
                        return cols[:, n:n + 1]

                    step(dve.tensor_scalar(conv_out[:, c, :], conv_in[:, c, 0:SEQ], tap(0), None, ALU.mult))
                    for j in range(1, CONV):
                        ins = dve.scalar_tensor_tensor(out=conv_out[:, c, :], in0=conv_in[:, c, j:j + SEQ], scalar=tap(j),
                                                       in1=conv_out[:, c, :], op0=ALU.mult, op1=ALU.add)
                        if j < CONV - 1:
                            step(ins)
                    ins.then_inc(conv_ready, 1)
                g = group_at(s, 3)
                if g is not None:
                    j, b = divmod(g, 2)
                    K = P * (b + 1)
                    st = a_stat[:, g % 2]
                    dve.wait_ge(scored, g + 1)
                    for hh in range(GROUP):
                        slope = float(np.exp2(np.float32(-8.0 * (GROUP * j + hh + 1) / HEADS)))
                        off = (hh // 2) * K
                        ins = dve.scalar_tensor_tensor(out=probs[:, g % 2, hh * K:(hh + 1) * K], in0=dist[:, 2 * P - K:2 * P],
                                                       scalar=-slope, in1=ps[:, hh % 2, off:off + K],
                                                       op0=ALU.mult, op1=ALU.add)
                    step(ins)
                    step(dve.tensor_reduce(st[:, 0, :], probs[:, g % 2, 0:GROUP * K].rearrange("p (h k) -> p h k", h=GROUP),
                                           AX.X, ALU.max))
                    sink = sinks[:, GROUP * j:GROUP * (j + 1)]
                    step(dve.tensor_tensor(st[:, 1, :], st[:, 0, :], sink, ALU.max))
                    dve.tensor_scalar(st[:, 2, :], st[:, 1, :], -1.0, None, ALU.mult)
                    dve.tensor_tensor(st[:, 3, :], sink, st[:, 1, :], ALU.subtract).then_inc(maxed, 1)
                g = group_at(s, 5)
                if g is not None:
                    K = P * (g % 2 + 1)
                    st = a_stat[:, g % 2]
                    dve.wait_ge(exped, g + 1)
                    step(dve.tensor_tensor(st[:, 6, :], st[:, 4, :], st[:, 5, :], ALU.add))
                    step(dve.reciprocal(st[:, 7, :], st[:, 6, :]))
                    pv = probs[:, g % 2, 0:GROUP * K].rearrange("p (h k) -> p h k", h=GROUP)
                    dve.tensor_tensor(pv, pv, st[:, 7, :].rearrange("p (h k) -> p h k", k=1).to_broadcast([P, GROUP, K]),
                                      ALU.mult).then_inc(normed, 1)
                g = group_at(s, 7)
                if g is not None and g % 2:
                    dve.wait_ge(p_turned, g + 1)
                    dve.tensor_copy(probs_T[:, g % 2, COLS:2 * COLS], ps[:, 3, :]).then_inc(pt_v, 1)
                if s == 80:
                    dve.wait_ge(ev_a, act_evacs(8))
                    for t in range(NT):
                        ins = dve.tensor_tensor(smo[:, t, :], smo[:, t, :], head_g[:, :], ALU.mult)
                    step(ins)
                if s == 87:
                    dve.wait_ge(neg_r, 1)
                    bc = ps[:, 0:2, :].rearrange("p a (c n) -> p (a c) n", c=2)
                    fut = future[:, :].rearrange("p (a n) -> p a n", a=1).to_broadcast([P, MH, P])
                    dve.tensor_tensor(wt[:, :, 0:P], bc[:, :, 0:P], fut, ALU.add)
                    dve.tensor_copy(wt[:, :, P:2 * P], bc[:, :, P:2 * P])
                    dve.tensor_tensor(wt[:, :, 2 * P:3 * P], bc[:, :, P:2 * P], fut, ALU.add).then_inc(wt_arg, 1)
                if s == 93:
                    dve.wait_ge(m_scored, 1)
                    dve.wait_ge(wt_ready, 1)
                    for hd in range(MH):
                        ins = dve.scalar_tensor_tensor(out=pt_m[:, hd, :], in0=ps[:, hd, 0:WTN], scalar=float(QKD) ** -0.5,
                                                       in1=wt[:, hd, :], op0=ALU.mult, op1=ALU.mult)
                    ins.then_inc(pt_m_ready, 1)
                for b in range(NT):
                    if s == 97 + 6 * b:
                        dve.wait_ge(num_done, b + 1)
                        dve.wait_ge(e_cols, 1)
                        d = den[:, b, :]
                        step(dve.tensor_copy(d, ps[:, 0:MH, VD]))
                        step(dve.scalar_tensor_tensor(out=d, in0=d, scalar=-1.0, in1=d, op0=ALU.mult, op1=ALU.max))
                        step(dve.tensor_tensor(d, d, e_col[:, b, :], ALU.max))
                        dve.reciprocal(rden[:, b, :], den[:, b, :]).then_inc(rden_ready, 1)
                        dve.wait_ge(rden_ready, b + 1)
                        for hd in range(2, MH):
                            ins = dve.tensor_scalar(m_h[:, b, hd * VD:(hd + 1) * VD], ps[:, hd, 0:VD], rden[:, b, hd:hd + 1],
                                                    None, ALU.mult)
                        ins.then_inc(mh_v, 1)
                    if s == 99 + 6 * b:
                        dve.wait_ge(m_squared, b + 1)
                        dve.tensor_scalar(ms_m[:, b, :], sq_m[:, b, :], 1.0 / VD, EPS, ALU.mult, ALU.add).then_inc(m_ms, 1)
                    if s == 101 + 6 * b:
                        dve.wait_ge(m_rstd, b + 1)
                        for hd in range(MH):
                            c = slice(hd * VD, (hd + 1) * VD)
                            ins = dve.scalar_tensor_tensor(out=smo[:, b, c], in0=m_h[:, b, c], scalar=rs_m[:, b, hd:hd + 1],
                                                           in1=smo[:, b, c], op0=ALU.mult, op1=ALU.mult)
                        ins.then_inc(m_rows, 1)
                if s == 115:
                    dve.wait_ge(m_turned, 1)
                    dve.tensor_copy(m_T[:, 4:8, :], ps[:, 2:4, :].rearrange("p a (c n) -> p (a c) n", c=2)).then_inc(mt_v, 1)
                if SPLIT_SLOT <= s < SPLIT_SLOT + 8:
                    q = s - SPLIT_SLOT
                    dve.wait_ge(att_split, q + 1)
                    src = att if q < 4 else m_T
                    k = k_tile(q)
                    dve.tensor_tensor(x_lo[:, k:k + 2, :], src[:, 2 * (q % 4):2 * (q % 4) + 2, :],
                                      x_hi[:, k:k + 2, :].bitcast(F32), ALU.subtract).then_inc(att_split_lo, 1)
                for j in range(NCB - 2):
                    if s == evac_slot(NIN + NCB + j) + 3:
                        copy_y(j)
            rows_quad(C_OUT, T_OUT, 0, "out", beside={0: lambda: copy_y(NCB - 2), 2: lambda: evacuate(NIN + 2 * NCB - 1),
                                                      5: lambda: copy_y(NCB - 1)}, edge=True)
            with dve.Fori(1, ND // RAW - 1) as i:
                rows_quad(C_OUT, T_OUT, i, "out")
            rows_quad(C_OUT, T_OUT, ND // RAW - 1, "out", edge=True)
            swiglu(1)
            norm_y(2, 0.5, NCB - 1)
            for i in range(1, NCB - 1):
                add_block(1, i)

        @block.tensor
        def _(pe):
            def three(dst, x_tile, t, w, n0, start, stop):
                xh = x_hi[:, x_tile, t * P:(t + 1) * P]
                pe.matmul(dst, xh, w_hi[:, w, n0:n0 + COLS], start=start, stop=False)
                pe.matmul(dst, xh, w_lo[:, w, n0:n0 + COLS], start=False, stop=False)
                return pe.matmul(dst, x_lo[:, x_tile, t * P:(t + 1) * P], w_hi[:, w, n0:n0 + COLS], start=False, stop=stop)

            def turn(dst, src):
                return pe.transpose(dst, src, ident[:, :])

            def turn_h(e, u):
                if e:
                    i = u // 2
                    pe.wait_ge(h_ready_0, (e - 1) * NCB + i + 1)
                    if i:
                        pe.wait_ge(h_ready_pool, (e - 1) * (NCB - 1) + i)
                    else:
                        pe.wait_ge(h_ready_1, (e - 1) * 2 + u + 1)
                elif u % 2 == 0:
                    pe.wait_ge(x_in[CBO[u // 2]], 16)
                if u >= 2:
                    pe.wait_ge(x_lo_ready, e * ND // 2 + u - 1)
                for kk in range(2):
                    for t in range(NT):
                        k = k_tile(u) + kk
                        n = kk * SEQ + t * P
                        ins = turn(ps[:, 6 + u % 2, n:n + P], h[:, t, k * P:(k + 1) * P])
                ins.then_inc(h_turned, 1)

            def begin(e, halves):
                turn_h(e, 0)
                turn_h(e, 1)
                for j in range(ND // 2):
                    pe.wait_ge(x_lo_ready, e * ND // 2 + j + 1)
                    halves(j, (lambda: turn_h(e, j + 2)) if j + 2 < ND // 2 else None)

            def turn_y(j):
                pe.wait_ge(y_ready, j + 1)
                if j == 2:
                    pe.wait_ge(yt_a, 1)
                    pe.wait_ge(yt_v, 1)
                for c in range(4):
                    for t in range(NT):
                        n = (c % 2) * SEQ + t * P
                        ins = turn(ps[:, Y_BANK[j] + c // 2, n:n + P], y[:, t, (4 * j + c) * P:(4 * j + c + 1) * P])
                ins.then_inc(y_turned, 1)

            def turn_hidden(e, i, base):
                pe.wait_ge(prod_ready, e * NFB + i + 1)
                pe.wait_ge(silu_ready, e * NFB + i + 1)
                for a in range(2):
                    for kk in range(2):
                        for t in range(NT):
                            c = (2 * a + kk) * P
                            ins = turn(ps[:, base + a, kk * SEQ + t * P:kk * SEQ + (t + 1) * P], prod[:, t, c:c + P])
                ins.then_inc(prod_turned, 1)

            def up_block(e, i, even, first, old):
                base = 4 if even else 0

                def halves(j, between=None):
                    n, q = divmod(j, 8)
                    pe.wait_ge(lo_ready, 2 * C_UP[e] + i * 4 * BLOCK_CHUNKS + j + 1)
                    for kk in range(2):
                        if kk and between:
                            between()
                        for t in range(NT):
                            ins = three(ps[:, base + 2 * n + t, :], k_tile(q) + kk, t, j % SPL, kk * COLS,
                                        q == kk == 0, q == 7 and kk == 1)
                    ins.then_inc(w_used, 1)

                if first:
                    begin(e and 2, halves)
                    if e == 0:
                        pe.wait_ge(rows_in, 64)
                        pe.transpose(ps[:, 0, 0:NROWS], rows[0:NROWS, :], ident[0:NROWS, 0:NROWS]).then_inc(rows_turned, 1)
                for j in range(ND // 2 if first else 0, 4 * BLOCK_CHUNKS):
                    if old and j == 0:
                        pe.wait_ge(hid_a, e * NFB + i - 1)
                        pe.wait_ge(hid_v, e * NFB + i - 1)
                    if isinstance(i, int) and i == 1 and e == 0 and j == 0:
                        pe.wait_ge(cols_ready, 2)
                    halves(j)
                    if j == 4 and not first:
                        turn_hidden(e, i - 1, 4 - base)

            def row_half(H, T, slot, w, half, start, stop):
                pe.wait_ge(lo_ready, H + 1)
                pe.wait_ge(xs_lo_ready, T + 1)
                for t in range(NT):
                    for c in range(2):
                        ins = three(ps[:, 4 * half + 2 * c + t, :], slot, t, w, c * COLS, start, stop)
                ins.then_inc(w_used, 1)

            def rows_quad(base_c, T0, i, first, before=()):
                for j, (q, half) in enumerate(EDGE_QUAD if first else QUAD):
                    if j in before:
                        before[j]()
                    row_half(2 * base_c + i * 2 * RAW + j, T0 + i * RAW + q, q, j % SPL, half,
                             first and q == 0, False)

            def last_rows_quad(base_c, T0, i):
                H = 2 * base_c + i * 2 * RAW
                for j, (q, half) in enumerate(EDGE_QUAD[:RAW]):
                    row_half(H + j, T0 + i * RAW + q, q, j % SPL, half, False, q == RAW - 1)
                for q in range(RAW):
                    pe.wait_ge(lo_ready, H + RAW + q + 1)
                    for c in range(2):
                        ins = three(ps[:, 4 + 2 * c, :], q, 0, q, c * COLS, False, q == RAW - 1)
                ins.then_inc(y_bank, 1)
                for c in range(2):
                    for q in range(RAW):
                        ins = three(ps[:, 5 + 2 * c, :], q, 1, q, c * COLS, False, q == RAW - 1)
                        if c == 1:
                            ins.then_inc(w_used, 1)
                        elif q == RAW - 1:
                            ins.then_inc(y_bank, 1)

            def by_rows(base_c, T0, n, before):
                rows_quad(base_c, T0, 0, True, before)
                if n > 2 * RAW:
                    with pe.Fori(1, n // RAW - 1) as i:
                        rows_quad(base_c, T0, i, False)
                last_rows_quad(base_c, T0, n // RAW - 1)

            def swiglu(e):
                up_block(e, 0, True, True, False)
                up_block(e, 1, False, False, False)
                up_block(e, 2, True, False, True)
                with pe.Fori(1, NFB // 2) as it:
                    up_block(e, it * 2 + 1, False, False, True)
                    up_block(e, it * 2 + 2, True, False, True)
                pe.wait_ge(hid_a, e * NFB + NFB - 1)
                pe.wait_ge(hid_v, e * NFB + NFB - 1)

                def banks_read():
                    pe.wait_ge(hid_a, (e + 1) * NFB)
                    pe.wait_ge(hid_v, (e + 1) * NFB)

                by_rows(C_DOWN[e], T_DOWN[e], NF, {3: lambda: turn_hidden(e, NFB - 1, 4), 4: banks_read})

            pe.wait_ge(const_step, 2)
            pe.wait_ge(gain_rows_in, 16)
            pe.transpose(ps[:, 5, 0:ND], rows[0:ND, :], ident[0:ND, 0:ND]).then_inc(rows_turned, 1)
            swiglu(0)

            def gates(s):
                if s == 4:
                    pe.wait_ge(wg_lo_ready, 1)
                for q in (2 * s - 8, 2 * s - 7):
                    for kk in range(2):
                        k = k_tile(q) + kk
                        dst = ps[0:2 * MH, 2, 0:SEQ]
                        pe.matmul(dst, wg_hi[:, k, :], x_hi[:, k, :], start=(q == kk == 0), stop=False, skip_group_check=True)
                        pe.matmul(dst, wg_lo[:, k, :], x_hi[:, k, :], start=False, stop=False, skip_group_check=True)
                        pe.matmul(dst, wg_hi[:, k, :], x_lo[:, k, :], start=False, stop=False, skip_group_check=True)

            def in_half(s, between=None):
                if s < A_SLOT:
                    b, q = divmod(s, 8)
                    last, k = q == 7, k_tile(q)
                else:
                    b, q = divmod(s - A_SLOT, 4)
                    b += NIN
                    last, k = q == 3, k_tile(q if s < M_SLOT else 4 + q)
                    if b == NIN:
                        pe.wait_ge(att_split_lo, q + 1)
                    if b == NIN + NCB:
                        pe.wait_ge(att_split_lo, 4 + q + 1)
                if q == 0 and b >= 2:
                    pe.wait_ge(ev_a, act_evacs(b - 2))
                    if dve_evacs(b - 2):
                        pe.wait_ge(ev_v, dve_evacs(b - 2))
                pe.wait_ge(lo_ready, H_MIX + s + 1)
                for kk in range(2):
                    if kk and between:
                        between()
                    for t in range(NT):
                        ins = three(ps[:, 4 + 2 * (b % 2) + t, :], k + kk, t, s % SPL, kk * COLS, q == kk == 0,
                                    last and kk == 1)
                ins.then_inc(w_used, 1)
                if 4 <= s < 8:
                    gates(s)

            begin(1, in_half)
            for s in range(ND // 2, END_SLOT):
                in_half(s)
                if s == 9:
                    pe.wait_ge(h_rstd, 2)
                    for t in range(NT):
                        ins = pe.matmul(ps[0:2 * MH, 2, SEQ + t * P:SEQ + (t + 1) * P],
                                        rs_h[:, t:t + 1].to_broadcast([P, 2 * MH]), ident[:, :], start=False,
                                        stop=(t == 1), skip_group_check=True)
                    ins.then_inc(gates_done, 1)
                if s == 14:
                    pe.wait_ge(gates_ready, 1)
                    for n in range(2):
                        ins = pe.matmul(ps[0:MH, 3, n * SEQ:(n + 1) * SEQ], ident[0:2 * MH, n * MH:(n + 1) * MH],
                                        gates8, start=(n == 0), stop=(n == 1), skip_group_check=True)
                    ins.then_inc(gates_turned, 1)
                if s == 24:
                    pe.wait_ge(rows_ready, 1)
                    for t in range(NT):
                        for n, row in enumerate((0, 2)):
                            c = t * 2 * MH + n * MH
                            ins = pe.transpose(ps[:, 3, c:c + MH], rows4[:, row, t * P:(t + 1) * P], ident[0:MH, 0:MH])
                    ins.then_inc(r_turned, 1)
                if s in TURN_B:
                    b = TURN_B[s]
                    pe.wait_ge(ev_a, act_evacs(b))
                    pe.wait_ge(ev_v, dve_evacs(b))
                    if b >= 2:
                        pe.wait_ge(maxed, b - 1)
                    if b:
                        pe.wait_ge(turn_a, b)
                        pe.wait_ge(turn_v, b)
                    for c in range(4):
                        for t in range(NT):
                            n = (c % 2) * SEQ + t * P
                            ins = turn(ps[:, c // 2, n:n + P], stage[:, t, c * P:(c + 1) * P])
                    ins.then_inc(stage_turned, 1)
                g = group_at(s, 0)
                if g is not None:
                    j, b = divmod(g, 2)
                    K = P * (b + 1)
                    turns = min(2 + g, 5)
                    pe.wait_ge(turn_a, turns)
                    pe.wait_ge(turn_v, turns)
                    if g:
                        pe.wait_ge(maxed, g)
                    for i in range(2):
                        for par in range(2):
                            lo, hi = par * HD, (par + 1) * HD
                            ins = pe.matmul(ps[:, par, i * K:(i + 1) * K], att_qT[lo:hi, 2 * j + i, b * P:(b + 1) * P],
                                            att_kT[lo:hi, j, 0:K], start=(i == 0), stop=(i == 1), skip_group_check=True)
                    ins.then_inc(scored, 1)
                g = group_at(s, 4)
                if g is not None:
                    j, b = divmod(g, 2)
                    K = P * (b + 1)
                    pe.wait_ge(normed, g + 1)
                    if g == 1:
                        pe.wait_ge(r_cols, 1)
                    if g:
                        pe.wait_ge(pv_out, g)
                    if g >= 2:
                        pe.wait_ge(pt_v, g // 2)
                    for kt in range(b + 1):
                        for hh in range(GROUP):
                            n = ((hh % 2) * 2 + hh // 2) * P
                            ins = turn(ps[:, 2 + kt, n:n + P], probs[:, g % 2, hh * K + kt * P:hh * K + (kt + 1) * P])
                    ins.then_inc(p_turned, 1)
                g = group_at(s, 6)
                if g is not None:
                    j, b = divmod(g, 2)
                    pe.wait_ge(pt_a, g + 1)
                    if b:
                        pe.wait_ge(pt_v, g // 2 + 1)
                    for par in range(2):
                        for kt in range(b + 1):
                            n = kt * COLS + par * 2 * P
                            ins = pe.matmul(ps[par * HD:(par + 1) * HD, 2, 0:2 * P], att_v[:, kt, j * HD:(j + 1) * HD],
                                            probs_T[:, g % 2, n:n + 2 * P], start=(kt == 0), stop=(kt == b))
                    ins.then_inc(pv_done, 1)
                if s == 84:
                    pe.wait_ge(maxed, NG)
                    pe.wait_ge(const_ready, 3)
                    for hd in range(MH):
                        ins = pe.matmul(ps[:, hd // 2, (hd % 2) * SEQ:(hd % 2 + 1) * SEQ], sel[:, hd, :], rows4[:, 1, :],
                                        start=(hd % 2 == 0), stop=(hd % 2 == 1), skip_group_check=True)
                    ins.then_inc(neg_r, 1)
                if s == 90:
                    pe.wait_ge(conv_silu, 2)
                    pe.wait_ge(wt_arg, 1)
                    pe.wait_ge(pv_out, NG)
                    pe.wait_ge(pt_v, NG // 2)
                    for hd in range(MH):
                        pe.matmul(ps[:, hd, 0:SEQ], conv_out[:, MH + hd, 0:P], conv_out[:, hd, :], start=True, stop=False,
                                  skip_group_check=True)
                        ins = pe.matmul(ps[:, hd, SEQ:WTN], conv_out[:, MH + hd, P:SEQ], conv_out[:, hd, P:SEQ],
                                        start=False, stop=True, skip_group_check=True)
                    ins.then_inc(m_scored, 1)
                for b in range(NT):
                    if s == 94 + 6 * b:
                        if b:
                            pe.wait_ge(mh_a, 1)
                            pe.wait_ge(mh_v, 1)
                        else:
                            pe.wait_ge(pt_m_ready, 1)
                            pe.wait_ge(ones_v, 1)
                            pe.wait_ge(ev_a, act_evacs(6))
                            pe.wait_ge(ev_v, dve_evacs(6))
                        for hd in range(MH):
                            for a in range(b + 1):
                                c = (b if a == 0 else 2) * P
                                ins = pe.matmul(ps[:, hd, 0:VD + 1], pt_m[:, hd, c:c + P], mval[:, a, hd, :],
                                                start=(a == 0), stop=(a == b))
                        ins.then_inc(num_done, 1)
                if s == 112:
                    pe.wait_ge(m_rows, NT)
                    pe.wait_ge(mh_a, NT)
                    pe.wait_ge(mh_v, NT)
                    for c in range(2 * MH):
                        for t in range(NT):
                            n = (c % 2) * SEQ + t * P
                            ins = turn(ps[:, c // 2, n:n + P], smo[:, t, c * P:(c + 1) * P])
                    ins.then_inc(m_turned, 1)
                for j in range(NCB - 1):
                    if s == evac_slot(NIN + NCB + j):
                        turn_y(j)
            pe.wait_ge(yt_a, NCB - 1)
            pe.wait_ge(yt_v, NCB - 1)

            def banks_read():
                pe.wait_ge(yt_a, NCB)
                pe.wait_ge(yt_v, NCB)

            by_rows(C_OUT, T_OUT, ND, {3: lambda: turn_y(NCB - 1), 4: banks_read})
            swiglu(1)


_INS = ["x", "ffn1_pre_g", "ffn1_wg", "ffn1_wu", "ffn1_wd", "ffn1_post_g", "mix_pre_g", "w_in", "conv_w", "conv_b",
        "attn_sinks", "m_igate_b", "m_fgate_b", "m_head_g", "w_attn_up", "w_mlstm_up", "w_out", "mix_post_g",
        "ffn2_pre_g", "ffn2_wg", "ffn2_wu", "ffn2_wd", "ffn2_post_g"]


def kernel(**inputs):
    import concourse.bacc as bacc
    from concourse.bass_utils import run_bass_kernel_spmd

    nc = bacc.Bacc("TRN2", target_bir_lowering=False, num_devices=1)
    arrays, args = {}, []
    for name in _INS:
        a = np.ascontiguousarray(inputs[name])
        arrays[f"in_{name}"] = a
        args.append(nc.dram_tensor(f"in_{name}", a.shape, mybir.dt.from_np(a.dtype), kind="ExternalInput").ap())
    shape = np.shape(inputs["x"])
    args.append(nc.dram_tensor("out_y", shape, F32, kind="ExternalOutput").ap())
    hybrid_layer(nc, *args)
    r = run_bass_kernel_spmd(nc, [arrays], core_ids=[0])
    return r.results[0]["out_y"]
```
